# Optimizing a Trainium2 kernel written in Bass

```python
import math
import jax
import jax.numpy as jnp
from jax import lax
import numpy as np

D_MODEL = 1024
BATCH = 1
SEQ = 1024
DEPTH = 1
DEC_BATCH = 8
DEC_SEQ = 4
PAST_LEN = 1024
PAGE_SIZE = 128

HEAD_DIM = 64
N_HEADS_A = D_MODEL // HEAD_DIM
D_ATTN = N_HEADS_A * HEAD_DIM
DILATED_BRANCHES = ((128, 1), (512, 4), (2048, 16))
MAX_WINDOW = max(w for w, _ in DILATED_BRANCHES)
BLK = 128
ATTN_SCALE = HEAD_DIM ** -0.5
N_BUCKETS = 32
MAX_EXACT = N_BUCKETS // 2
MAX_DISTANCE = MAX_WINDOW
SSM_HEAD_DIM = 64
N_HEADS_S = D_MODEL // SSM_HEAD_DIM
D_SSM = N_HEADS_S * SSM_HEAD_DIM
SSM_GROUPS = 2
D_STATE = 128
CONV_WIDTH = 4
CONV_DIM = D_SSM + 2 * SSM_GROUPS * D_STATE
SSD_CHUNK = 128
D_MIX = D_ATTN + D_SSM
D_IN_PROJ = 3 * D_ATTN + D_SSM + CONV_DIM + N_HEADS_S
D_FF = 4 * D_MODEL
EPS = 1e-6

kernel_name = 'hymba_dilated_ssd_decoder_step'

def rmsnorm(x, g):
    xf = x.astype(jnp.float32)
    y = xf * lax.rsqrt(jnp.mean(xf * xf, axis=-1, keepdims=True) + EPS)
    return (y * g.astype(jnp.float32)).astype(x.dtype)

def t5_bucket(dist):
    small = dist < MAX_EXACT
    df = jnp.maximum(dist, 1).astype(jnp.float32)
    large = MAX_EXACT + (jnp.log(df / MAX_EXACT) / math.log(MAX_DISTANCE / MAX_EXACT)
                         * (N_BUCKETS - MAX_EXACT)).astype(jnp.int32)
    return jnp.where(small, dist, jnp.minimum(large, N_BUCKETS - 1))

def project(x, norm_mix, w_in, q_norm, k_norm):
    b, t = x.shape[:2]
    p = rmsnorm(x, norm_mix) @ w_in
    q, k, v, z, xbc, dt_raw = jnp.split(
        p, [D_ATTN, 2 * D_ATTN, 3 * D_ATTN, 3 * D_ATTN + D_SSM, 3 * D_ATTN + D_SSM + CONV_DIM], axis=-1)
    q = rmsnorm(q.reshape(b, t, N_HEADS_A, HEAD_DIM), q_norm)
    k = rmsnorm(k.reshape(b, t, N_HEADS_A, HEAD_DIM), k_norm)
    v = v.reshape(b, t, N_HEADS_A, HEAD_DIM)
    return q, k, v, z, xbc, dt_raw

def dilated_branch_prompt(q, k, v, rel_bias, window, dil):
    b, s, h, dh = q.shape
    span = window // dil
    L = s // dil
    nb = -(-L // BLK)
    pad = nb * BLK - L

    def to_phase(t):
        return t.reshape(b, L, dil, h, dh).transpose(0, 2, 1, 3, 4).reshape(b * dil, L, h, dh)

    def key_blocks(t):
        tp = jnp.pad(to_phase(t), ((0, 0), (BLK, pad), (0, 0), (0, 0))).reshape(b * dil, nb + 1, BLK, h, dh)
        return jnp.concatenate([tp[:, :-1], tp[:, 1:]], axis=2)

    qb = jnp.pad(to_phase(q), ((0, 0), (0, pad), (0, 0), (0, 0))).reshape(b * dil, nb, BLK, h, dh)
    kb, vb = key_blocks(k), key_blocks(v)
    rel = jnp.arange(BLK)[:, None] + BLK - jnp.arange(2 * BLK)[None, :]
    band = (rel >= 0) & (rel <= span)
    not_pad = (jnp.arange(nb)[:, None, None] > 0) | (jnp.arange(2 * BLK)[None, None, :] >= BLK)
    valid = band[None] & not_pad
    bias = rel_bias[t5_bucket(jnp.clip(rel, 0, span) * dil)].astype(jnp.float32).transpose(2, 0, 1)
    logits = jnp.einsum('gnqhd,gnkhd->gnhqk', qb, kb, preferred_element_type=jnp.float32) * ATTN_SCALE
    logits = jnp.where(valid[None, :, None], logits + bias[None, None], -jnp.inf)
    m = jnp.max(logits, axis=-1, keepdims=True)
    pr = jnp.exp(logits - m)
    den = jnp.sum(pr, axis=-1)
    o = jnp.einsum('gnhqk,gnkhd->gnqhd', pr, vb.astype(jnp.float32)) / jnp.swapaxes(den, 2, 3)[..., None]
    lse = jnp.swapaxes(m[..., 0] + jnp.log(den), 2, 3)

    def from_phase(t):
        t = t.reshape(b * dil, nb * BLK, *t.shape[3:])[:, :L]
        return t.reshape(b, dil, L, *t.shape[2:]).swapaxes(1, 2).reshape(b, s, *t.shape[2:])

    return from_phase(o), from_phase(lse)

def dilated_branch_sample(q, k_all, v_all, rel_bias, window, dil):
    t = q.shape[1]
    n_past = k_all.shape[1] - t
    span = window // dil
    j = jnp.arange(span + 1)
    idx = n_past + jnp.arange(t)[:, None] - j[None, :] * dil
    valid = idx >= 0
    idx = jnp.maximum(idx, 0)
    kg = k_all[:, idx]
    vg = v_all[:, idx]
    bias = rel_bias[t5_bucket(j * dil)].astype(jnp.float32).T
    logits = jnp.einsum('bthd,btjhd->bthj', q, kg, preferred_element_type=jnp.float32) * ATTN_SCALE
    logits = jnp.where(valid[None, :, None, :], logits + bias[None, None], -jnp.inf)
    m = jnp.max(logits, axis=-1, keepdims=True)
    pr = jnp.exp(logits - m)
    den = jnp.sum(pr, axis=-1)
    o = jnp.einsum('bthj,btjhd->bthd', pr, vg.astype(jnp.float32)) / den[..., None]
    return o, m[..., 0] + jnp.log(den)

def merge_branches(branches):
    outs = jnp.stack([o for o, _ in branches])
    lse = jnp.stack([s for _, s in branches])
    w = jax.nn.softmax(lse, axis=0)
    return jnp.einsum('gbth,gbthd->bthd', w, outs)

def causal_conv(xbc, prior, conv_w, conv_b):
    t = xbc.shape[1]
    xpad = jnp.concatenate([prior, xbc], axis=1)
    out = sum(xpad[:, i:i + t] * conv_w[i] for i in range(CONV_WIDTH)) + conv_b
    return jax.nn.silu(out), xpad[:, t:]

def ssd(xh, dt, a, bm, cm, h0):
    b, s, nh, hp = xh.shape
    q = SSD_CHUNK if s % SSD_CHUNK == 0 else s
    nc = s // q
    g, r = SSM_GROUPS, nh // SSM_GROUPS
    xc = xh.astype(jnp.float32).reshape(b, nc, q, g, r, hp)
    dtc = dt.reshape(b, nc, q, g, r)
    bc = bm.astype(jnp.float32).reshape(b, nc, q, g, D_STATE)
    cc = cm.astype(jnp.float32).reshape(b, nc, q, g, D_STATE)
    cum = jnp.cumsum(dtc * a.reshape(g, r), axis=2)
    causal = jnp.tril(jnp.ones((q, q), bool))[None, None, :, :, None, None]
    seg = cum[:, :, :, None] - cum[:, :, None, :]
    decay = jnp.exp(jnp.where(causal, seg, -jnp.inf))
    cb = jnp.einsum('bcign,bcjgn->bcijg', cc, bc)
    y_diag = jnp.einsum('bcijgr,bcjgrp->bcigrp', cb[..., None] * decay * dtc[:, :, None], xc)
    to_end = jnp.exp(cum[:, :, -1:] - cum) * dtc
    states = jnp.einsum('bcjgn,bcjgr,bcjgrp->bcgrpn', bc, to_end, xc)
    chunk_decay = jnp.exp(cum[:, :, -1])

    def step(hc, inp):
        dec, st = inp
        return dec[..., None, None] * hc + st, hc

    h_last, h_prev = lax.scan(step, h0.astype(jnp.float32).reshape(b, g, r, hp, D_STATE),
                              (jnp.moveaxis(chunk_decay, 1, 0), jnp.moveaxis(states, 1, 0)))
    h_prev = jnp.moveaxis(h_prev, 0, 1)
    y_off = jnp.einsum('bcign,bcigr,bcgrpn->bcigrp', cc, jnp.exp(cum), h_prev)
    return (y_diag + y_off).reshape(b, s, nh, hp), h_last.reshape(b, nh, hp, D_STATE)

def ssm_mixer(z, xbc, dt_raw, conv_prior, h0, conv_w, conv_b, dt_bias, a_log, d_skip, ssm_norm):
    b, t = z.shape[:2]
    xc, conv_state = causal_conv(xbc, conv_prior, conv_w, conv_b)
    xs, bm, cm = jnp.split(xc, [D_SSM, D_SSM + SSM_GROUPS * D_STATE], axis=-1)
    xs = xs.reshape(b, t, N_HEADS_S, SSM_HEAD_DIM)
    bm = bm.reshape(b, t, SSM_GROUPS, D_STATE)
    cm = cm.reshape(b, t, SSM_GROUPS, D_STATE)
    dt = jax.nn.softplus(dt_raw.astype(jnp.float32) + dt_bias.astype(jnp.float32))
    a = -jnp.exp(a_log.astype(jnp.float32))
    y, h_last = ssd(xs, dt, a, bm, cm, h0)
    y = y + xs.astype(jnp.float32) * d_skip.astype(jnp.float32)[:, None]
    y = y.reshape(b, t, D_SSM) * jax.nn.silu(z.astype(jnp.float32))
    yg = y.reshape(b, t, SSM_GROUPS, D_SSM // SSM_GROUPS)
    yg = yg * lax.rsqrt(jnp.mean(yg * yg, axis=-1, keepdims=True) + EPS)
    y = yg.reshape(b, t, D_SSM) * ssm_norm.astype(jnp.float32)
    return y.astype(z.dtype), conv_state, h_last

def residual_out(x, attn_o, ssm_o, w_out, norm_ffn, w_up, w_down):
    h = x + jnp.concatenate([attn_o, ssm_o], axis=-1) @ w_out
    u = rmsnorm(h, norm_ffn) @ w_up
    return h + jnp.square(jax.nn.relu(u)) @ w_down

def setup_inputs(seed: int = 0) -> dict:
    key = jax.random.key(seed)
    ks = jax.random.split(key, 24)
    nrm = jax.random.normal
    win_buf = min(MAX_WINDOW, PAST_LEN)

    def gain(k, n):
        return 1.0 + 0.05 * nrm(k, (DEPTH, n), jnp.float32)

    dt0 = jnp.exp(jax.random.uniform(ks[12], (DEPTH, N_HEADS_S), jnp.float32, math.log(1e-3), math.log(1e-1)))
    return {
        'x_prompt': nrm(ks[0], (BATCH, SEQ, D_MODEL), jnp.float32),
        'x_sample': nrm(ks[1], (DEC_BATCH, DEC_SEQ, D_MODEL), jnp.float32),
        'cache_attn_k': nrm(ks[2], (DEPTH, DEC_BATCH, win_buf, N_HEADS_A, HEAD_DIM), jnp.float32),
        'cache_attn_v': nrm(ks[3], (DEPTH, DEC_BATCH, win_buf, N_HEADS_A, HEAD_DIM), jnp.float32),
        'state_conv': nrm(ks[4], (DEPTH, DEC_BATCH, CONV_WIDTH - 1, CONV_DIM), jnp.float32),
        'state_ssm': 0.1 * nrm(ks[5], (DEPTH, DEC_BATCH, N_HEADS_S, SSM_HEAD_DIM, D_STATE), jnp.float32),
        'norm_mix': gain(ks[6], D_MODEL),
        'w_in': nrm(ks[7], (DEPTH, D_MODEL, D_IN_PROJ), jnp.float32) * D_MODEL ** -0.5,
        'q_norm': gain(ks[8], HEAD_DIM),
        'k_norm': gain(ks[9], HEAD_DIM),
        'rel_bias': 0.5 * nrm(ks[10], (N_BUCKETS, N_HEADS_A), jnp.float32),
        'conv_w': nrm(ks[11], (DEPTH, CONV_WIDTH, CONV_DIM), jnp.float32) * CONV_WIDTH ** -0.5,
        'conv_b': 0.01 * nrm(ks[13], (DEPTH, CONV_DIM), jnp.float32),
        'dt_bias': dt0 + jnp.log(-jnp.expm1(-dt0)),
        'a_log': jnp.log(jax.random.uniform(ks[14], (DEPTH, N_HEADS_S), jnp.float32, 1.0, 16.0)),
        'd_skip': 1.0 + 0.1 * nrm(ks[15], (DEPTH, N_HEADS_S), jnp.float32),
        'ssm_norm': gain(ks[16], D_SSM),
        'w_out': nrm(ks[17], (DEPTH, D_MIX, D_MODEL), jnp.float32) * D_MIX ** -0.5,
        'norm_ffn': gain(ks[18], D_MODEL),
        'w_up': nrm(ks[19], (DEPTH, D_MODEL, D_FF), jnp.float32) * D_MODEL ** -0.5,
        'w_down': nrm(ks[20], (DEPTH, D_FF, D_MODEL), jnp.float32) * D_FF ** -0.5,
    }

def reference(x_prompt, x_sample, cache_attn_k, cache_attn_v, state_conv, state_ssm,
              norm_mix, w_in, q_norm, k_norm, rel_bias, conv_w, conv_b, dt_bias, a_log,
              d_skip, ssm_norm, w_out, norm_ffn, w_up, w_down):
    yp, ys = x_prompt, x_sample
    bp, sp = yp.shape[:2]
    bs, ts = ys.shape[:2]
    keep = min(MAX_WINDOW, sp)
    kp_rows, vp_rows, conv_p, ssm_p = [], [], [], []
    ks_rows, vs_rows, conv_s, ssm_s = [], [], [], []
    for l in range(DEPTH):
        ssm_params = (conv_w[l], conv_b[l], dt_bias[l], a_log[l], d_skip[l], ssm_norm[l])
        ffn_params = (w_out[l], norm_ffn[l], w_up[l], w_down[l])
        q, k, v, z, xbc, dt_raw = project(yp, norm_mix[l], w_in[l], q_norm[l], k_norm[l])
        attn = merge_branches([dilated_branch_prompt(q, k, v, rel_bias, w, d) for w, d in DILATED_BRANCHES])
        attn = attn.reshape(bp, sp, D_ATTN).astype(yp.dtype)
        conv0 = jnp.zeros((bp, CONV_WIDTH - 1, CONV_DIM), yp.dtype)
        h0 = jnp.zeros((bp, N_HEADS_S, SSM_HEAD_DIM, D_STATE), jnp.float32)
        ssm_o, cst, hst = ssm_mixer(z, xbc, dt_raw, conv0, h0, *ssm_params)
        kp_rows.append(k[:, sp - keep:])
        vp_rows.append(v[:, sp - keep:])
        conv_p.append(cst)
        ssm_p.append(hst.astype(yp.dtype))
        yp = residual_out(yp, attn, ssm_o, *ffn_params)
        qs, kn, vn, zs, xbcs, dts = project(ys, norm_mix[l], w_in[l], q_norm[l], k_norm[l])
        k_all = jnp.concatenate([cache_attn_k[l].astype(kn.dtype), kn], axis=1)
        v_all = jnp.concatenate([cache_attn_v[l].astype(vn.dtype), vn], axis=1)
        attn_s = merge_branches([dilated_branch_sample(qs, k_all, v_all, rel_bias, w, d) for w, d in DILATED_BRANCHES])
        attn_s = attn_s.reshape(bs, ts, D_ATTN).astype(ys.dtype)
        ssm_os, csts, hsts = ssm_mixer(zs, xbcs, dts, state_conv[l].astype(ys.dtype), state_ssm[l], *ssm_params)
        ks_rows.append(kn)
        vs_rows.append(vn)
        conv_s.append(csts)
        ssm_s.append(hsts.astype(state_ssm.dtype))
        ys = residual_out(ys, attn_s, ssm_os, *ffn_params)
    new_k_prompt = jnp.stack(kp_rows)
    new_v_prompt = jnp.stack(vp_rows)
    new_conv_prompt = jnp.stack(conv_p)
    new_ssm_prompt = jnp.stack(ssm_p)
    new_k_sample = jnp.stack(ks_rows)
    new_v_sample = jnp.stack(vs_rows)
    new_conv_sample = jnp.stack(conv_s)
    new_ssm_sample = jnp.stack(ssm_s)
    return (yp, ys, new_k_prompt, new_v_prompt, new_conv_prompt, new_ssm_prompt,
            new_k_sample, new_v_sample, new_conv_sample, new_ssm_sample)


_drawn_inputs = setup_inputs


def setup_inputs(seed=0):
    import zlib

    import numpy as np

    out = dict(_drawn_inputs(seed))
    spreads = {}
    factors = {'q_norm': 8.0, 'conv_b': 2.808}
    for name, (base, spread) in spreads.items():
        noise = np.random.default_rng([zlib.crc32(name.encode()), seed]).standard_normal(out[name].shape)
        drawn = base * np.exp(spread * noise) if base else spread * noise
        out[name] = jnp.asarray(drawn.astype(out[name].dtype))
    for name, factor in factors.items():
        out[name] = (out[name] * factor).astype(out[name].dtype)
    return out
```

```python
import math
from contextlib import ExitStack, contextmanager

import numpy as np
import concourse.bass as bass
from concourse import mybir
from concourse.alu_op_type import AluOpType as ALU

ACT = mybir.ActivationFunctionType
F32 = mybir.dt.float32
F32R = mybir.dt.float32r
AX = mybir.AxisListType.X

P = 128
D = 1024
KD = D // P
SEQ = 1024
NT = SEQ // P
NB_DEC, T_DEC = 8, 4
NS = NB_DEC * T_DEC
NTOK = SEQ + NS
NPAD = SEQ + P
PAST = 1024
HD = 64
NH = D // HD
NPAIR = NH // 2
XBC = 1536
NSTATE = 128
WIDTH = 4
DFF = 4 * D
EPS = 1e-6
QK_TILES, XBC_TILES, Z_TILES = 2 * KD, XBC // P, KD
START = 1
NEG = -1e30
BRANCHES = ((128, 1), (512, 4), (2048, 16))
NBUCKET = 32
LMAX = PAST + T_DEC - 1
LLEN = LMAX + P
FAR = P
DENSE = 512
NKEY = FAR + DENSE + T_DEC
VT = (FAR + DENSE) // P
GROUPS = ((0, 512), (512, 512), (1024, NS))
FC = 512
FT = FC // P
NFC = DFF // FC

C_IDENT, C_UPPER, C_LOWER, C_ONES, C_HEADONE = 0, P, 2 * P, 3 * P, 4 * P
C_UPPER_S, C_LOWER_S = 5 * P, 5 * P + NS
C_BMASK = C_LOWER_S + NS
C_BROW = C_BMASK + NB_DEC * NS
C_DIAG = C_BROW + NB_DEC
C_SEL = C_DIAG + D
C_END = C_SEL + T_DEC


def shape_constants():
    c = np.zeros((P, C_END), np.float32)
    r = np.arange(P)
    c[:, C_IDENT:C_IDENT + P] = np.eye(P)
    c[:, C_UPPER:C_UPPER + P] = r[:, None] <= r[None, :]
    c[:, C_LOWER:C_LOWER + P] = r[:, None] > r[None, :]
    c[:, C_ONES:C_ONES + P] = 1.0
    c[:, C_HEADONE:C_HEADONE + P] = r[:, None] // HD == r[None, :] // HD
    s = np.arange(NS)
    same = s[:, None] // T_DEC == s[None, :] // T_DEC
    c[:NS, C_UPPER_S:C_UPPER_S + NS] = same & (s[:, None] <= s[None, :])
    c[:NS, C_LOWER_S:C_LOWER_S + NS] = same & (s[:, None] > s[None, :])
    for b in range(NB_DEC):
        c[:, C_BMASK + b * NS:C_BMASK + (b + 1) * NS] = (s // T_DEC == b)[None, :]
        c[:NS, C_BROW + b] = s // T_DEC == b
    ht = np.arange(NH * T_DEC)
    c[:len(ht), C_DIAG:C_DIAG + D] = ht[:, None] // T_DEC == np.arange(D)[None, :] // HD
    c[:len(ht), C_SEL:C_SEL + T_DEC] = ht[:, None] % T_DEC == np.arange(T_DEC)[None, :]
    return c


def distance_constants():
    dist = LMAX - np.arange(LLEN)
    exact = NBUCKET // 2
    df = np.maximum(dist, 1).astype(np.float32)
    top = max(w for w, _ in BRANCHES)
    large = exact + (np.log(df / np.float32(exact)) / np.float32(math.log(top / exact))
                     * np.float32(NBUCKET - exact)).astype(np.int32)
    bucket = np.where(dist < exact, np.maximum(dist, 0), np.minimum(large, NBUCKET - 1))
    out = np.zeros((NBUCKET + 1, LLEN), np.float32)
    out[bucket, np.arange(LLEN)] = 1.0
    count = sum(((dist >= 0) & (dist <= w) & (dist % d == 0)).astype(np.int32) for w, d in BRANCHES)
    out[NBUCKET] = np.where(count > 0, np.log(np.maximum(count, 1)), NEG)
    return out


class Kit:

    def __init__(self, nc, stack, dram):
        self.nc, self.stack = nc, stack
        self.dram = dram
        self.const = stack.enter_context(nc.sbuf_tensor("const", [P, C_END], F32))
        self.part_stack, self.unprimed = None, []
        self.const_loaded = self.sems("const_loaded")
        self.skewed = self.sems("bias_skewed")

    def sems(self, name, n=1):
        made = [(self.part_stack or self.stack).enter_context(self.nc.semaphore(f"{name}{i}")) for i in range(n)]
        if self.part_stack:
            self.part_sems += made
            self.unprimed += made
        return made if n > 1 else made[0]

    @contextmanager
    def part(self):
        with ExitStack() as self.part_stack:
            self.part_sems = []
            names = ("tensor", "vector", "gpsimd")
            engines = (self.nc.tensor, self.nc.vector, self.nc.gpsimd)
            self.settled = {e.engine: self.sems(f"settled_{n}") for n, e in zip(names, engines)}
            yield
            used = self.part_sems
            with self.nc.Block() as block:
                @block.gpsimd
                def _(pool):
                    for sem in used:
                        pool.sem_clear(sem)
        self.part_stack, self.unprimed = None, []

    def prime(self, pool):
        for sem in self.unprimed:
            pool.sem_inc(sem, START)
        self.unprimed = []

    def settle(self, eng):
        eng.sem_inc(self.settled[eng.engine], 1)

    def c(self, start, width, rows=P):
        return self.const[0:rows, start:start + width]


def split_matmuls(pe, out, w_hi, w_lo, x_hi, x_lo, first, last):
    pe.matmul(out, w_hi, x_hi, start=first, stop=False)
    pe.matmul(out, w_hi, x_lo, start=False, stop=False)
    return pe.matmul(out, w_lo, x_hi, start=False, stop=last)


def load_constants(kit):
    nc = kit.nc
    with nc.Block() as block:
        @block.gpsimd
        def _(pool):
            kit.prime(pool)

        @block.sync
        def _(sp):
            sp.dma_start(kit.const[:], kit.dram["consts"]).then_inc(kit.const_loaded, 16)
            sp.wait_ge(kit.const_loaded, 16)


def distance_table(kit):
    nc, dram = kit.nc, kit.dram
    with ExitStack() as mem:
        onehot = mem.enter_context(nc.sbuf_tensor("onehot", [NBUCKET + 1, LLEN], F32))
        bias = mem.enter_context(nc.sbuf_tensor("bias_aug", [NBUCKET + 1, NH], F32))
        table = mem.enter_context(nc.sbuf_tensor("table", [NH, LLEN], F32))
        acc = mem.enter_context(nc.psum_tensor("table_ps", [P, 3 * 512], F32))
        loaded, made, copied, stored = (kit.sems(f"dist_{n}") for n in ("loaded", "made", "copied", "stored"))
        ones_set = kit.sems("dist_ones")
        with nc.Block() as block:
            @block.gpsimd
            def _(pool):
                kit.prime(pool)

            @block.sync
            def _(sp):
                sp.dma_start(onehot[:], dram["onehot"]).then_inc(loaded, 16)
                sp.dma_start(bias[0:NBUCKET, :], dram["rel_bias"]).then_inc(loaded, 16)
                sp.wait_ge(copied, START + 1)
                sp.dma_start(dram["table"], table[:]).then_inc(stored, 16)
                sp.wait_ge(stored, START + 16)
                table_of, rows = dram["table"].tensor, dram["bias_rows"].rearrange("(h p) c -> h p c", h=NH)
                sp.dma_start(rows, bass.AP(table_of, LMAX - (NT - 1) * P, [[LLEN, NH], [-1, P], [1, SEQ]])
                             ).then_inc(kit.skewed, 16)
                rows = dram["bias_sample"].rearrange("(h t) c -> h t c", h=NH)
                for t in range(T_DEC):
                    sp.dma_start(rows[:, t, 0:FAR].rearrange("h (g r) -> h g r", r=4),
                                 bass.AP(table_of, LMAX - PAST - t, [[LLEN, NH], [16, FAR // 4], [1, 4]])
                                 ).then_inc(kit.skewed, 16)
                    sp.dma_start(rows[:, t, FAR:NKEY],
                                 bass.AP(table_of, LMAX - DENSE - t, [[LLEN, NH], [1, DENSE + T_DEC]])
                                 ).then_inc(kit.skewed, 16)

            @block.vector
            def _(dve):
                dve.memset(bias[NBUCKET:NBUCKET + 1, :], 1.0).then_inc(ones_set, 1)

            @block.tensor
            def _(pe):
                pe.wait_ge(loaded, START + 32)
                pe.wait_ge(ones_set, START + 1)
                for c in range(0, LLEN, 512):
                    w = min(512, LLEN - c)
                    mm = pe.matmul(acc[0:NH, c:c + w], bias[:], onehot[:, c:c + w], start=True, stop=True)
                mm.then_inc(made, 1)

            @block.scalar
            def _(act):
                act.wait_ge(made, START + 1)
                act.activation(table[:], acc[0:NH, 0:LLEN], ACT.Copy).then_inc(copied, 1)


def rms_split(kit, name, x, loads, gain, x_hi, x_lo):
    nc = kit.nc
    with ExitStack() as mem:
        sq = mem.enter_context(nc.sbuf_tensor(f"{name}_sq", [P, 2, NTOK], F32))
        rinv = mem.enter_context(nc.sbuf_tensor(f"{name}_rinv", [P, NTOK], F32))
        u = mem.enter_context(nc.sbuf_tensor(f"{name}_u", [P, 2, NTOK], F32))
        eps = mem.enter_context(nc.sbuf_tensor(f"{name}_eps", [P, 1], F32))
        acc = mem.enter_context(nc.psum_tensor(f"{name}_ps", [P, 3 * 512], F32))
        loaded = kit.sems(f"{name}_loaded", KD)
        squared, summed = kit.sems(f"{name}_squared", 2), kit.sems(f"{name}_summed", 2)
        rooted, inverted = kit.sems(f"{name}_rooted"), kit.sems(f"{name}_inverted")
        scaled, hi_made, lo_made = (kit.sems(f"{name}_{n}", 2) for n in ("scaled", "hi", "lo"))
        eps_set = kit.sems(f"{name}_eps")
        with nc.Block() as block:
            @block.gpsimd
            def _(pool):
                kit.prime(pool)

            @block.sync
            def _(sp):
                for k, pairs in enumerate(loads):
                    for dst, src in pairs:
                        sp.dma_start(dst, src).then_inc(loaded[k], 16)

            @block.scalar
            def _(act):
                for k in range(KD):
                    if loads:
                        act.wait_ge(loaded[k], START + 16 * len(loads[k]))
                    if k >= 2:
                        act.wait_ge(summed[k % 2], START + k // 2)
                    act.activation(sq[:, k % 2, :], x[:, k, :], ACT.Square).then_inc(squared[k % 2], 1)
                act.wait_ge(summed[(KD - 1) % 2], START + KD // 2)
                act.wait_ge(eps_set, START + 1)
                act.activation(rinv[:], acc[:, 0:NTOK], ACT.Sqrt, bias=eps[:], scale=1.0 / D).then_inc(rooted, 1)
                for k in range(KD):
                    act.wait_ge(scaled[k % 2], START + k // 2 + 1)
                    act.activation(x_hi[:, k, 0:NTOK], u[:, k % 2, :], ACT.Copy).then_inc(hi_made[k % 2], 1)

            @block.tensor
            def _(pe):
                for k in range(KD):
                    pe.wait_ge(squared[k % 2], START + k // 2 + 1)
                    for c, w in GROUPS:
                        mm = pe.matmul(acc[:, c:c + w], kit.c(C_ONES, P), sq[:, k % 2, c:c + w],
                                       start=(k == 0), stop=(k == KD - 1))
                    mm.then_inc(summed[k % 2], 1)

            @block.vector
            def _(dve):
                dve.memset(eps[:], EPS).then_inc(eps_set, 1)
                dve.wait_ge(rooted, START + 1)
                dve.reciprocal(rinv[:], rinv[:]).then_inc(inverted, 1)
                dve.wait_ge(inverted, START + 1)
                for k in range(KD):
                    if k >= 2:
                        dve.wait_ge(lo_made[k % 2], START + k // 2)
                    dve.scalar_tensor_tensor(out=u[:, k % 2, :], in0=x[:, k, :], scalar=gain[:, k:k + 1],
                                             in1=rinv[:], op0=ALU.mult, op1=ALU.mult).then_inc(scaled[k % 2], 1)
                    dve.wait_ge(hi_made[k % 2], START + k // 2 + 1)
                    dve.tensor_tensor(x_lo[:, k, 0:NTOK], u[:, k % 2, :], x_hi[:, k, 0:NTOK].bitcast(F32),
                                      ALU.subtract).then_inc(lo_made[k % 2], 1)
                dve.wait_ge(lo_made[(KD - 1) % 2], START + KD // 2)


def project(kit, x_hi, x_lo, gains):
    nc, dram = kit.nc, kit.dram
    NQ, NX, NZ = QK_TILES, XBC_TILES, Z_TILES
    with ExitStack() as mem:
        def sb(n, s, d=F32):
            return mem.enter_context(nc.sbuf_tensor(n, s, d))

        w_raw, w_hi, w_lo = sb("w_raw", [P, 2, D]), sb("w_hi", [P, 2, KD, P], F32R), sb("w_lo", [P, 2, KD, P], F32R)
        out = sb("proj_out", [P, 2, NTOK])
        raw, sq, rinv = sb("proj_raw", [P, 2, NTOK]), sb("proj_sq", [P, 2, NTOK]), sb("proj_rinv", [P, 2, NTOK])
        pre = sb("conv_pre", [P, 2, WIDTH - 1 + SEQ])
        pre_s = sb("conv_pre_s", [P, 2, NB_DEC, WIDTH - 1 + T_DEC])
        past_s = sb("conv_past", [P, XBC_TILES, NB_DEC * (WIDTH - 1)])
        taps = sb("conv_taps", [P, XBC_TILES, WIDTH + 1])
        tap = sb("conv_tap", [P, 2, WIDTH + 1])
        tail = sb("conv_tail", [P, XBC_TILES, (NB_DEC + 1) * (WIDTH - 1)])
        gain = sb("qk_gain", [P, 2, 1])
        eps = sb("qk_eps", [P, 1])
        acc = [mem.enter_context(nc.psum_tensor(f"proj_ps{j}", [P, 3 * 512], F32)) for j in range(2)]
        ssq = [mem.enter_context(nc.psum_tensor(f"proj_ss{j}", [P, 512], F32)) for j in range(2)]

        w_loaded, w_hi_made, w_split = (kit.sems(f"w_{n}", 2) for n in ("loaded", "hi", "split"))
        made, freed = kit.sems("proj_made", 2), kit.sems("proj_freed", 2)
        squared = kit.sems("qk_squared", 2)
        summed, rooted = kit.sems("qk_summed", 2), kit.sems("qk_rooted", 2)
        inverted, normed = kit.sems("qk_inverted", 2), kit.sems("qk_normed", 2)
        gained = kit.sems("qk_gained", 2)
        stored = kit.sems("proj_stored", 2)
        small = kit.sems("proj_small")
        zeroed = kit.sems("proj_zeroed")
        tapped, padded, conv, activated = (kit.sems(f"conv_{n}", 2) for n in ("tapped", "padded", "mac", "silu"))
        tails, tail_stored = kit.sems("conv_tails", 2), kit.sems("tail_stored")
        z_silu = kit.sems("z_silu", 2)

        def tile_range(kind):
            return {"qk": (0, NQ // 2), "xbc": (NQ // 2, NX // 2), "z": ((NQ + NX) // 2, NZ // 2)}[kind]

        with nc.Block() as block:
            @block.sync
            def _(sp):
                sp.dma_start(taps[:], dram["conv_taps"]).then_inc(small, 16)
                sp.dma_start(past_s[:], dram["conv_past"]).then_inc(small, 16)
                with sp.Fori(0, (NQ + NX + NZ) // 2) as i:
                    for j in range(2):
                        sp.wait_ge(w_split[j], START + i)
                        sp.dma_start(w_raw[:, j, :], dram["w_feat"][bass.ds(2 * i + j, 1)]
                                     .rearrange("o p c -> p (o c)")).then_inc(w_loaded[j], 16)

            @block.gpsimd
            def _(pool):
                kit.prime(pool)
                with pool.Fori(0, (NQ + NX + NZ) // 2) as i:
                    for j in range(2):
                        pool.wait_ge(w_loaded[j], START + 16 * (i + 1))
                        pool.wait_ge(made[j], START + i)
                        raw_w = w_raw[:, j, :].rearrange("p (k m) -> p k m", k=KD)
                        kit.settle(pool)
                        pool.tensor_copy(w_hi[:, j], raw_w).then_inc(w_hi_made[j], 1)
                        pool.wait_ge(w_hi_made[j], START + i + 1)
                        pool.tensor_tensor(w_lo[:, j], raw_w, w_hi[:, j].bitcast(F32),
                                           ALU.subtract).then_inc(w_split[j], 1)

            @block.tensor
            def _(pe):
                def main(n, j):
                    pe.wait_ge(w_split[j], START + n + 1)
                    pe.wait_ge(freed[j], START + n)
                    for k in range(KD):
                        for wt, xt in ((w_hi, x_hi), (w_hi, x_lo), (w_lo, x_hi)):
                            for c, w in GROUPS:
                                first = k == 0 and wt is w_hi and xt is x_hi
                                last = k == KD - 1 and wt is w_lo
                                mm = pe.matmul(acc[j][:, c:c + w], wt[:, j, k, :], xt[:, k, c:c + w],
                                               start=first, stop=last)
                    mm.then_inc(made[j], 1)

                def head_sums(n, j):
                    pe.wait_ge(squared[j], START + n + 1)
                    for g, (c, w) in enumerate(GROUPS):
                        s = g % 2
                        if s == 0:
                            pe.wait_ge(rooted[0], START + 2 * (2 * n + j) + g // 2)
                        else:
                            pe.wait_ge(rooted[1], START + 2 * n + j)
                        pe.matmul(ssq[s][:, 0:w], kit.c(C_HEADONE, P), sq[:, j, c:c + w],
                                  start=True, stop=True).then_inc(summed[s], 1)

                main(0, 0)
                with pe.Fori(0, NQ // 2 - 1) as i:
                    main(i, 1)
                    head_sums(i, 0)
                    main(i + 1, 0)
                    head_sums(i, 1)
                main(NQ // 2 - 1, 1)
                head_sums(NQ // 2 - 1, 0)
                head_sums(NQ // 2 - 1, 1)
                with pe.Fori(NQ // 2, (NQ + NX + NZ) // 2) as i:
                    main(i, 0)
                    main(i, 1)

            @block.scalar
            def _(act):
                act.wait_ge(zeroed, START + 4)
                with act.Fori(0, NQ // 2) as i:
                    for j in range(2):
                        act.wait_ge(made[j], START + i + 1)
                        act.wait_ge(normed[j], START + i)
                        if True:
                            act.activation(raw[:, j, :], acc[j][:, 0:NTOK], ACT.Copy)
                        act.activation(sq[:, j, :], acc[j][:, 0:NTOK], ACT.Square).then_inc(squared[j], 1)
                        act.wait_ge(squared[j], START + i + 1)
                        act.sem_inc(freed[j], 1)
                        for g, (c, w) in enumerate(GROUPS):
                            s = g % 2
                            n = 2 * (2 * i + j) + g // 2 if s == 0 else 2 * i + j
                            act.wait_ge(summed[s], START + n + 1)
                            act.activation(rinv[:, j, c:c + w], ssq[s][:, 0:w], ACT.Sqrt, bias=eps[:],
                                           scale=1.0 / HD).then_inc(rooted[s], 1)
                        act.wait_ge(normed[j], START + i + 1)
                        act.dma_start(dram["qk"][bass.ds((2 * i + j) * P, P), :], out[:, j, :]).then_inc(stored[j], 16)

                base, pairs = tile_range("xbc")
                with act.Fori(0, pairs) as i:
                    for j in range(2):
                        act.wait_ge(made[j], START + i + base + 1)
                        act.wait_ge(conv[j], START + i * WIDTH)
                        act.wait_ge(tails[j], START + i)
                        act.activation(pre[:, j, WIDTH - 1:], acc[j][:, 0:SEQ], ACT.Copy)
                        act.activation(pre_s[:, j, :, WIDTH - 1:],
                                       acc[j][:, SEQ:NTOK].rearrange("p (b t) -> p b t", b=NB_DEC),
                                       ACT.Copy).then_inc(padded[j], 1)
                        act.wait_ge(padded[j], START + i + 1)
                        act.sem_inc(freed[j], 1)
                        act.wait_ge(conv[j], START + (i + 1) * WIDTH)
                        act.activation(out[:, j, :], raw[:, j, :], ACT.Silu,
                                       bias=tap[:, j, WIDTH:WIDTH + 1]).then_inc(activated[j], 1)
                        act.wait_ge(activated[j], START + i + 1)
                        act.dma_start(dram["xbc"][bass.ds((2 * i + j) * P, P), :], out[:, j, :]).then_inc(stored[j], 16)

                zbase, zpairs = tile_range("z")
                with act.Fori(0, zpairs) as i:
                    for j in range(2):
                        act.wait_ge(made[j], START + i + zbase + 1)
                        act.wait_ge(stored[j], START + 16 * (i + zbase))
                        act.activation(out[:, j, :], acc[j][:, 0:NTOK], ACT.Silu).then_inc(z_silu[j], 1)
                        act.wait_ge(z_silu[j], START + i + 1)
                        act.sem_inc(freed[j], 1)
                        act.dma_start(dram["z"][bass.ds((2 * i + j) * P, P), :], out[:, j, :]).then_inc(stored[j], 16)
                for j in range(2):
                    act.wait_ge(stored[j], START + 16 * (NQ + NX + NZ) // 2)
                act.wait_ge(tails[0], START + NX // 2)
                act.wait_ge(tails[1], START + NX // 2)
                act.dma_start(dram["conv_tail"], tail[:].rearrange("p f c -> p (f c)")).then_inc(tail_stored, 16)
                act.wait_ge(tail_stored, START + 16)

            @block.vector
            def _(dve):
                dve.memset(eps[:], EPS).then_inc(zeroed, 1)
                dve.memset(pre[:, :, 0:WIDTH - 1], 0.0).then_inc(zeroed, 1)
                dve.memset(x_hi[:, :, NTOK:NPAD].bitcast(F32), 0.0).then_inc(zeroed, 1)
                dve.memset(x_lo[:, :, NTOK:NPAD].bitcast(F32), 0.0).then_inc(zeroed, 1)
                dve.wait_ge(small, START + 32)
                with dve.Fori(0, NQ // 2) as i:
                    for j in range(2):
                        dve.wait_ge(normed[j], START + i)
                        dve.tensor_copy(gain[:, j, :], gains[:, bass.ds(2 * i + j, 1)]).then_inc(gained[j], 1)
                        dve.wait_ge(rooted[0], START + 2 * (2 * i + j) + 2)
                        dve.wait_ge(rooted[1], START + 2 * i + j + 1)
                        dve.reciprocal(rinv[:, j, :], rinv[:, j, :]).then_inc(inverted[j], 1)
                        dve.wait_ge(inverted[j], START + i + 1)
                        dve.wait_ge(gained[j], START + i + 1)
                        dve.wait_ge(stored[j], START + 16 * i)
                        dve.scalar_tensor_tensor(out=out[:, j, :], in0=raw[:, j, :], scalar=gain[:, j, :],
                                                 in1=rinv[:, j, :], op0=ALU.mult, op1=ALU.mult).then_inc(normed[j], 1)
                for j in range(2):
                    dve.wait_ge(normed[j], START + NQ // 2)
                base, pairs = tile_range("xbc")
                with dve.Fori(0, pairs) as i:
                    for j in range(2):
                        f = bass.ds(2 * i + j, 1)
                        dve.wait_ge(activated[j], START + i)
                        dve.tensor_copy(tap[:, j, :], taps[:, f, :].rearrange("p o t -> p (o t)"))
                        dve.tensor_copy(pre_s[:, j, :, 0:WIDTH - 1],
                                        past_s[:, f, :].rearrange("p o (b t) -> p (o b) t", b=NB_DEC)
                                        ).then_inc(tapped[j], 1)
                        dve.wait_ge(tapped[j], START + i + 1)
                        dve.wait_ge(padded[j], START + i + 1)
                        dve.wait_ge(stored[j], START + 16 * (i + base))
                        acc_p = raw[:, j, 0:SEQ]
                        acc_s = raw[:, j, SEQ:NTOK].rearrange("p (b t) -> p b t", b=NB_DEC)
                        for t in range(WIDTH):
                            w = tap[:, j, t:t + 1]
                            if t == 0:
                                dve.tensor_scalar(acc_p, pre[:, j, 0:SEQ], w, None, ALU.mult)
                                dve.tensor_scalar(acc_s, pre_s[:, j, :, 0:T_DEC], w, None,
                                                  ALU.mult).then_inc(conv[j], 1)
                            else:
                                dve.wait_ge(conv[j], START + i * WIDTH + t)
                                dve.scalar_tensor_tensor(out=acc_p, in0=pre[:, j, t:t + SEQ], scalar=w,
                                                         in1=acc_p, op0=ALU.mult, op1=ALU.add)
                                dve.scalar_tensor_tensor(out=acc_s, in0=pre_s[:, j, :, t:t + T_DEC], scalar=w,
                                                         in1=acc_s, op0=ALU.mult, op1=ALU.add).then_inc(conv[j], 1)
                        dve.tensor_copy(tail[:, f, 0:WIDTH - 1].rearrange("p o t -> p (o t)"),
                                        pre[:, j, SEQ:SEQ + WIDTH - 1])
                        dve.tensor_copy(tail[:, f, WIDTH - 1:].rearrange("p o (b t) -> p (o b) t", b=NB_DEC),
                                        pre_s[:, j, :, T_DEC:]).then_inc(tails[j], 1)


def project_tokens(kit, x_hi, x_lo):
    nc, dram = kit.nc, kit.dram
    NTT = NT + 1
    NV = D + NH
    with ExitStack() as mem:
        def sb(n, s, d=F32):
            return mem.enter_context(nc.sbuf_tensor(n, s, d))

        w_raw = sb("wv_raw", [P, 2, NV])
        w_hi, w_lo = sb("wv_hi", [P, KD, NV], F32R), sb("wv_lo", [P, KD, NV], F32R)
        v_out = sb("v_out", [P, 2, D])
        dt_raw, dt_abs, dt_exp, dt_all = (sb(n, [P, NTT, NH]) for n in ("dt_raw", "dt_abs", "dt_exp", "dt_all"))
        bias = sb("dt_bias", [P, NH])
        acc = [mem.enter_context(nc.psum_tensor(f"v_ps{j}", [P, 3 * 512], F32)) for j in range(2)]
        w_loaded, w_hi_made, w_split = (kit.sems(f"wv_{n}", 2) for n in ("loaded", "hi", "split"))
        made, v_copied, dt_copied, stored = (kit.sems(f"v_{n}", 2) for n in ("made", "copied", "dt", "stored"))
        small, soft, dt_stored = kit.sems("dt_small"), kit.sems("dt_soft"), kit.sems("dt_stored")

        with nc.Block() as block:
            @block.sync
            def _(sp):
                sp.dma_start(bias[:], dram["dt_bias"].partition_broadcast(P)).then_inc(small, 16)
                for k in range(KD):
                    if k >= 2:
                        sp.wait_ge(w_split[k % 2], START + k // 2)
                    sp.dma_start(w_raw[:, k % 2, :], dram["w_tok"][k]).then_inc(w_loaded[k % 2], 16)

            @block.gpsimd
            def _(pool):
                kit.prime(pool)
                for k in range(KD):
                    pool.wait_ge(w_loaded[k % 2], START + 16 * (k // 2 + 1))
                    pool.tensor_copy(w_hi[:, k, :], w_raw[:, k % 2, :]).then_inc(w_hi_made[k % 2], 1)
                    pool.wait_ge(w_hi_made[k % 2], START + k // 2 + 1)
                    pool.tensor_tensor(w_lo[:, k, :], w_raw[:, k % 2, :], w_hi[:, k, :].bitcast(F32),
                                       ALU.subtract).then_inc(w_split[k % 2], 1)

            @block.tensor
            def _(pe):
                for t in range(NTT):
                    j = t % 2
                    if t >= 2:
                        pe.wait_ge(v_copied[j], START + t // 2)
                        pe.wait_ge(dt_copied[j], START + t // 2)
                    for k in range(KD):
                        if t == 0:
                            pe.wait_ge(w_split[k % 2], START + k // 2 + 1)
                        tok = slice(t * P, (t + 1) * P)
                        for wt, xt in ((w_hi, x_hi), (w_lo, x_hi), (w_hi, x_lo)):
                            for c, w in ((0, 512), (512, 512), (1024, NH)):
                                mm = pe.matmul(acc[j][:, c:c + w], xt[:, k, tok], wt[:, k, c:c + w],
                                               start=(k == 0 and wt is w_hi and xt is x_hi),
                                               stop=(k == KD - 1 and xt is x_lo))
                    mm.then_inc(made[j], 1)

            @block.scalar
            def _(act):
                for t in range(NTT):
                    j = t % 2
                    act.wait_ge(made[j], START + t // 2 + 1)
                    if t >= 2:
                        act.wait_ge(stored[j], START + 16 * (t // 2))
                    act.activation(v_out[:, j, :], acc[j][:, 0:D], ACT.Copy).then_inc(v_copied[j], 1)
                    act.wait_ge(v_copied[j], START + t // 2 + 1)
                    act.dma_start(dram["v"][t * P:(t + 1) * P, :], v_out[:, j, :]).then_inc(stored[j], 16)
                act.wait_ge(soft, START + 2)
                act.activation(dt_exp[:], dt_abs[:], ACT.Exp).then_inc(soft, 1)
                act.wait_ge(soft, START + 3)
                act.activation(dt_abs[:], dt_exp[:], ACT.Ln, bias=1.0).then_inc(soft, 1)
                act.wait_ge(soft, START + 5)
                act.dma_start(dram["dt"].rearrange("(t p) h -> p t h", p=P), dt_all[:]).then_inc(dt_stored, 16)
                act.wait_ge(dt_stored, START + 16)
                for j in range(2):
                    act.wait_ge(stored[j], START + 16 * ((NTT + 1 - j) // 2))

            @block.vector
            def _(dve):
                dve.wait_ge(small, START + 16)
                for t in range(NTT):
                    j = t % 2
                    dve.wait_ge(v_copied[j], START + t // 2 + 1)
                    dve.tensor_tensor(dt_raw[:, t, :], acc[j][:, D:NV], bias[:], ALU.add).then_inc(dt_copied[j], 1)
                dve.wait_ge(dt_copied[0], START + (NTT + 1) // 2)
                dve.wait_ge(dt_copied[1], START + NTT // 2)
                dve.tensor_scalar(dt_all[:], dt_raw[:], -1.0, None, ALU.mult).then_inc(soft, 1)
                dve.wait_ge(soft, START + 1)
                dve.tensor_tensor(dt_abs[:], dt_all[:], dt_raw[:], ALU.min).then_inc(soft, 1)
                dve.wait_ge(soft, START + 4)
                dve.scalar_tensor_tensor(out=dt_all[:], in0=dt_raw[:], scalar=0.0, in1=dt_abs[:],
                                         op0=ALU.max, op1=ALU.add).then_inc(soft, 1)


def attend_prompt(kit):
    nc, dram = kit.nc, kit.dram
    NQT = NT
    ITEMS = 2 * NQT
    PIECES = sum(-(-(i + 1) // 4) for i in range(NQT)) * 2
    with ExitStack() as mem:
        def sb(n, s, d=F32):
            return mem.enter_context(nc.sbuf_tensor(n, s, d))

        qT, kT, v = sb("att_q", [P, 2, SEQ]), sb("att_k", [P, 2, SEQ]), sb("att_v", [P, 2, NT, P])
        bias = sb("att_bias", [P, 2, 2, SEQ])
        logits, probs, turned = sb("att_s", [P, 2, SEQ]), sb("att_p", [P, 2, SEQ]), sb("att_pT", [P, 2, NT, P])
        top, neg, den, rden = (sb(f"att_{n}", [P, 2, 1]) for n in ("max", "negmax", "den", "rden"))
        o_tok, oT = sb("att_o", [P, 2, P]), sb("att_oT", [P, 2, SEQ])
        s_ps = [mem.enter_context(nc.psum_tensor(f"att_s_ps{j}", [P, 1024], F32)) for j in range(2)]
        t_ps = [mem.enter_context(nc.psum_tensor(f"att_t_ps{j}", [P, 512], F32)) for j in range(2)]
        pv_ps = mem.enter_context(nc.psum_tensor("att_pv_ps", [P, 512], F32))
        ot_ps = mem.enter_context(nc.psum_tensor("att_ot_ps", [P, 512], F32))

        loaded, stored, pair_done = (kit.sems(f"att_{n}", 2) for n in ("loaded", "stored", "pair"))
        scored, biased, negated, exped = (kit.sems(f"att_{n}", 2) for n in ("scored", "biased", "negated", "exped"))
        flipped, turned_done = kit.sems("att_flipped", 2), kit.sems("att_turned", 2)
        multiplied, inverted = kit.sems("att_multiplied", 2), kit.sems("att_inverted", 2)
        normed = kit.sems("att_normed", 2)
        o_flipped, o_turned = kit.sems("att_o_flipped"), kit.sems("att_o_turned")

        def items():
            return [(jp, jp * ITEMS + 2 * qt + h, qt, h) for jp in range(2) for qt in range(NQT) for h in range(2)]

        def pieces():
            out, n = [], 0
            for _, _, qt, _ in items():
                row = []
                for b0 in range(0, qt + 1, 4):
                    row.append((n, b0, min(4, qt + 1 - b0)))
                    n += 1
                out.append(row)
            assert n == 2 * PIECES
            return out

        with nc.Block() as block:
            @block.gpsimd
            def _(pool):
                kit.prime(pool)

            @block.sync
            def _(sp):
                sp.wait_ge(kit.skewed, 16 * (1 + 2 * T_DEC))
                with sp.Fori(0, NPAIR // 2) as i:
                    for jp in range(2):
                        pair = 2 * i + jp
                        sp.wait_ge(pair_done[jp], START + i)
                        sp.dma_start(qT[:, jp, :], dram["qk"][bass.ds(pair * P, P), 0:SEQ]).then_inc(loaded[jp], 16)
                        sp.dma_start(kT[:, jp, :], dram["qk"][bass.ds(pair * P + D, P), 0:SEQ]).then_inc(loaded[jp], 16)
                        sp.dma_start(v[:, jp], dram["v"][0:SEQ, bass.ds(pair * P, P)]
                                     .rearrange("(t p) c -> p t c", p=P)).then_inc(loaded[jp], 16)
                        for h in range(2):
                            sp.dma_start(bias[:, jp, h, :], dram["bias_rows"][bass.ds((2 * pair + h) * P, P), :]
                                         ).then_inc(loaded[jp], 16)

            @block.tensor
            def _(pe):
                todo, parts = items(), pieces()

                def score(i, jp, m, qt, h):
                    j = m % 2
                    if (m % ITEMS) == 0:
                        pe.wait_ge(loaded[jp], START + 80 * (i + 1))
                    pe.wait_ge(biased[j], START + ITEMS * i + m // 2)
                    rows = slice(h * HD, (h + 1) * HD)
                    for c in range(0, (qt + 1) * P, 512):
                        w = min(512, (qt + 1) * P - c)
                        mm = pe.matmul(s_ps[j][:, c:c + w], qT[rows, jp, qt * P:(qt + 1) * P],
                                       kT[rows, jp, c:c + w], start=True, stop=True)
                    mm.then_inc(scored[j], 1)

                def weigh(i, jp, m, qt, h, row):
                    j = m % 2
                    pe.wait_ge(exped[j], START + ITEMS * i + m // 2 + 1)
                    for n, b0, nb in row:
                        s = n % 2
                        pe.wait_ge(turned_done[s], START + PIECES * i + n // 2)
                        for b in range(nb):
                            mm = pe.transpose(t_ps[s][:, b * P:(b + 1) * P],
                                              probs[:, j, (b0 + b) * P:(b0 + b + 1) * P], kit.c(C_IDENT, P))
                        mm.then_inc(flipped[s], 1)

                def values(i, jp, m, qt, h, row):
                    j = m % 2
                    if m:
                        pe.wait_ge(normed[1 - j], START + ITEMS * i + (m - 1) // 2 + 1)
                    else:
                        pe.wait_ge(normed[1], START + ITEMS * i)
                    for b in range(qt + 1):
                        for n, b0, nb in row:
                            if b == b0:
                                pe.wait_ge(turned_done[n % 2], START + PIECES * i + n // 2 + 1)
                        mm = pe.matmul(pv_ps[:, 0:HD], turned[:, j, b, :], v[:, jp, b, h * HD:(h + 1) * HD],
                                       start=(b == 0), stop=(b == qt))
                    mm.then_inc(multiplied[j], 1)

                def turn_out(i, m):
                    pe.wait_ge(normed[1], START + ITEMS * i + m // 2 + 1)
                    pe.wait_ge(normed[0], START + ITEMS * i + m // 2 + 1)
                    pe.wait_ge(o_turned, START + ITEMS * i + m // 2)
                    pe.transpose(ot_ps[:, 0:P], o_tok[:, (m // 2) % 2, :], kit.c(C_IDENT, P)).then_inc(o_flipped, 1)

                with pe.Fori(0, NPAIR // 2) as i:
                    score(i, *todo[0])
                    for n, it in enumerate(todo):
                        if n + 1 < len(todo):
                            score(i, *todo[n + 1])
                        weigh(i, *it, parts[n])
                        if n >= 1 and n % 2 == 0:
                            turn_out(i, n - 1)
                        values(i, *it, parts[n])
                    turn_out(i, len(todo) - 1)

            @block.vector
            def _(dve):
                def bias_max(i, jp, m, qt, h):
                    j, w = m % 2, (qt + 1) * P
                    dve.wait_ge(scored[j], START + ITEMS * i + m // 2 + 1)
                    dve.wait_ge(exped[j], START + ITEMS * i + m // 2)
                    kit.settle(dve)
                    dve.tensor_tensor_reduce(out=logits[:, j, 0:w], in0=s_ps[j][:, 0:w],
                                             in1=bias[:, jp, h, SEQ - w:SEQ], scale=1.0, scalar=-3e38,
                                             op0=ALU.add, op1=ALU.max,
                                             accum_out=top[:, j, :]).then_inc(biased[j], 1)
                    dve.wait_ge(biased[j], START + ITEMS * i + m // 2 + 1)
                    dve.tensor_scalar(neg[:, j, :], top[:, j, :], -1.0, None, ALU.mult).then_inc(negated[j], 1)

                def keep_turned(i, m, row):
                    for n, b0, nb in row:
                        if n % 2 == 1:
                            dve.wait_ge(flipped[1], START + PIECES * i + n // 2 + 1)
                            dve.wait_ge(multiplied[m % 2], START + ITEMS * i + m // 2)
                            dve.tensor_copy(turned[:, m % 2, b0:b0 + nb, :].rearrange("p b q -> p (b q)"),
                                            t_ps[1][:, 0:nb * P]).then_inc(turned_done[1], 1)

                def norm_out(i, jp, m, qt, h):
                    j = m % 2
                    dve.wait_ge(exped[j], START + ITEMS * i + m // 2 + 1)
                    dve.reciprocal(rden[:, j, :], den[:, j, :]).then_inc(inverted[j], 1)
                    dve.wait_ge(inverted[j], START + ITEMS * i + m // 2 + 1)
                    dve.wait_ge(multiplied[j], START + ITEMS * i + m // 2 + 1)
                    if m // 2 >= 2:
                        dve.wait_ge(o_flipped, START + ITEMS * i + m // 2 - 1)
                    else:
                        dve.wait_ge(o_flipped, START + ITEMS * i)
                    dve.tensor_scalar(o_tok[:, (m // 2) % 2, h * HD:(h + 1) * HD], pv_ps[:, 0:HD],
                                      rden[:, j, :], None, ALU.mult).then_inc(normed[j], 1)

                todo, parts = items(), pieces()
                with dve.Fori(0, NPAIR // 2) as i:
                    dve.wait_ge(loaded[0], START + 80 * (i + 1))
                    bias_max(i, *todo[0])
                    for n, it in enumerate(todo):
                        if n + 1 < len(todo):
                            if (n + 1) % ITEMS == 0:
                                dve.wait_ge(loaded[1], START + 80 * (i + 1))
                            bias_max(i, *todo[n + 1])
                        keep_turned(i, it[1], parts[n])
                        norm_out(i, *it)

            @block.scalar
            def _(act):
                def keep_out(i, g):
                    jp, qt = g // NQT, g % NQT
                    act.wait_ge(o_flipped, START + ITEMS * i + g + 1)
                    if qt == 0:
                        act.wait_ge(stored[jp], START + 16 * i)
                    act.activation(oT[:, jp, qt * P:(qt + 1) * P], ot_ps[:, 0:P], ACT.Copy).then_inc(o_turned, 1)
                    if qt == NQT - 1:
                        act.wait_ge(o_turned, START + ITEMS * i + g + 1)
                        act.sem_inc(pair_done[jp], 1)
                        act.dma_start(dram["mix"][bass.ds((2 * i + jp) * P, P), 0:SEQ], oT[:, jp, :]).then_inc(stored[jp], 16)

                todo, parts = items(), pieces()
                with act.Fori(0, NPAIR // 2) as i:
                    for n, (jp, m, qt, h) in enumerate(todo):
                        j, w = m % 2, (qt + 1) * P
                        act.wait_ge(negated[j], START + ITEMS * i + m // 2 + 1)
                        act.wait_ge(inverted[j], START + ITEMS * i + m // 2)
                        if n >= 2:
                            for pn, _, _ in parts[n - 2]:
                                act.wait_ge(flipped[pn % 2], START + PIECES * i + pn // 2 + 1)
                        else:
                            act.wait_ge(flipped[0], START + PIECES * i)
                            act.wait_ge(flipped[1], START + PIECES * i)
                        act.activation(probs[:, j, 0:w], logits[:, j, 0:w], ACT.Exp, bias=neg[:, j, :],
                                       accum_out=den[:, j, :]).then_inc(exped[j], 1)
                        for pn, b0, nb in parts[n]:
                            if pn % 2 == 0:
                                act.wait_ge(flipped[0], START + PIECES * i + pn // 2 + 1)
                                act.wait_ge(multiplied[j], START + ITEMS * i + m // 2)
                                act.activation(turned[:, j, b0:b0 + nb, :].rearrange("p b q -> p (b q)"),
                                               t_ps[0][:, 0:nb * P], ACT.Copy).then_inc(turned_done[0], 1)
                        if n >= 2 and n % 2 == 0:
                            keep_out(i, n // 2 - 1)
                    keep_out(i, len(todo) // 2 - 1)
                for jp in range(2):
                    act.wait_ge(stored[jp], START + 16 * (NPAIR // 2))


def attend_sample(kit):
    nc, dram = kit.nc, kit.dram
    R = NH * T_DEC
    with ExitStack() as mem:
        def sb(n, s, d=F32):
            return mem.enter_context(nc.sbuf_tensor(n, s, d))

        kT, v = sb("sa_k", [P, 2, NPAIR, NKEY]), sb("sa_v", [P, 2, VT, D])
        v_new = sb("sa_vnew", [T_DEC, 2, D])
        q_all, k_new = sb("sa_q", [P, NPAIR, NS]), sb("sa_knew", [P, NPAIR, NS])
        q_diag = sb("sa_qdiag", [P, 2, NPAIR, R])
        bias = sb("sa_bias", [R, NKEY])
        logits, probs = sb("sa_s", [R, 2, NKEY]), sb("sa_p", [R, 2, NKEY])
        turned, turned_new = sb("sa_pT", [P, 2, VT, R]), sb("sa_pTn", [T_DEC, 2, R])
        top, neg, den, rden = (sb(f"sa_{n}", [R, 2, 1]) for n in ("max", "negmax", "den", "rden"))
        own, o_tok = sb("sa_own", [R, 2, D]), sb("sa_o", [T_DEC, 2, D])
        oT = sb("sa_oT", [P, KD, NS])
        s_ps = mem.enter_context(nc.psum_tensor("sa_s_ps", [P, 1024], F32))
        t_ps = mem.enter_context(nc.psum_tensor("sa_t_ps", [P, 512], F32))
        pv_ps = mem.enter_context(nc.psum_tensor("sa_pv_ps", [P, 1024], F32))
        o_ps = mem.enter_context(nc.psum_tensor("sa_o_ps", [P, 1024], F32))
        ot_ps = mem.enter_context(nc.psum_tensor("sa_ot_ps", [P, 512], F32))

        loaded, placed = kit.sems("sa_loaded", 2), kit.sems("sa_placed", 2)
        common, zeroed, placing = kit.sems("sa_common"), kit.sems("sa_zeroed"), kit.sems("sa_placing")
        scored, biased, negated, exped = (kit.sems(f"sa_{n}", 2) for n in ("scored", "biased", "negated", "exped"))
        flipped, turned_done, multiplied = (kit.sems(f"sa_{n}", 2) for n in ("flipped", "turned", "multiplied"))
        inverted, owned, gathered, copied = (kit.sems(f"sa_{n}", 2) for n in ("inverted", "owned", "gathered", "copied"))
        o_turned, o_kept, stored = kit.sems("sa_oturned"), kit.sems("sa_okept"), kit.sems("sa_stored")

        with nc.Block() as block:
            @block.sync
            def _(sp):
                qk = dram["qk"].rearrange("(f p) t -> p f t", p=P)
                sp.dma_start(q_all[:], qk[:, 0:NPAIR, SEQ:NTOK]).then_inc(common, 16)
                sp.dma_start(k_new[:], qk[:, NPAIR:2 * NPAIR, SEQ:NTOK]).then_inc(common, 16)
                sp.dma_start(bias[:], dram["bias_sample"]).then_inc(common, 16)
                with sp.Fori(0, NB_DEC // 2) as i:
                    for j in range(2):
                        b = 2 * i + j
                        sp.wait_ge(multiplied[j], START + i)
                        sp.dma_start(kT[:, j, :, 0:FAR + DENSE], dram["cache_k"][bass.ds(b, 1)]
                                     .rearrange("o p (f t) -> p (o f) t", f=NPAIR)).then_inc(loaded[j], 16)
                        sp.dma_start(v[:, j], dram["cache_v"][bass.ds(b, 1)]
                                     .rearrange("o p (t c) -> p (o t) c", t=VT)).then_inc(loaded[j], 16)
                        sp.dma_start(v_new[:, j, :], dram["v"][bass.ds(b * T_DEC + SEQ, T_DEC), :]).then_inc(loaded[j], 16)

            @block.gpsimd
            def _(pool):
                kit.prime(pool)
                pool.memset(q_diag[:], 0.0).then_inc(zeroed, 1)
                pool.wait_ge(zeroed, START + 1)
                pool.wait_ge(common, START + 48)
                with pool.Fori(0, NB_DEC // 2) as i:
                    for j in range(2):
                        tok = bass.ds((2 * i + j) * T_DEC, T_DEC)
                        pool.wait_ge(scored[j], START + i)
                        pool.tensor_copy(kT[:, j, :, FAR + DENSE:], k_new[:, :, tok]).then_inc(placing, 1)
                        for h in range(2):
                            pool.wait_ge(placing, START + 2 * (2 * i + j) + h + 1)
                            rows = q_diag[h * HD:(h + 1) * HD, j]
                            cols = bass.AP(rows.tensor, rows.offset + h * T_DEC,
                                           [list(rows.ap[0]), [R + 2 * T_DEC, NPAIR], [1, T_DEC]])
                            pool.tensor_copy(cols, q_all[h * HD:(h + 1) * HD, :, tok]).then_inc(
                                placed[j] if h else placing, 1)
                        pool.wait_ge(placed[j], START + i + 1)

            @block.tensor
            def _(pe):
                with pe.Fori(0, NB_DEC // 2) as i:
                    for j in range(2):
                        pe.wait_ge(loaded[j], START + 48 * (i + 1))
                        pe.wait_ge(placed[j], START + i + 1)
                        if j:
                            pe.wait_ge(biased[0], START + i + 1)
                        else:
                            pe.wait_ge(biased[1], START + i)
                        for f in range(NPAIR):
                            for c, w in ((0, 512), (512, NKEY - 512)):
                                mm = pe.matmul(s_ps[0:R, c:c + w], q_diag[:, j, f, :], kT[:, j, f, c:c + w],
                                               start=(f == 0), stop=(f == NPAIR - 1))
                        mm.then_inc(scored[j], 1)
                        pe.wait_ge(exped[j], START + i + 1)
                        if j:
                            pe.wait_ge(turned_done[0], START + i + 1)
                        else:
                            pe.wait_ge(turned_done[1], START + i)
                        kit.settle(pe)
                        for t in range(VT):
                            pe.transpose(t_ps[:, t * R:(t + 1) * R], probs[:, j, t * P:(t + 1) * P],
                                         kit.c(C_IDENT, R, R))
                        pe.transpose(t_ps[0:T_DEC, VT * R:(VT + 1) * R], probs[:, j, VT * P:NKEY],
                                     kit.c(C_IDENT, R, R)).then_inc(flipped[j], 1)
                        pe.wait_ge(turned_done[j], START + i + 1)
                        if j:
                            pe.wait_ge(owned[0], START + i + 1)
                        else:
                            pe.wait_ge(owned[1], START + i)
                        for c in (0, 512):
                            for t in range(VT):
                                pe.matmul(pv_ps[0:R, c:c + 512], turned[:, j, t, :], v[:, j, t, c:c + 512],
                                          start=(t == 0), stop=False)
                            mm = pe.matmul(pv_ps[0:R, c:c + 512], turned_new[:, j, :], v_new[:, j, c:c + 512],
                                           start=False, stop=True)
                        mm.then_inc(multiplied[j], 1)
                        pe.wait_ge(owned[j], START + i + 1)
                        if j:
                            pe.wait_ge(copied[0], START + i + 1)
                        else:
                            pe.wait_ge(copied[1], START + i)
                        kit.settle(pe)
                        for c in (0, 512):
                            mm = pe.matmul(o_ps[0:T_DEC, c:c + 512], kit.c(C_SEL, T_DEC, R), own[:, j, c:c + 512],
                                           start=True, stop=True)
                        mm.then_inc(gathered[j], 1)
                        pe.wait_ge(copied[j], START + i + 1)
                        if j:
                            pe.wait_ge(o_kept, START + 2 * i + 1)
                        else:
                            pe.wait_ge(o_kept, START + 2 * i)
                        kit.settle(pe)
                        for f in range(KD):
                            mm = pe.transpose(ot_ps[:, f * T_DEC:(f + 1) * T_DEC], o_tok[:, j, f * P:(f + 1) * P],
                                              kit.c(C_IDENT, T_DEC, T_DEC))
                        mm.then_inc(o_turned, 1)

            @block.vector
            def _(dve):
                dve.wait_ge(common, START + 48)
                with dve.Fori(0, NB_DEC // 2) as i:
                    for j in range(2):
                        dve.wait_ge(scored[j], START + i + 1)
                        dve.wait_ge(exped[j], START + i)
                        kit.settle(dve)
                        dve.tensor_tensor_reduce(out=logits[:, j, :], in0=s_ps[0:R, 0:NKEY], in1=bias[:], scale=1.0,
                                                 scalar=-3e38, op0=ALU.add, op1=ALU.max,
                                                 accum_out=top[:, j, :]).then_inc(biased[j], 1)
                        dve.wait_ge(biased[j], START + i + 1)
                        dve.tensor_scalar(neg[:, j, :], top[:, j, :], -1.0, None, ALU.mult).then_inc(negated[j], 1)
                        dve.wait_ge(exped[j], START + i + 1)
                        dve.reciprocal(rden[:, j, :], den[:, j, :]).then_inc(inverted[j], 1)
                        dve.wait_ge(inverted[j], START + i + 1)
                        dve.wait_ge(multiplied[j], START + i + 1)
                        dve.wait_ge(gathered[j], START + i)
                        dve.scalar_tensor_tensor(out=own[:, j, :], in0=pv_ps[0:R, :], scalar=rden[:, j, :],
                                                 in1=kit.c(C_DIAG, D, R), op0=ALU.mult, op1=ALU.mult).then_inc(owned[j], 1)
                        dve.wait_ge(o_turned, START + 2 * i + j + 1)
                        dve.tensor_copy(oT[:, :, bass.ds((2 * i + j) * T_DEC, T_DEC)],
                                        ot_ps[:, 0:KD * T_DEC].rearrange("p (f t) -> p f t", f=KD)).then_inc(o_kept, 1)

            @block.scalar
            def _(act):
                with act.Fori(0, NB_DEC // 2) as i:
                    for j in range(2):
                        act.wait_ge(negated[j], START + i + 1)
                        act.wait_ge(inverted[j], START + i)
                        act.wait_ge(flipped[j], START + i)
                        act.activation(probs[:, j, :], logits[:, j, :], ACT.Exp, bias=neg[:, j, :],
                                       accum_out=den[:, j, :]).then_inc(exped[j], 1)
                        act.wait_ge(flipped[j], START + i + 1)
                        act.wait_ge(multiplied[j], START + i)
                        act.activation(turned[:, j].rearrange("p t r -> p (t r)"), t_ps[:, 0:VT * R], ACT.Copy)
                        act.activation(turned_new[:, j, :], t_ps[0:T_DEC, VT * R:(VT + 1) * R],
                                       ACT.Copy).then_inc(turned_done[j], 1)
                        act.wait_ge(gathered[j], START + i + 1)
                        act.wait_ge(o_turned, START + 2 * i + j)
                        act.activation(o_tok[:, j, :], o_ps[0:T_DEC, :], ACT.Copy).then_inc(copied[j], 1)
                act.wait_ge(o_kept, START + NB_DEC)
                act.dma_start(dram["mix"][0:D, SEQ:NTOK].rearrange("(f p) t -> p f t", p=P), oT[:]).then_inc(stored, 16)
                act.wait_ge(stored, START + 16)


def scan_prompt(kit, neg_a, skip):
    nc, dram = kit.nc, kit.dram
    HG = NH // 2
    with ExitStack() as mem:
        def sb(n, s, d=F32):
            return mem.enter_context(nc.sbuf_tensor(n, s, d))

        def ps(n, w):
            return mem.enter_context(nc.psum_tensor(n, [P, w], F32))

        xbc, zT, dt = sb("ssd_xbc", [P, 2, XBC_TILES, P]), sb("ssd_z", [P, 2, KD, P]), sb("ssd_dt", [P, 2, NH])
        dta, decays = sb("ssd_dta", [P, NH]), sb("ssd_decays", [P, 3, NH])
        x_tok, xdt, xw = sb("ssd_x", [P, D]), sb("ssd_xdt", [P, D]), sb("ssd_xw", [P, D])
        b_tok, cb = sb("ssd_btok", [P, 2 * P]), sb("ssd_cb", [P, 2, P])
        steps, mixm = sb("ssd_steps", [P, 2, 4, P]), sb("ssd_m", [P, 4, 4, P])
        y, yT, state = sb("ssd_y", [P, D]), sb("ssd_yT", [P, 2, KD, P]), sb("ssd_state", [P, D])
        skipped = sb("ssd_skip", [P, KD, P])
        turn_ps, misc_ps, seg_ps = ps("ssd_turn", D), ps("ssd_misc", 512), ps("ssd_seg", 512)
        in_ps, off_ps = ps("ssd_in", D), ps("ssd_off", D)

        loaded = kit.sems("ssd_loaded", 2)
        (zeroed, dta_made, x_turned, bcb_made, sums_made, sums_exp, x_kept, xdt_made, xw_made, btok_kept, cb_masked,
         steps_made, seg_made, seg_exp, mix_made, in_made, off_made, y_scaled, y_summed, y_turned, skip_made, y_skipped,
         state_made, state_decayed, state_summed) = (kit.sems(f"ssd_{n}") for n in (
             "zeroed", "dta_done", "xturned", "bcb", "sums", "sumsexp", "xkept", "xdtdone", "xwdone", "btokkept",
             "cbmasked", "stepsdone", "segdone", "segexp", "mixdone", "indone", "offdone", "yscaled", "ysummed",
             "yturned", "skipdone", "yskipped", "stdone", "stdecayed", "stsummed"))
        gated = kit.sems("ssd_gated", 2)
        stored, state_stored = kit.sems("ssd_stored", 2), kit.sems("ssd_ststored")

        def heads(ap):
            return ap.rearrange("p (h c) -> p h c", h=NH)

        def per_head(ap, w=HD):
            return ap.unsqueeze(2).broadcast_to([P, ap.shape[1], w])

        with nc.Block() as block:
            @block.sync
            def _(sp):
                def load(i, j):
                    sp.wait_ge(gated[j], START + i)
                    cols = bass.ds((2 * i + j) * P, P)
                    sp.dma_start(xbc[:, j], dram["xbc"][:, cols].rearrange("(f p) t -> p f t", p=P)).then_inc(loaded[j], 16)
                    sp.dma_start(zT[:, j], dram["z"][:, cols].rearrange("(f p) t -> p f t", p=P)).then_inc(loaded[j], 16)
                    sp.dma_start(dt[:, j, :], dram["dt"][cols, :]).then_inc(loaded[j], 16)

                def store(i, j):
                    sp.wait_ge(gated[j], START + i + 1)
                    sp.dma_start(dram["mix"][D:2 * D, bass.ds((2 * i + j) * P, P)].rearrange("(f p) t -> p f t", p=P),
                                 yT[:, j]).then_inc(stored[j], 16)

                load(0, 0)
                with sp.Fori(0, NT // 2 - 1) as i:
                    load(i, 1)
                    store(i, 0)
                    load(i + 1, 0)
                    store(i, 1)
                load(NT // 2 - 1, 1)
                store(NT // 2 - 1, 0)
                store(NT // 2 - 1, 1)
                for j in range(2):
                    sp.wait_ge(stored[j], START + 16 * (NT // 2))

            @block.tensor
            def _(pe):
                with pe.Fori(0, NT // 2) as i:
                    for j in range(2):
                        n = 2 * i + j
                        pe.wait_ge(loaded[j], START + 48 * (i + 1))
                        pe.wait_ge(y_skipped, START + n)
                        for f in range(KD):
                            mm = pe.transpose(turn_ps[:, f * P:(f + 1) * P], xbc[:, j, f, :], kit.c(C_IDENT, P))
                        mm.then_inc(x_turned, 1)
                        pe.wait_ge(btok_kept, START + n)
                        pe.wait_ge(cb_masked, START + n)
                        for g in range(2):
                            pe.transpose(misc_ps[:, g * P:(g + 1) * P], xbc[:, j, KD + g, :], kit.c(C_IDENT, P))
                        for g in range(2):
                            mm = pe.matmul(misc_ps[:, (2 + g) * P:(3 + g) * P], xbc[:, j, KD + g, :],
                                           xbc[:, j, KD + 2 + g, :], start=True, stop=True)
                        mm.then_inc(bcb_made, 1)
                        pe.wait_ge(dta_made, START + n + 1)
                        pe.wait_ge(seg_exp, START + 4 * n)
                        for s, m in enumerate((C_UPPER, C_LOWER, C_ONES)):
                            mm = pe.matmul(seg_ps[:, s * NH:(s + 1) * NH], kit.c(m, P), dta[:], start=True, stop=True)
                        mm.then_inc(sums_made, 1)
                        pe.wait_ge(state_summed, START + n)
                        pe.wait_ge(zeroed, START + 1)
                        for g in range(2):
                            mm = pe.matmul(off_ps[:, g * 512:(g + 1) * 512], xbc[:, j, KD + 2 + g, :],
                                           state[:, g * 512:(g + 1) * 512], start=True, stop=True)
                        mm.then_inc(off_made, 1)
                        for q in range(4):
                            pe.wait_ge(steps_made, START + 4 * n + q + 1)
                            if q == 0:
                                pe.wait_ge(sums_exp, START + n + 1)
                            else:
                                pe.wait_ge(seg_exp, START + 4 * n + q)
                            pe.matmul(seg_ps[:], kit.c(C_LOWER, P), steps[:, q % 2].rearrange("p h t -> p (h t)"),
                                      start=True, stop=True).then_inc(seg_made, 1)
                        pe.wait_ge(y_scaled, START + n + 1)
                        pe.wait_ge(xw_made, START + n + 1)
                        pe.wait_ge(btok_kept, START + n + 1)
                        for g in range(2):
                            mm = pe.matmul(off_ps[:, g * 512:(g + 1) * 512], b_tok[:, g * P:(g + 1) * P],
                                           xw[:, g * 512:(g + 1) * 512], start=True, stop=True)
                        mm.then_inc(state_made, 1)
                        for h in range(NH):
                            if h == 0:
                                pe.wait_ge(xdt_made, START + n + 1)
                                pe.wait_ge(y_summed, START + n)
                            if h % 4 == 0:
                                pe.wait_ge(mix_made, START + 4 * n + h // 4 + 1)
                            mm = pe.matmul(in_ps[:, h * HD:(h + 1) * HD], mixm[:, h // 4, h % 4, :],
                                           xdt[:, h * HD:(h + 1) * HD], start=True, stop=True)
                        mm.then_inc(in_made, 1)
                        pe.wait_ge(y_summed, START + n + 1)
                        for f in range(KD):
                            mm = pe.transpose(turn_ps[:, f * P:(f + 1) * P], y[:, f * P:(f + 1) * P], kit.c(C_IDENT, P))
                        mm.then_inc(y_turned, 1)

            @block.gpsimd
            def _(pool):
                kit.prime(pool)
                pool.memset(state[:], 0.0).then_inc(zeroed, 1)
                with pool.Fori(0, NT // 2) as i:
                    for j in range(2):
                        n = 2 * i + j
                        pool.wait_ge(loaded[j], START + 48 * (i + 1))
                        pool.wait_ge(sums_made, START + n)
                        pool.tensor_tensor(dta[:], dt[:, j, :], neg_a[:], ALU.mult).then_inc(dta_made, 1)
                        pool.wait_ge(dta_made, START + n + 1)
                        for q in range(4):
                            if q < 2:
                                pool.wait_ge(seg_made, START + 4 * n)
                            else:
                                pool.wait_ge(seg_made, START + 4 * n + q - 1)
                            pool.tensor_tensor(steps[:, q % 2], kit.c(C_UPPER, P).unsqueeze(1).broadcast_to([P, 4, P]),
                                               per_head(dta[:, 4 * q:4 * q + 4], P), ALU.mult).then_inc(steps_made, 1)
                        pool.wait_ge(x_kept, START + n + 1)
                        pool.wait_ge(in_made, START + n)
                        pool.tensor_tensor(heads(xdt[:]), heads(x_tok[:]), per_head(dt[:, j, :]), ALU.mult).then_inc(xdt_made, 1)
                        pool.wait_ge(xdt_made, START + n + 1)
                        pool.wait_ge(sums_exp, START + n + 1)
                        pool.wait_ge(state_made, START + n)
                        pool.tensor_tensor(heads(xw[:]), heads(xdt[:]), per_head(decays[:, 1, :]), ALU.mult).then_inc(xw_made, 1)
                        pool.wait_ge(y_skipped, START + n)
                        pool.tensor_tensor(skipped[:], xbc[:, j, 0:KD, :],
                                           skip[:].unsqueeze(2).broadcast_to([P, KD, P]), ALU.mult).then_inc(skip_made, 1)
                        pool.wait_ge(off_made, START + n + 1)
                        pool.tensor_tensor(heads(state[:]), heads(state[:]), per_head(decays[:, 2, :]),
                                           ALU.mult).then_inc(state_decayed, 1)

            @block.scalar
            def _(act):
                with act.Fori(0, NT // 2) as i:
                    for j in range(2):
                        n = 2 * i + j
                        act.wait_ge(x_turned, START + n + 1)
                        act.wait_ge(xdt_made, START + n)
                        act.activation(x_tok[:], turn_ps[:], ACT.Copy).then_inc(x_kept, 1)
                        act.wait_ge(bcb_made, START + n + 1)
                        act.wait_ge(state_made, START + n)
                        act.activation(b_tok[:], misc_ps[:, 0:2 * P], ACT.Copy).then_inc(btok_kept, 1)
                        act.wait_ge(sums_made, START + n + 1)
                        act.wait_ge(state_decayed, START + n)
                        act.wait_ge(y_scaled, START + n)
                        act.activation(decays[:].rearrange("p s h -> p (s h)"), seg_ps[:, 0:3 * NH],
                                       ACT.Exp).then_inc(sums_exp, 1)
                        for q in range(4):
                            act.wait_ge(seg_made, START + 4 * n + q + 1)
                            act.wait_ge(in_made, START + n)
                            act.activation(mixm[:, q].rearrange("p h t -> p (h t)"), seg_ps[:], ACT.Exp).then_inc(seg_exp, 1)

            @block.vector
            def _(dve):
                with dve.Fori(0, NT // 2) as i:
                    for j in range(2):
                        n = 2 * i + j
                        dve.wait_ge(btok_kept, START + n + 1)
                        dve.wait_ge(mix_made, START + 4 * n)
                        dve.tensor_tensor(cb[:], misc_ps[:, 2 * P:4 * P].rearrange("p (g t) -> p g t", g=2),
                                          kit.c(C_UPPER, P).unsqueeze(1).broadcast_to([P, 2, P]),
                                          ALU.mult).then_inc(cb_masked, 1)
                        dve.wait_ge(off_made, START + n + 1)
                        dve.wait_ge(sums_exp, START + n + 1)
                        dve.wait_ge(y_turned, START + n)
                        dve.tensor_tensor(heads(y[:]), heads(off_ps[:]), per_head(decays[:, 0, :]),
                                          ALU.mult).then_inc(y_scaled, 1)
                        dve.wait_ge(cb_masked, START + n + 1)
                        for q in range(4):
                            dve.wait_ge(seg_exp, START + 4 * n + q + 1)
                            dve.tensor_tensor(mixm[:, q], mixm[:, q], cb[:, q // 2, :].unsqueeze(1).broadcast_to([P, 4, P]),
                                              ALU.mult).then_inc(mix_made, 1)
                        dve.wait_ge(state_made, START + n + 1)
                        dve.wait_ge(state_decayed, START + n + 1)
                        dve.tensor_tensor(state[:], state[:], off_ps[:], ALU.add).then_inc(state_summed, 1)
                        dve.wait_ge(in_made, START + n + 1)
                        dve.wait_ge(y_scaled, START + n + 1)
                        dve.tensor_tensor(y[:], y[:], in_ps[:], ALU.add).then_inc(y_summed, 1)
                        dve.wait_ge(y_turned, START + n + 1)
                        dve.wait_ge(skip_made, START + n + 1)
                        dve.wait_ge(stored[j], START + 16 * i)
                        yt = yT[:, j].rearrange("p f t -> p (f t)")
                        dve.tensor_tensor(yt, turn_ps[:], skipped[:].rearrange("p f t -> p (f t)"),
                                          ALU.add).then_inc(y_skipped, 1)
                        dve.wait_ge(y_skipped, START + n + 1)
                        dve.tensor_tensor(yt, yt, zT[:, j].rearrange("p f t -> p (f t)"), ALU.mult).then_inc(gated[j], 1)

        with nc.Block() as block:
            @block.gpsimd
            def _(pool):
                kit.prime(pool)

            @block.sync
            def _(sp):
                sp.dma_start(dram["ssm_p"], state[:]).then_inc(state_stored, 16)
                sp.wait_ge(state_stored, START + 16)


def scan_sample(kit, neg_a, skip):
    nc, dram = kit.nc, kit.dram
    with ExitStack() as mem:
        def sb(n, s, d=F32):
            return mem.enter_context(nc.sbuf_tensor(n, s, d))

        def ps(n, w):
            return mem.enter_context(nc.psum_tensor(n, [P, w], F32))

        xbc, zT, dt = sb("ss_xbc", [P, XBC_TILES, NS]), sb("ss_z", [P, KD, NS]), sb("ss_dt", [NS, NH])
        dta, decays = sb("ss_dta", [NS, NH]), sb("ss_decays", [NS, 2, NH])
        x_tok, xdt, xw = sb("ss_x", [NS, D]), sb("ss_xdt", [NS, D]), sb("ss_xw", [NS, D])
        b_tok, cb = sb("ss_btok", [NS, 2 * P]), sb("ss_cb", [NS, 2, NS])
        steps, mixm = sb("ss_steps", [NS, NH, NS]), sb("ss_m", [NS, NH, NS])
        y, yT, skipped = sb("ss_y", [NS, D]), sb("ss_yT", [P, KD, NS]), sb("ss_skip", [P, KD, NS])
        off_sum = sb("ss_offsum", [NS, D])
        state, total = sb("ss_state", [P, 2, D]), sb("ss_total", [P, 2, NH])
        c_own, b_own, row_own = sb("ss_cown", [P, 2, 2, NS]), sb("ss_bown", [NS, 2, 2 * P]), sb("ss_rown", [NS, 2, P])
        turn_ps, misc_ps, seg_ps = ps("ss_turn", D), ps("ss_misc", 512), ps("ss_seg", 512)
        in_ps, off_ps = ps("ss_in", D), ps("ss_off", D)

        loaded, state_loaded = kit.sems("ss_loaded"), kit.sems("ss_stloaded", 2)
        (dta_made, x_turned, bc_made, sums_made, kept, cb_masked, steps_made, seg_made, seg_exp, mix_made, xdt_made,
         xw_made, in_made, in_kept, zeroed) = (kit.sems(f"ss_{n}") for n in (
             "dta_done", "xturned", "bc", "sums", "kept", "cbm", "stepsd", "segd", "sege", "mixd", "xdtd", "xwd",
             "ind", "ink", "zero"))
        owned, off_made, off_summed, state_made, total_exp, decayed, updated, state_stored = (
            kit.sems(f"ss_{n}", 2) for n in ("owned", "offd", "offs", "std", "totd", "dec", "upd", "sts"))
        finish = kit.sems("ss_finish")
        y_turned, stored = kit.sems("ss_yturned"), kit.sems("ss_stored")

        def heads(ap):
            return ap.rearrange("p (h c) -> p h c", h=NH)

        def per_head(ap, rows, w=HD):
            return ap.unsqueeze(2).broadcast_to([rows, NH, w])

        with nc.Block() as block:
            @block.gpsimd
            def _(pool):
                kit.prime(pool)

            @block.sync
            def _(sp):
                sp.dma_start(xbc[:], dram["xbc"][:, SEQ:NTOK].rearrange("(f p) t -> p f t", p=P)).then_inc(loaded, 16)
                sp.dma_start(zT[:], dram["z"][:, SEQ:NTOK].rearrange("(f p) t -> p f t", p=P)).then_inc(loaded, 16)
                sp.dma_start(dt[:], dram["dt"][SEQ:NTOK, :]).then_inc(loaded, 16)
                with sp.Fori(0, NB_DEC // 2) as i:
                    for j in range(2):
                        sp.wait_ge(state_stored[j], START + 16 * i)
                        sp.dma_start(state[:, j, :], dram["state_in"][bass.ds(2 * i + j, 1)]
                                     .rearrange("o n c -> n (o c)")).then_inc(state_loaded[j], 16)

            @block.tensor
            def _(pe):
                pe.wait_ge(loaded, START + 48)
                for f in range(KD):
                    mm = pe.transpose(turn_ps[0:NS, f * P:(f + 1) * P], xbc[:, f, :], kit.c(C_IDENT, P))
                mm.then_inc(x_turned, 1)
                for g in range(2):
                    pe.transpose(misc_ps[0:NS, g * P:(g + 1) * P], xbc[:, KD + g, :], kit.c(C_IDENT, P))
                for g in range(2):
                    mm = pe.matmul(misc_ps[0:NS, 2 * P + g * NS:2 * P + (g + 1) * NS], xbc[:, KD + g, :],
                                   xbc[:, KD + 2 + g, :], start=True, stop=True)
                mm.then_inc(bc_made, 1)
                pe.wait_ge(dta_made, START + 1)
                for s, m in enumerate((C_UPPER_S, C_LOWER_S)):
                    mm = pe.matmul(seg_ps[0:NS, s * NH:(s + 1) * NH], kit.c(m, NS, NS), dta[:], start=True, stop=True)
                mm.then_inc(sums_made, 1)
                pe.wait_ge(steps_made, START + 1)
                pe.wait_ge(kept, START + 3)
                pe.matmul(seg_ps[0:NS, :], kit.c(C_LOWER_S, NS, NS), steps[:].rearrange("p h t -> p (h t)"),
                          start=True, stop=True).then_inc(seg_made, 1)
                pe.wait_ge(mix_made, START + 1)
                pe.wait_ge(xdt_made, START + 1)
                for h in range(NH):
                    mm = pe.matmul(in_ps[0:NS, h * HD:(h + 1) * HD], mixm[:, h, :], xdt[:, h * HD:(h + 1) * HD],
                                   start=True, stop=True)
                mm.then_inc(in_made, 1)
                pe.wait_ge(in_kept, START + 1)
                pe.wait_ge(xw_made, START + 1)
                with pe.Fori(0, NB_DEC // 2) as i:
                    for j in range(2):
                        pe.wait_ge(state_loaded[j], START + 16 * (i + 1))
                        pe.wait_ge(owned[j], START + i + 1)
                        if j:
                            pe.wait_ge(off_summed[0], START + i + 1)
                        else:
                            pe.wait_ge(off_summed[1], START + i)
                        for g in range(2):
                            mm = pe.matmul(off_ps[0:NS, g * 512:(g + 1) * 512], c_own[:, j, g, :],
                                           state[:, j, g * 512:(g + 1) * 512], start=True, stop=True)
                        mm.then_inc(off_made[j], 1)
                        if j:
                            pe.wait_ge(updated[0], START + i + 1)
                        else:
                            pe.wait_ge(updated[1], START + i)
                        pe.matmul(misc_ps[:, 0:NH], row_own[:, j, :], dta[:], start=True, stop=True)
                        for g in range(2):
                            mm = pe.matmul(in_ps[:, g * 512:(g + 1) * 512], b_own[:, j, g * P:(g + 1) * P],
                                           xw[:, g * 512:(g + 1) * 512], start=True, stop=True)
                        mm.then_inc(state_made[j], 1)
                pe.wait_ge(finish, START + 3)
                for f in range(KD):
                    mm = pe.transpose(turn_ps[:, f * NS:(f + 1) * NS], y[:, f * P:(f + 1) * P], kit.c(C_IDENT, NS, NS))
                mm.then_inc(y_turned, 1)

            @block.scalar
            def _(act):
                act.wait_ge(x_turned, START + 1)
                act.activation(x_tok[:], turn_ps[0:NS, :], ACT.Copy).then_inc(kept, 1)
                act.wait_ge(bc_made, START + 1)
                act.activation(b_tok[:], misc_ps[0:NS, 0:2 * P], ACT.Copy).then_inc(kept, 1)
                act.wait_ge(sums_made, START + 1)
                act.activation(decays[:].rearrange("p s h -> p (s h)"), seg_ps[0:NS, 0:2 * NH], ACT.Exp).then_inc(kept, 1)
                act.wait_ge(seg_made, START + 1)
                act.activation(mixm[:].rearrange("p h t -> p (h t)"), seg_ps[0:NS, :], ACT.Exp).then_inc(seg_exp, 1)
                with act.Fori(0, NB_DEC // 2) as i:
                    for j in range(2):
                        act.wait_ge(state_made[j], START + i + 1)
                        act.wait_ge(updated[j], START + i)
                        act.activation(total[:, j, :], misc_ps[:, 0:NH], ACT.Exp).then_inc(total_exp[j], 1)
                        act.wait_ge(updated[j], START + i + 1)
                        act.dma_start(dram["ssm_s"][bass.ds(2 * i + j, 1)].rearrange("o n c -> n (o c)"),
                                      state[:, j, :]).then_inc(state_stored[j], 16)
                for j in range(2):
                    act.wait_ge(state_stored[j], START + 16 * (NB_DEC // 2))
                act.wait_ge(finish, START + 5)
                act.dma_start(dram["mix"][D:2 * D, SEQ:NTOK].rearrange("(f p) t -> p f t", p=P), yT[:]).then_inc(stored, 16)
                act.wait_ge(stored, START + 16)

            @block.vector
            def _(dve):
                dve.memset(off_sum[:], 0.0).then_inc(zeroed, 1)
                dve.wait_ge(loaded, START + 48)
                dve.tensor_tensor(dta[:], dt[:], neg_a[0:NS, :], ALU.mult).then_inc(dta_made, 1)
                dve.wait_ge(dta_made, START + 1)
                dve.tensor_tensor(steps[:], kit.c(C_UPPER_S, NS, NS).unsqueeze(1).broadcast_to([NS, NH, NS]),
                                  per_head(dta[:], NS, NS), ALU.mult).then_inc(steps_made, 1)
                dve.wait_ge(kept, START + 3)
                dve.tensor_tensor(heads(xdt[:]), heads(x_tok[:]), per_head(dt[:], NS), ALU.mult).then_inc(xdt_made, 1)
                dve.wait_ge(xdt_made, START + 1)
                dve.tensor_tensor(heads(xw[:]), heads(xdt[:]), per_head(decays[:, 1, :], NS), ALU.mult).then_inc(xw_made, 1)
                dve.tensor_tensor(cb[:], misc_ps[0:NS, 2 * P:2 * P + 2 * NS].rearrange("p (g t) -> p g t", g=2),
                                  kit.c(C_UPPER_S, NS, NS).unsqueeze(1).broadcast_to([NS, 2, NS]),
                                  ALU.mult).then_inc(cb_masked, 1)
                dve.wait_ge(cb_masked, START + 1)
                dve.wait_ge(seg_exp, START + 1)
                for g in range(2):
                    last = dve.tensor_tensor(mixm[:, g * NH // 2:(g + 1) * NH // 2, :], mixm[:, g * NH // 2:(g + 1) * NH // 2, :],
                                             cb[:, g, :].unsqueeze(1).broadcast_to([NS, NH // 2, NS]), ALU.mult)
                last.then_inc(mix_made, 1)
                dve.wait_ge(in_made, START + 1)
                dve.tensor_copy(y[:], in_ps[0:NS, :]).then_inc(in_kept, 1)
                dve.tensor_tensor(skipped[:], xbc[:, 0:KD, :], skip[:].unsqueeze(2).broadcast_to([P, KD, NS]),
                                  ALU.mult)
                dve.wait_ge(zeroed, START + 1)
                with dve.Fori(0, NB_DEC // 2) as i:
                    for j in range(2):
                        b = 2 * i + j
                        dve.wait_ge(state_made[j], START + i)
                        dve.tensor_tensor(c_own[:, j], xbc[:, KD + 2:KD + 4, :],
                                          kit.const[:, bass.ds(b * NS + C_BMASK, NS)].unsqueeze(1).broadcast_to([P, 2, NS]),
                                          ALU.mult)
                        own = kit.const[0:NS, bass.ds(b + C_BROW, 1)]
                        dve.tensor_tensor(b_own[:, j, :], b_tok[:], own.broadcast_to([NS, 2 * P]), ALU.mult)
                        dve.tensor_tensor(row_own[:, j, :], kit.c(C_ONES, P, NS), own.broadcast_to([NS, P]),
                                          ALU.mult).then_inc(owned[j], 1)
                        dve.wait_ge(off_made[j], START + i + 1)
                        if j:
                            dve.wait_ge(off_summed[0], START + i + 1)
                        else:
                            dve.wait_ge(off_summed[1], START + i)
                        dve.tensor_tensor(off_sum[:], off_sum[:], off_ps[0:NS, :], ALU.add).then_inc(off_summed[j], 1)
                        dve.wait_ge(total_exp[j], START + i + 1)
                        dve.tensor_tensor(heads(state[:, j, :]), heads(state[:, j, :]), per_head(total[:, j, :], P),
                                          ALU.mult).then_inc(decayed[j], 1)
                        dve.wait_ge(decayed[j], START + i + 1)
                        dve.tensor_tensor(state[:, j, :], state[:, j, :], in_ps[:], ALU.add).then_inc(updated[j], 1)
                dve.wait_ge(off_summed[1], START + NB_DEC // 2)
                dve.tensor_tensor(heads(off_sum[:]), heads(off_sum[:]), per_head(decays[:, 0, :], NS), ALU.mult).then_inc(finish, 1)
                dve.wait_ge(finish, START + 1)
                dve.tensor_tensor(y[:], y[:], off_sum[:], ALU.add).then_inc(finish, 2)
                dve.wait_ge(y_turned, START + 1)
                dve.tensor_tensor(yT[:].rearrange("p f t -> p (f t)"), turn_ps[:, 0:KD * NS],
                                  skipped[:].rearrange("p f t -> p (f t)"), ALU.add).then_inc(finish, 1)
                dve.wait_ge(finish, START + 4)
                dve.tensor_tensor(yT[:], yT[:], zT[:], ALU.mult).then_inc(finish, 1)


def out_project(kit, h, gain):
    nc, dram = kit.nc, kit.dram
    KM = 2 * KD
    with ExitStack() as mem:
        def sb(n, s, d=F32):
            return mem.enter_context(nc.sbuf_tensor(n, s, d))

        m_hi, m_lo = sb("mix_hi", [P, KM, NTOK], F32R), sb("mix_lo", [P, KM, NTOK], F32R)
        eps = sb("mix_eps", [P, 1])
        loaded, hi_made, split = (kit.sems(f"mix_{n}", 2) for n in ("loaded", "hi", "split"))
        squared, summed = kit.sems("mix_squared", 2), kit.sems("mix_summed", 2)
        rooted, inverted = kit.sems("mix_rooted"), kit.sems("mix_inverted")
        reloaded, scaled = kit.sems("mix_reloaded", 2), kit.sems("mix_scaled", 2)
        eps_set, hi2, split2 = kit.sems("mix_eps"), kit.sems("mix_hi2", 2), kit.sems("mix_split2", 2)
        with ExitStack() as tmp:
            sq, raw, rinv = (tmp.enter_context(nc.sbuf_tensor(f"mix_{n}", [P, 2, NTOK], F32))
                             for n in ("sq", "raw", "rinv"))
            acc = [tmp.enter_context(nc.psum_tensor(f"mix_ps{g}", [P, 3 * 512], F32)) for g in range(2)]
            with nc.Block() as block:
                @block.gpsimd
                def _(pool):
                    kit.prime(pool)

                @block.sync
                def _(sp):
                    for k in range(KD):
                        if k >= 2:
                            sp.wait_ge(squared[k % 2], START + k // 2)
                        sp.dma_start(raw[:, k % 2, :], dram["mix"][D + k * P:D + (k + 1) * P, :]).then_inc(loaded[k % 2], 16)
                    for k in range(KM):
                        if k < 2:
                            sp.wait_ge(squared[k % 2], START + KD // 2)
                        else:
                            sp.wait_ge(split[k % 2], START + k // 2)
                        sp.dma_start(raw[:, k % 2, :], dram["mix"][k * P:(k + 1) * P, :]).then_inc(reloaded[k % 2], 16)

                @block.scalar
                def _(act):
                    for k in range(KD):
                        act.wait_ge(loaded[k % 2], START + 16 * (k // 2 + 1))
                        if k >= 2:
                            act.wait_ge(summed[k % 2], START + k // 2)
                        act.activation(sq[:, k % 2, :], raw[:, k % 2, :], ACT.Square).then_inc(squared[k % 2], 1)
                    act.wait_ge(eps_set, START + 1)
                    act.wait_ge(summed[0], START + KD // 2)
                    act.wait_ge(summed[1], START + KD // 2)
                    for g in range(2):
                        last = act.activation(rinv[:, g, :], acc[g][:, 0:NTOK], ACT.Sqrt, bias=eps[:], scale=2.0 / D)
                    last.then_inc(rooted, 1)
                    for k in range(KM):
                        act.wait_ge(reloaded[k % 2], START + 16 * (k // 2 + 1))
                        if k >= KD:
                            act.wait_ge(scaled[k % 2], START + (k - KD) // 2 + 1)
                        act.activation(m_hi[:, k, :], raw[:, k % 2, :], ACT.Copy).then_inc(hi_made[k % 2], 1)

                @block.tensor
                def _(pe):
                    for k in range(KD):
                        g = k // (KD // 2)
                        pe.wait_ge(squared[k % 2], START + k // 2 + 1)
                        for c, w in GROUPS:
                            mm = pe.matmul(acc[g][:, c:c + w], kit.c(C_ONES, P), sq[:, k % 2, c:c + w],
                                           start=(k % (KD // 2) == 0), stop=(k % (KD // 2) == KD // 2 - 1))
                        mm.then_inc(summed[k % 2], 1)

                @block.vector
                def _(dve):
                    dve.memset(eps[:], EPS).then_inc(eps_set, 1)
                    dve.wait_ge(rooted, START + 1)
                    dve.reciprocal(rinv[:], rinv[:]).then_inc(inverted, 1)
                    dve.wait_ge(inverted, START + 1)
                    for k in range(KM):
                        if k >= KD:
                            dve.wait_ge(reloaded[k % 2], START + 16 * (k // 2 + 1))
                            dve.scalar_tensor_tensor(out=raw[:, k % 2, :], in0=raw[:, k % 2, :],
                                                     scalar=gain[:, k - KD:k - KD + 1],
                                                     in1=rinv[:, (k - KD) // (KD // 2), :],
                                                     op0=ALU.mult, op1=ALU.mult).then_inc(scaled[k % 2], 1)
                        dve.wait_ge(hi_made[k % 2], START + k // 2 + 1)
                        dve.tensor_tensor(m_lo[:, k, :], raw[:, k % 2, :], m_hi[:, k, :].bitcast(F32),
                                          ALU.subtract).then_inc(split[k % 2], 1)
                    dve.wait_ge(split[1], START + KM // 2)

        with ExitStack() as tmp:
            w_raw = tmp.enter_context(nc.sbuf_tensor("wo_raw", [P, 2, KM // 2 * P], F32))
            w_hi = tmp.enter_context(nc.sbuf_tensor("wo_hi", [P, 2, KM // 2, P], F32R))
            w_lo = tmp.enter_context(nc.sbuf_tensor("wo_lo", [P, 2, KM // 2, P], F32R))
            acc = [tmp.enter_context(nc.psum_tensor(f"wo_ps{g}", [P, 3 * 512], F32)) for g in range(2)]
            w_loaded, w_hi_made, w_split, w_used = (kit.sems(f"wo_{n}", 2) for n in ("loaded", "hi", "split", "used"))
            made, added, x_loaded = kit.sems("wo_made", 2), kit.sems("wo_added", 2), kit.sems("wo_x")
            with nc.Block() as block:
                @block.sync
                def _(sp):
                    sp.dma_start(h[:], dram["x"].rearrange("(f p) t -> p f t", p=P)).then_inc(x_loaded, 16)
                    with sp.Fori(0, KD) as i:
                        for s in range(2):
                            sp.wait_ge(w_split[s], START + i)
                            sp.dma_start(w_raw[:, s, :], dram["w_out"][bass.ds(i, 1), :, s * D:(s + 1) * D]
                                         .rearrange("o p c -> p (o c)")).then_inc(w_loaded[s], 16)

                @block.gpsimd
                def _(pool):
                    kit.prime(pool)
                    with pool.Fori(0, KD) as i:
                        for s in range(2):
                            pool.wait_ge(w_loaded[s], START + 16 * (i + 1))
                            pool.wait_ge(w_used[s], START + i)
                            raw_w = w_raw[:, s, :].rearrange("p (k m) -> p k m", m=P)
                            kit.settle(pool)
                            pool.tensor_copy(w_hi[:, s], raw_w).then_inc(w_hi_made[s], 1)
                            pool.wait_ge(w_hi_made[s], START + i + 1)
                            pool.tensor_tensor(w_lo[:, s], raw_w, w_hi[:, s].bitcast(F32), ALU.subtract).then_inc(w_split[s], 1)

                @block.tensor
                def _(pe):
                    with pe.Fori(0, KD // 2) as i:
                        for j in range(2):
                            pe.wait_ge(added[j], START + i)
                            for s in range(2):
                                pe.wait_ge(w_split[s], START + 2 * i + j + 1)
                                for kk in range(KM // 2):
                                    k = s * (KM // 2) + kk
                                    for wt, xt in ((w_hi, m_hi), (w_hi, m_lo), (w_lo, m_hi)):
                                        for c, w in GROUPS:
                                            mm = pe.matmul(acc[j][:, c:c + w], wt[:, s, kk, :], xt[:, k, c:c + w],
                                                           start=(k == 0 and wt is w_hi and xt is m_hi),
                                                           stop=(k == KM - 1 and wt is w_lo))
                                if s == 0:
                                    mm.then_inc(w_used[0], 1)
                            mm.then_inc(made[j], 1)

                @block.vector
                def _(dve):
                    dve.wait_ge(x_loaded, START + 16)
                    with dve.Fori(0, KD // 2) as i:
                        for j in range(2):
                            row = h[:, bass.ds(2 * i + j, 1), :].rearrange("p o t -> p (o t)")
                            dve.wait_ge(made[j], START + i + 1)
                            dve.sem_inc(w_used[1], 1)
                            dve.tensor_tensor(row, row, acc[j][:, 0:NTOK], ALU.add).then_inc(added[j], 1)
                    for j in range(2):
                        dve.wait_ge(added[j], START + KD // 2)


def feed_forward(kit, h, x_hi, x_lo):
    nc, dram = kit.nc, kit.dram
    with ExitStack() as mem:
        def sb(n, s, d=F32):
            return mem.enter_context(nc.sbuf_tensor(n, s, d))

        w_raw, w_hi, w_lo = sb("wf_raw", [P, 2, D]), sb("wf_hi", [P, 2, KD, P], F32R), sb("wf_lo", [P, 2, KD, P], F32R)
        r_hi, r_lo = sb("r_hi", [P, FT, NTOK], F32R), sb("r_lo", [P, FT, NTOK], F32R)
        relu, r_sq = sb("relu", [P, 2, NTOK]), sb("r_sq", [P, 2, NTOK])
        acc = [mem.enter_context(nc.psum_tensor(f"ff_ps{j}", [P, 3 * 512], F32)) for j in range(2)]
        w_loaded, w_hi_made, w_split = (kit.sems(f"wf_{n}", 2) for n in ("loaded", "hi", "split"))
        w_used = kit.sems("wf_used", 2)
        up_made, relued, squared, hi_made, split = (kit.sems(f"ff_{n}", 2) for n in ("up", "relu", "sq", "hi", "split"))
        down_made, added = kit.sems("ff_down", 2), kit.sems("ff_added", 2)
        stored = kit.sems("ff_stored")
        UN = 2 * FT // 2

        with nc.Block() as block:
            @block.sync
            def _(sp):
                with sp.Fori(0, NFC) as i:
                    for n in range(2 * FT):
                        j = n % 2
                        sp.wait_ge(w_split[j], START + UN * i + n // 2)
                        src = dram["w_up"] if n < FT else dram["w_down"]
                        sp.dma_start(w_raw[:, j, :], src[bass.ds(FT * i + n % FT, 1)]
                                     .rearrange("o p c -> p (o c)")).then_inc(w_loaded[j], 16)

            @block.gpsimd
            def _(pool):
                kit.prime(pool)
                with pool.Fori(0, NFC) as i:
                    for n in range(2 * FT):
                        j = n % 2
                        pool.wait_ge(w_loaded[j], START + (UN * i + n // 2 + 1) * 16)
                        pool.wait_ge(w_used[j], START + UN * i + n // 2)
                        raw_w = w_raw[:, j, :].rearrange("p (k m) -> p k m", m=P)
                        kit.settle(pool)
                        pool.tensor_copy(w_hi[:, j], raw_w).then_inc(w_hi_made[j], 1)
                        pool.wait_ge(w_hi_made[j], START + UN * i + n // 2 + 1)
                        pool.tensor_tensor(w_lo[:, j], raw_w, w_hi[:, j].bitcast(F32),
                                           ALU.subtract).then_inc(w_split[j], 1)

            @block.tensor
            def _(pe):
                with pe.Fori(0, NFC) as i:
                    for f in range(FT):
                        j = f % 2
                        pe.wait_ge(w_split[j], START + UN * i + f // 2 + 1)
                        if f < 2:
                            pe.wait_ge(added[j], START + KD // 2 * i)
                        else:
                            pe.wait_ge(squared[j], START + FT // 2 * i + f // 2)
                        for k in range(KD):
                            for wt, xt in ((w_hi, x_hi), (w_hi, x_lo), (w_lo, x_hi)):
                                for c, w in GROUPS:
                                    mm = pe.matmul(acc[j][:, c:c + w], wt[:, j, k, :], xt[:, k, c:c + w],
                                                   start=(k == 0 and wt is w_hi and xt is x_hi),
                                                   stop=(k == KD - 1 and wt is w_lo))
                        mm.then_inc(up_made[j], 1)
                    for o in range(KD):
                        j, n = o % 2, FT + o // 2
                        s = n % 2
                        if o % 2 == 0:
                            pe.wait_ge(w_split[s], START + UN * i + n // 2 + 1)
                        if o < 2:
                            pe.wait_ge(squared[j], START + FT // 2 * (i + 1))
                        else:
                            pe.wait_ge(added[j], START + KD // 2 * i + o // 2)
                        for k in range(FT):
                            if o == 0:
                                pe.wait_ge(split[k % 2], START + FT // 2 * i + k // 2 + 1)
                            for wt, xt in ((w_hi, r_hi), (w_hi, r_lo), (w_lo, r_hi)):
                                for c, w in GROUPS:
                                    mm = pe.matmul(acc[j][:, c:c + w], wt[:, s, (o % 2) * FT + k, :], xt[:, k, c:c + w],
                                                   start=(k == 0 and wt is w_hi and xt is r_hi),
                                                   stop=(k == FT - 1 and wt is w_lo))
                        mm.then_inc(down_made[j], 1)

            @block.scalar
            def _(act):
                with act.Fori(0, NFC) as i:
                    for f in range(FT):
                        j = f % 2
                        u = FT // 2 * i + f // 2
                        act.wait_ge(up_made[j], START + u + 1)
                        act.wait_ge(squared[j], START + u)
                        act.activation(relu[:, j, :], acc[j][:, 0:NTOK], ACT.Relu).then_inc(relued[j], 1)
                        act.wait_ge(squared[j], START + u + 1)
                        act.wait_ge(down_made[0], START + KD // 2 * i)
                        act.wait_ge(down_made[1], START + KD // 2 * i)
                        act.activation(r_hi[:, f, :], r_sq[:, j, :], ACT.Copy).then_inc(hi_made[j], 1)
                        act.sem_inc(w_used[j], 1)
                    for o in range(KD):
                        j = o % 2
                        act.wait_ge(down_made[j], START + KD // 2 * i + o // 2 + 1)
                        if o % 2 == 1:
                            act.sem_inc(w_used[(o // 2) % 2], 1)

            @block.vector
            def _(dve):
                with dve.Fori(0, NFC) as i:
                    for f in range(FT):
                        j = f % 2
                        u = FT // 2 * i + f // 2
                        dve.wait_ge(relued[j], START + u + 1)
                        dve.wait_ge(split[j], START + u)
                        dve.tensor_tensor(r_sq[:, j, :], relu[:, j, :], relu[:, j, :], ALU.mult).then_inc(squared[j], 1)
                        dve.wait_ge(hi_made[j], START + u + 1)
                        dve.tensor_tensor(r_lo[:, f, :], r_sq[:, j, :], r_hi[:, f, :].bitcast(F32),
                                          ALU.subtract).then_inc(split[j], 1)
                    for o in range(KD):
                        j = o % 2
                        dve.wait_ge(down_made[j], START + KD // 2 * i + o // 2 + 1)
                        if o >= 2:
                            dve.wait_ge(added[j], START + KD // 2 * i + o // 2)
                        dve.tensor_tensor(h[:, o, :], h[:, o, :], acc[j][:, 0:NTOK], ALU.add).then_inc(added[j], 1)
                for j in range(2):
                    dve.wait_ge(added[j], START + KD // 2 * NFC)

        with nc.Block() as block:
            @block.gpsimd
            def _(pool):
                kit.prime(pool)

            @block.sync
            def _(sp):
                sp.dma_start(dram["y"].rearrange("(f p) t -> p f t", p=P), h[:]).then_inc(stored, 16)
                sp.wait_ge(stored, START + 16)


def prepare_parameters(kit, small, neg_a):
    nc, dram = kit.nc, kit.dram
    loaded, made = kit.sems("param_loaded"), kit.sems("param_made")
    with nc.Block() as block:
        @block.gpsimd
        def _(pool):
            kit.prime(pool)

        @block.sync
        def _(sp):
            sp.dma_start(small[:], dram["params"]).then_inc(loaded, 16)
            sp.dma_start(neg_a[:], dram["a_log"].partition_broadcast(P)).then_inc(loaded, 16)

        @block.scalar
        def _(act):
            act.wait_ge(loaded, START + 32)
            act.activation(neg_a[:], neg_a[:], ACT.Exp).then_inc(made, 1)

        @block.vector
        def _(dve):
            dve.wait_ge(made, START + 1)
            dve.tensor_scalar(neg_a[:], neg_a[:], -1.0, None, ALU.mult).then_inc(made, 1)
            dve.tensor_scalar(small[:, PAR_Q:PAR_Q + KD], small[:, PAR_Q:PAR_Q + KD], HD ** -0.5, None,
                              ALU.mult).then_inc(made, 1)
            dve.wait_ge(made, START + 3)


PAR_MIX, PAR_Q, PAR_K, PAR_FFN, PAR_SSM, PAR_SKIP = (KD * n for n in range(6))
PAR_END = 6 * KD


def build(nc, dram):
    with ExitStack() as stack:
        kit = Kit(nc, stack, dram)
        small = stack.enter_context(nc.sbuf_tensor("params", [P, PAR_END], F32))
        neg_a = stack.enter_context(nc.sbuf_tensor("neg_a", [P, NH], F32))
        skip = small[:, PAR_SKIP:PAR_SKIP + KD]
        with kit.part(), ExitStack() as mem:
            load_constants(kit)
            prepare_parameters(kit, small, neg_a)
            distance_table(kit)
            x_hi = mem.enter_context(nc.sbuf_tensor("u_hi", [P, KD, NPAD], F32R))
            x_lo = mem.enter_context(nc.sbuf_tensor("u_lo", [P, KD, NPAD], F32R))
            with ExitStack() as tmp:
                x = tmp.enter_context(nc.sbuf_tensor("x", [P, KD, NTOK], F32))
                loads = [[(x[:, k, :], dram["x"][k * P:(k + 1) * P, :])] for k in range(KD)]
                rms_split(kit, "mixnorm", x, loads, small[:, PAR_MIX:PAR_MIX + KD], x_hi, x_lo)
            project(kit, x_hi, x_lo, small[:, PAR_Q:PAR_Q + QK_TILES])
            project_tokens(kit, x_hi, x_lo)
        with kit.part():
            attend_prompt(kit)
            attend_sample(kit)
        with kit.part():
            scan_prompt(kit, neg_a, skip)
            scan_sample(kit, neg_a, skip)
        with kit.part(), ExitStack() as mem:
            h = mem.enter_context(nc.sbuf_tensor("h", [P, KD, NTOK], F32))
            out_project(kit, h, small[:, PAR_SSM:PAR_SSM + KD])
            x_hi = mem.enter_context(nc.sbuf_tensor("uf_hi", [P, KD, NTOK], F32R))
            x_lo = mem.enter_context(nc.sbuf_tensor("uf_lo", [P, KD, NTOK], F32R))
            rms_split(kit, "ffnnorm", h, [], small[:, PAR_FFN:PAR_FFN + KD], x_hi, x_lo)
            feed_forward(kit, h, x_hi, x_lo)


def tiles(w, rows_of_tile, cols_of_tile):
    k, n = w.shape
    t = w.reshape(k // rows_of_tile, rows_of_tile, n // cols_of_tile, cols_of_tile)
    return np.ascontiguousarray(t.transpose(2, 1, 0, 3)).reshape(n // cols_of_tile, rows_of_tile, -1)


def by_tile(v):
    return v.reshape(-1, P).T


def lay_out(a):
    f = {k: np.asarray(v) for k, v in a.items()}
    w_in = f["w_in"][0]
    q, k, v, z, xbc, dt = np.split(w_in, [D, 2 * D, 3 * D, 4 * D, 4 * D + XBC], axis=1)
    w_tok = np.concatenate([v, dt], axis=1).reshape(KD, P, D + NH)
    w_down = f["w_down"][0].reshape(NFC, FT, P, KD // 2, 2, P)
    def reach(cache):
        c = cache[0].reshape(NB_DEC, PAST, D)
        far = c.reshape(NB_DEC, PAST // 16, 16, D)[:, :FAR // 4, :4].reshape(NB_DEC, FAR, D)
        return np.concatenate([far, c[:, PAST - DENSE:]], axis=1)
    ck, cv = reach(f["cache_attn_k"]), reach(f["cache_attn_v"])
    taps = np.concatenate([f["conv_w"][0], f["conv_b"]], axis=0)
    params = np.concatenate([by_tile(f["norm_mix"][0]),
                             by_tile(np.tile(f["q_norm"][0], NH)), by_tile(np.tile(f["k_norm"][0], NH)),
                             by_tile(f["norm_ffn"][0]), by_tile(f["ssm_norm"][0]),
                             by_tile(np.repeat(f["d_skip"][0], HD))], axis=1)
    x = np.concatenate([f["x_prompt"][0], f["x_sample"].reshape(NS, D)], axis=0)
    out = {
        "x": x.T,
        "w_feat": tiles(np.concatenate([q, k, xbc, z], axis=1), P, P),
        "w_tok": w_tok,
        "conv_taps": taps.reshape(WIDTH + 1, XBC_TILES, P).transpose(2, 1, 0),
        "conv_past": f["state_conv"][0].reshape(NB_DEC * (WIDTH - 1), XBC_TILES, P).transpose(2, 1, 0),
        "dt_bias": f["dt_bias"].reshape(NH), "a_log": f["a_log"].reshape(NH), "rel_bias": f["rel_bias"],
        "params": params,
        "cache_k": ck.reshape(NB_DEC, FAR + DENSE, NPAIR, P).transpose(0, 3, 2, 1).reshape(NB_DEC, P, -1),
        "cache_v": cv.reshape(NB_DEC, VT, P, D).transpose(0, 2, 1, 3).reshape(NB_DEC, P, -1),
        "state_in": f["state_ssm"][0].reshape(NB_DEC, D, NSTATE).transpose(0, 2, 1),
        "w_out": tiles(f["w_out"][0], P, P),
        "w_up": tiles(f["w_up"][0], P, P),
        "w_down": w_down.transpose(0, 3, 2, 4, 1, 5).reshape(NFC * KD // 2, P, 2 * FT * P),
        "consts": shape_constants(), "onehot": distance_constants(),
    }
    return {n: np.ascontiguousarray(v) for n, v in out.items()}


_OUTS = {"y": (D, NTOK), "qk": (2 * D, NTOK), "v": (NPAD, D), "conv_tail": (P, XBC_TILES * 27),
         "ssm_p": (NSTATE, D), "ssm_s": (NB_DEC, NSTATE, D)}
_SCRATCH = {"xbc": (XBC, NTOK), "z": (D, NTOK), "dt": (NPAD, NH), "mix": (2 * D, NTOK), "table": (NH, LLEN), "bias_rows": (NH * P, SEQ),
            "bias_sample": (NH * T_DEC, NKEY)}


def kernel(**inputs):
    import concourse.bacc as bacc
    from concourse.bass_utils import run_bass_kernel_spmd

    nc = bacc.Bacc("TRN2", target_bir_lowering=False, num_devices=1)
    arrays, dram = {}, {}
    for name, a in lay_out(inputs).items():
        arrays[f"in_{name}"] = a
        dram[name] = nc.dram_tensor(f"in_{name}", a.shape, F32, kind="ExternalInput").ap()
    for name, shape in _OUTS.items():
        dram[name] = nc.dram_tensor(f"out_{name}", shape, F32, kind="ExternalOutput").ap()
    for name, shape in _SCRATCH.items():
        dram[name] = nc.dram_tensor(f"tmp_{name}", shape, F32).ap()
    build(nc, dram)
    r = run_bass_kernel_spmd(nc, [arrays], core_ids=[0]).results[0]
    y, qk, v, tail = r["out_y"], r["out_qk"], r["out_v"], r["out_conv_tail"]
    k = np.ascontiguousarray(qk[D:].T)
    conv = tail.reshape(P, XBC_TILES, (NB_DEC + 1) * (WIDTH - 1)).transpose(2, 1, 0).reshape(NB_DEC + 1, WIDTH - 1, XBC)
    outs = (
        y[:, :SEQ].T.reshape(1, SEQ, D),
        y[:, SEQ:].T.reshape(NB_DEC, T_DEC, D),
        k[:SEQ].reshape(1, 1, SEQ, NH, HD),
        v[:SEQ].reshape(1, 1, SEQ, NH, HD),
        conv[0].reshape(1, 1, WIDTH - 1, XBC),
        r["out_ssm_p"].T.reshape(1, 1, NH, HD, NSTATE),
        k[SEQ:].reshape(1, NB_DEC, T_DEC, NH, HD),
        v[SEQ:NTOK].reshape(1, NB_DEC, T_DEC, NH, HD),
        conv[1:].reshape(1, NB_DEC, WIDTH - 1, XBC),
        r["out_ssm_s"].transpose(0, 2, 1).reshape(1, NB_DEC, NH, HD, NSTATE),
    )
    return tuple(np.ascontiguousarray(o) for o in outs)
```

```python
import math
from contextlib import ExitStack, contextmanager

import numpy as np
import concourse.bass as bass
from concourse import mybir
from concourse.alu_op_type import AluOpType as ALU

ACT = mybir.ActivationFunctionType
F32 = mybir.dt.float32
F32R = mybir.dt.float32r
AX = mybir.AxisListType.X

P = 128
D = 1024
KD = D // P
SEQ = 1024
NT = SEQ // P
NB_DEC, T_DEC = 8, 4
NS = NB_DEC * T_DEC
NTOK = SEQ + NS
NPAD = SEQ + P
PAST = 1024
HD = 64
NH = D // HD
NPAIR = NH // 2
XBC = 1536
NSTATE = 128
WIDTH = 4
DFF = 4 * D
EPS = 1e-6
QK_TILES, XBC_TILES, Z_TILES = 2 * KD, XBC // P, KD
START = 1
NEG = -1e30
BRANCHES = ((128, 1), (512, 4), (2048, 16))
NBUCKET = 32
LMAX = PAST + T_DEC - 1
LLEN = LMAX + P
FAR = P
DENSE = 512
NKEY = FAR + DENSE + T_DEC
VT = (FAR + DENSE) // P
NG = 3
TG = NTOK // NG
GROUPS = tuple((g * TG, TG) for g in range(NG))
FC = 512
FT = FC // P
NFC = DFF // FC

C_IDENT, C_UPPER, C_LOWER, C_ONES, C_HEADONE = 0, P, 2 * P, 3 * P, 4 * P
C_UPPER_S, C_LOWER_S = 5 * P, 5 * P + NS
C_BMASK = C_LOWER_S + NS
C_BROW = C_BMASK + NB_DEC * NS
C_DIAG = C_BROW + NB_DEC
C_SEL = C_DIAG + D
C_END = C_SEL + T_DEC


def shape_constants():
    c = np.zeros((P, C_END), np.float32)
    r = np.arange(P)
    c[:, C_IDENT:C_IDENT + P] = np.eye(P)
    c[:, C_UPPER:C_UPPER + P] = r[:, None] <= r[None, :]
    c[:, C_LOWER:C_LOWER + P] = r[:, None] > r[None, :]
    c[:, C_ONES:C_ONES + P] = 1.0
    c[:, C_HEADONE:C_HEADONE + P] = r[:, None] // HD == r[None, :] // HD
    s = np.arange(NS)
    same = s[:, None] // T_DEC == s[None, :] // T_DEC
    c[:NS, C_UPPER_S:C_UPPER_S + NS] = same & (s[:, None] <= s[None, :])
    c[:NS, C_LOWER_S:C_LOWER_S + NS] = same & (s[:, None] > s[None, :])
    for b in range(NB_DEC):
        c[:, C_BMASK + b * NS:C_BMASK + (b + 1) * NS] = (s // T_DEC == b)[None, :]
        c[:NS, C_BROW + b] = s // T_DEC == b
    ht = np.arange(NH * T_DEC)
    c[:len(ht), C_DIAG:C_DIAG + D] = ht[:, None] // T_DEC == np.arange(D)[None, :] // HD
    c[:len(ht), C_SEL:C_SEL + T_DEC] = ht[:, None] % T_DEC == np.arange(T_DEC)[None, :]
    return c


def distance_constants():
    dist = LMAX - np.arange(LLEN)
    exact = NBUCKET // 2
    df = np.maximum(dist, 1).astype(np.float32)
    top = max(w for w, _ in BRANCHES)
    large = exact + (np.log(df / np.float32(exact)) / np.float32(math.log(top / exact))
                     * np.float32(NBUCKET - exact)).astype(np.int32)
    bucket = np.where(dist < exact, np.maximum(dist, 0), np.minimum(large, NBUCKET - 1))
    out = np.zeros((NBUCKET + 1, LLEN), np.float32)
    out[bucket, np.arange(LLEN)] = 1.0
    count = sum(((dist >= 0) & (dist <= w) & (dist % d == 0)).astype(np.int32) for w, d in BRANCHES)
    out[NBUCKET] = np.where(count > 0, np.log(np.maximum(count, 1)), NEG)
    return out


class Kit:

    def __init__(self, nc, stack, dram):
        self.nc, self.stack = nc, stack
        self.dram = dram
        self.const = stack.enter_context(nc.sbuf_tensor("const", [P, C_END], F32))
        self.part_stack, self.unprimed = None, []
        self.const_loaded = self.sems("const_loaded")
        self.skewed = self.sems("bias_skewed")

    def sems(self, name, n=1):
        made = [(self.part_stack or self.stack).enter_context(self.nc.semaphore(f"{name}{i}")) for i in range(n)]
        if self.part_stack:
            self.part_sems += made
            self.unprimed += made
        return made if n > 1 else made[0]

    @contextmanager
    def part(self):
        with ExitStack() as self.part_stack:
            self.part_sems = []
            names = ("tensor", "vector", "gpsimd")
            engines = (self.nc.tensor, self.nc.vector, self.nc.gpsimd)
            self.settled = {e.engine: self.sems(f"settled_{n}") for n, e in zip(names, engines)}
            yield
            used = self.part_sems
            with self.nc.Block() as block:
                @block.gpsimd
                def _(pool):
                    for sem in used:
                        pool.sem_clear(sem)
        self.part_stack, self.unprimed = None, []

    def prime(self, pool):
        for sem in self.unprimed:
            pool.sem_inc(sem, START)
        self.unprimed = []

    def settle(self, eng):
        eng.sem_inc(self.settled[eng.engine], 1)

    def c(self, start, width, rows=P):
        return self.const[0:rows, start:start + width]


def bank(acc, c, w):
    return acc[:, c // TG * 512:c // TG * 512 + w]


def in_banks(acc):
    return acc[:].rearrange("p (g c) -> p g c", g=NG)[:, :, 0:TG]


def grouped(ap):
    return ap.rearrange("p (g c) -> p g c", g=NG)


def load_constants(kit):
    nc = kit.nc
    with nc.Block() as block:
        @block.gpsimd
        def _(pool):
            kit.prime(pool)

        @block.sync
        def _(sp):
            sp.dma_start(kit.const[:], kit.dram["consts"]).then_inc(kit.const_loaded, 16)
            sp.wait_ge(kit.const_loaded, 16)


def distance_table(kit):
    nc, dram = kit.nc, kit.dram
    with ExitStack() as mem:
        onehot = mem.enter_context(nc.sbuf_tensor("onehot", [NBUCKET + 1, LLEN], F32))
        bias = mem.enter_context(nc.sbuf_tensor("bias_aug", [NBUCKET + 1, NH], F32))
        table = mem.enter_context(nc.sbuf_tensor("table", [NH, LLEN], F32))
        acc = mem.enter_context(nc.psum_tensor("table_ps", [P, 3 * 512], F32))
        loaded, made, copied, stored = (kit.sems(f"dist_{n}") for n in ("loaded", "made", "copied", "stored"))
        ones_set = kit.sems("dist_ones")
        with nc.Block() as block:
            @block.gpsimd
            def _(pool):
                kit.prime(pool)

            @block.sync
            def _(sp):
                sp.dma_start(onehot[:], dram["onehot"]).then_inc(loaded, 16)
                sp.dma_start(bias[0:NBUCKET, :], dram["rel_bias"]).then_inc(loaded, 16)
                sp.wait_ge(copied, START + 1)
                sp.dma_start(dram["table"], table[:]).then_inc(stored, 16)
                sp.wait_ge(stored, START + 16)
                table_of, rows = dram["table"].tensor, dram["bias_rows"].rearrange("(h p) c -> h p c", h=NH)
                sp.dma_start(rows, bass.AP(table_of, LMAX - (NT - 1) * P, [[LLEN, NH], [-1, P], [1, SEQ]])
                             ).then_inc(kit.skewed, 16)
                rows = dram["bias_sample"].rearrange("(h t) c -> h t c", h=NH)
                for t in range(T_DEC):
                    sp.dma_start(rows[:, t, 0:FAR].rearrange("h (g r) -> h g r", r=4),
                                 bass.AP(table_of, LMAX - PAST - t, [[LLEN, NH], [16, FAR // 4], [1, 4]])
                                 ).then_inc(kit.skewed, 16)
                    sp.dma_start(rows[:, t, FAR:NKEY],
                                 bass.AP(table_of, LMAX - DENSE - t, [[LLEN, NH], [1, DENSE + T_DEC]])
                                 ).then_inc(kit.skewed, 16)

            @block.vector
            def _(dve):
                dve.memset(bias[NBUCKET:NBUCKET + 1, :], 1.0).then_inc(ones_set, 1)

            @block.tensor
            def _(pe):
                pe.wait_ge(loaded, START + 32)
                pe.wait_ge(ones_set, START + 1)
                for c in range(0, LLEN, 512):
                    w = min(512, LLEN - c)
                    mm = pe.matmul(acc[0:NH, c:c + w], bias[:], onehot[:, c:c + w], start=True, stop=True)
                mm.then_inc(made, 1)

            @block.scalar
            def _(act):
                act.wait_ge(made, START + 1)
                act.activation(table[:], acc[0:NH, 0:LLEN], ACT.Copy).then_inc(copied, 1)


def rms_split(kit, name, x, loads, gain, x_hi, x_lo):
    nc = kit.nc
    with ExitStack() as mem:
        sq = mem.enter_context(nc.sbuf_tensor(f"{name}_sq", [P, 2, NTOK], F32))
        rinv = mem.enter_context(nc.sbuf_tensor(f"{name}_rinv", [P, NTOK], F32))
        u = mem.enter_context(nc.sbuf_tensor(f"{name}_u", [P, 2, NTOK], F32))
        eps = mem.enter_context(nc.sbuf_tensor(f"{name}_eps", [P, 1], F32))
        acc = mem.enter_context(nc.psum_tensor(f"{name}_ps", [P, 3 * 512], F32))
        loaded = kit.sems(f"{name}_loaded", KD)
        squared, summed = kit.sems(f"{name}_squared", 2), kit.sems(f"{name}_summed", 2)
        rooted, inverted = kit.sems(f"{name}_rooted"), kit.sems(f"{name}_inverted")
        scaled, hi_made, lo_made = (kit.sems(f"{name}_{n}", 2) for n in ("scaled", "hi", "lo"))
        eps_set = kit.sems(f"{name}_eps")
        with nc.Block() as block:
            @block.gpsimd
            def _(pool):
                kit.prime(pool)

            @block.sync
            def _(sp):
                for k, pairs in enumerate(loads):
                    for dst, src in pairs:
                        sp.dma_start(dst, src).then_inc(loaded[k], 16)

            @block.scalar
            def _(act):
                for k in range(KD):
                    if loads:
                        act.wait_ge(loaded[k], START + 16 * len(loads[k]))
                    if k >= 2:
                        act.wait_ge(summed[k % 2], START + k // 2)
                    act.activation(sq[:, k % 2, :], x[:, k, :], ACT.Square).then_inc(squared[k % 2], 1)
                act.wait_ge(summed[(KD - 1) % 2], START + KD // 2)
                act.wait_ge(eps_set, START + 1)
                act.activation(grouped(rinv[:]), in_banks(acc), ACT.Sqrt, bias=eps[:], scale=1.0 / D).then_inc(rooted, 1)
                for k in range(KD):
                    act.wait_ge(scaled[k % 2], START + k // 2 + 1)
                    act.activation(x_hi[:, k, 0:NTOK], u[:, k % 2, :], ACT.Copy).then_inc(hi_made[k % 2], 1)

            @block.tensor
            def _(pe):
                for k in range(KD):
                    pe.wait_ge(squared[k % 2], START + k // 2 + 1)
                    for c, w in GROUPS:
                        mm = pe.matmul(bank(acc, c, w), kit.c(C_ONES, P), sq[:, k % 2, c:c + w],
                                       start=(k == 0), stop=(k == KD - 1))
                    mm.then_inc(summed[k % 2], 1)

            @block.vector
            def _(dve):
                dve.memset(eps[:], EPS).then_inc(eps_set, 1)
                dve.wait_ge(rooted, START + 1)
                dve.reciprocal(rinv[:], rinv[:]).then_inc(inverted, 1)
                dve.wait_ge(inverted, START + 1)
                for k in range(KD):
                    if k >= 2:
                        dve.wait_ge(lo_made[k % 2], START + k // 2)
                    dve.scalar_tensor_tensor(out=u[:, k % 2, :], in0=x[:, k, :], scalar=gain[:, k:k + 1],
                                             in1=rinv[:], op0=ALU.mult, op1=ALU.mult).then_inc(scaled[k % 2], 1)
                    dve.wait_ge(hi_made[k % 2], START + k // 2 + 1)
                    dve.tensor_tensor(x_lo[:, k, 0:NTOK], u[:, k % 2, :], x_hi[:, k, 0:NTOK].bitcast(F32),
                                      ALU.subtract).then_inc(lo_made[k % 2], 1)
                dve.wait_ge(lo_made[(KD - 1) % 2], START + KD // 2)


def project(kit, x_hi, x_lo, gains):
    nc, dram = kit.nc, kit.dram
    NQ, NX, NZ = QK_TILES, XBC_TILES, Z_TILES
    with ExitStack() as mem:
        def sb(n, s, d=F32):
            return mem.enter_context(nc.sbuf_tensor(n, s, d))

        w_raw, w_hi, w_lo = sb("w_raw", [P, 2, D]), sb("w_hi", [P, 2, KD, P], F32R), sb("w_lo", [P, 2, KD, P], F32R)
        out = sb("proj_out", [P, 2, NTOK])
        raw, sq, rinv = sb("proj_raw", [P, 2, NTOK]), sb("proj_sq", [P, 2, NTOK]), sb("proj_rinv", [P, 2, NTOK])
        pre = sb("conv_pre", [P, 2, WIDTH - 1 + SEQ])
        pre_s = sb("conv_pre_s", [P, 2, NB_DEC, WIDTH - 1 + T_DEC])
        past_s = sb("conv_past", [P, XBC_TILES, NB_DEC * (WIDTH - 1)])
        taps = sb("conv_taps", [P, XBC_TILES, WIDTH + 1])
        tap = sb("conv_tap", [P, 2, WIDTH + 1])
        tail = sb("conv_tail", [P, XBC_TILES, (NB_DEC + 1) * (WIDTH - 1)])
        gain = sb("qk_gain", [P, 2, 1])
        eps = sb("qk_eps", [P, 1])
        acc = [mem.enter_context(nc.psum_tensor(f"proj_ps{j}", [P, 3 * 512], F32)) for j in range(2)]
        ssq = [mem.enter_context(nc.psum_tensor(f"proj_ss{j}", [P, 512], F32)) for j in range(2)]

        w_loaded, w_hi_made, w_split = (kit.sems(f"w_{n}", 2) for n in ("loaded", "hi", "split"))
        made, freed = kit.sems("proj_made", 2), kit.sems("proj_freed", 2)
        squared = kit.sems("qk_squared", 2)
        summed, rooted = kit.sems("qk_summed", 2), kit.sems("qk_rooted", 2)
        inverted, normed = kit.sems("qk_inverted", 2), kit.sems("qk_normed", 2)
        gained = kit.sems("qk_gained", 2)
        stored = kit.sems("proj_stored", 2)
        small = kit.sems("proj_small")
        zeroed = kit.sems("proj_zeroed")
        tapped, padded, conv, activated = (kit.sems(f"conv_{n}", 2) for n in ("tapped", "padded", "mac", "silu"))
        tails, tail_stored = kit.sems("conv_tails", 2), kit.sems("tail_stored")
        z_silu = kit.sems("z_silu", 2)

        def tile_range(kind):
            return {"qk": (0, NQ // 2), "xbc": (NQ // 2, NX // 2), "z": ((NQ + NX) // 2, NZ // 2)}[kind]

        with nc.Block() as block:
            @block.sync
            def _(sp):
                sp.dma_start(taps[:], dram["conv_taps"]).then_inc(small, 16)
                sp.dma_start(past_s[:], dram["conv_past"]).then_inc(small, 16)
                with sp.Fori(0, (NQ + NX + NZ) // 2) as i:
                    for j in range(2):
                        sp.wait_ge(w_split[j], START + i)
                        sp.dma_start(w_raw[:, j, :], dram["w_feat"][bass.ds(2 * i + j, 1)]
                                     .rearrange("o p c -> p (o c)")).then_inc(w_loaded[j], 16)

            @block.gpsimd
            def _(pool):
                kit.prime(pool)
                with pool.Fori(0, (NQ + NX + NZ) // 2) as i:
                    for j in range(2):
                        pool.wait_ge(w_loaded[j], START + 16 * (i + 1))
                        pool.wait_ge(made[j], START + i)
                        raw_w = w_raw[:, j, :].rearrange("p (k m) -> p k m", k=KD)
                        kit.settle(pool)
                        pool.tensor_copy(w_hi[:, j], raw_w).then_inc(w_hi_made[j], 1)
                        pool.wait_ge(w_hi_made[j], START + i + 1)
                        pool.tensor_tensor(w_lo[:, j], raw_w, w_hi[:, j].bitcast(F32),
                                           ALU.subtract).then_inc(w_split[j], 1)

            @block.tensor
            def _(pe):
                def main(n, j):
                    pe.wait_ge(w_split[j], START + n + 1)
                    pe.wait_ge(freed[j], START + n)
                    for k in range(KD):
                        for wt, xt in ((w_hi, x_hi), (w_hi, x_lo), (w_lo, x_hi)):
                            for c, w in GROUPS:
                                first = k == 0 and wt is w_hi and xt is x_hi
                                last = k == KD - 1 and wt is w_lo
                                mm = pe.matmul(bank(acc[j], c, w), wt[:, j, k, :], xt[:, k, c:c + w],
                                               start=first, stop=last)
                    mm.then_inc(made[j], 1)

                def head_sums(n, j):
                    pe.wait_ge(squared[j], START + n + 1)
                    for g, (c, w) in enumerate(GROUPS):
                        s = g % 2
                        if s == 0:
                            pe.wait_ge(rooted[0], START + 2 * (2 * n + j) + g // 2)
                        else:
                            pe.wait_ge(rooted[1], START + 2 * n + j)
                        pe.matmul(ssq[s][:, 0:w], kit.c(C_HEADONE, P), sq[:, j, c:c + w],
                                  start=True, stop=True).then_inc(summed[s], 1)

                main(0, 0)
                with pe.Fori(0, NQ // 2 - 1) as i:
                    main(i, 1)
                    head_sums(i, 0)
                    main(i + 1, 0)
                    head_sums(i, 1)
                main(NQ // 2 - 1, 1)
                head_sums(NQ // 2 - 1, 0)
                head_sums(NQ // 2 - 1, 1)
                with pe.Fori(NQ // 2, (NQ + NX + NZ) // 2) as i:
                    main(i, 0)
                    main(i, 1)

            @block.scalar
            def _(act):
                act.wait_ge(zeroed, START + 4)
                with act.Fori(0, NQ // 2) as i:
                    for j in range(2):
                        act.wait_ge(made[j], START + i + 1)
                        act.wait_ge(normed[j], START + i)
                        act.activation(grouped(raw[:, j, :]), in_banks(acc[j]), ACT.Copy)
                        act.activation(grouped(sq[:, j, :]), in_banks(acc[j]), ACT.Square).then_inc(squared[j], 1)
                        act.wait_ge(squared[j], START + i + 1)
                        act.sem_inc(freed[j], 1)
                        for g, (c, w) in enumerate(GROUPS):
                            s = g % 2
                            n = 2 * (2 * i + j) + g // 2 if s == 0 else 2 * i + j
                            act.wait_ge(summed[s], START + n + 1)
                            act.activation(rinv[:, j, c:c + w], ssq[s][:, 0:w], ACT.Sqrt, bias=eps[:],
                                           scale=1.0 / HD).then_inc(rooted[s], 1)
                        act.wait_ge(normed[j], START + i + 1)
                        act.dma_start(dram["qk"][bass.ds((2 * i + j) * P, P), :], out[:, j, :]).then_inc(stored[j], 16)

                base, pairs = tile_range("xbc")
                with act.Fori(0, pairs) as i:
                    for j in range(2):
                        act.wait_ge(made[j], START + i + base + 1)
                        act.wait_ge(conv[j], START + i * WIDTH)
                        act.wait_ge(tails[j], START + i)
                        full = SEQ // TG
                        act.activation(pre[:, j, WIDTH - 1:WIDTH - 1 + full * TG].rearrange("p (g c) -> p g c", g=full),
                                       in_banks(acc[j])[:, 0:full, :], ACT.Copy)
                        act.activation(pre[:, j, WIDTH - 1 + full * TG:], in_banks(acc[j])[:, full, 0:SEQ - full * TG],
                                       ACT.Copy)
                        act.activation(pre_s[:, j, :, WIDTH - 1:],
                                       in_banks(acc[j])[:, full, SEQ - full * TG:].rearrange("p (b t) -> p b t", b=NB_DEC),
                                       ACT.Copy).then_inc(padded[j], 1)
                        act.wait_ge(padded[j], START + i + 1)
                        act.sem_inc(freed[j], 1)
                        act.wait_ge(conv[j], START + (i + 1) * WIDTH)
                        act.activation(out[:, j, :], raw[:, j, :], ACT.Silu,
                                       bias=tap[:, j, WIDTH:WIDTH + 1]).then_inc(activated[j], 1)
                        act.wait_ge(activated[j], START + i + 1)
                        act.dma_start(dram["xbc"][bass.ds((2 * i + j) * P, P), :], out[:, j, :]).then_inc(stored[j], 16)

                zbase, zpairs = tile_range("z")
                with act.Fori(0, zpairs) as i:
                    for j in range(2):
                        act.wait_ge(made[j], START + i + zbase + 1)
                        act.wait_ge(stored[j], START + 16 * (i + zbase))
                        act.activation(grouped(out[:, j, :]), in_banks(acc[j]), ACT.Silu).then_inc(z_silu[j], 1)
                        act.wait_ge(z_silu[j], START + i + 1)
                        act.sem_inc(freed[j], 1)
                        act.dma_start(dram["z"][bass.ds((2 * i + j) * P, P), :], out[:, j, :]).then_inc(stored[j], 16)
                for j in range(2):
                    act.wait_ge(stored[j], START + 16 * (NQ + NX + NZ) // 2)
                act.wait_ge(tails[0], START + NX // 2)
                act.wait_ge(tails[1], START + NX // 2)
                act.dma_start(dram["conv_tail"], tail[:].rearrange("p f c -> p (f c)")).then_inc(tail_stored, 16)
                act.wait_ge(tail_stored, START + 16)

            @block.vector
            def _(dve):
                dve.memset(eps[:], EPS).then_inc(zeroed, 1)
                dve.memset(pre[:, :, 0:WIDTH - 1], 0.0).then_inc(zeroed, 1)
                dve.memset(x_hi[:, :, NTOK:NPAD].bitcast(F32), 0.0).then_inc(zeroed, 1)
                dve.memset(x_lo[:, :, NTOK:NPAD].bitcast(F32), 0.0).then_inc(zeroed, 1)
                dve.wait_ge(small, START + 32)
                with dve.Fori(0, NQ // 2) as i:
                    for j in range(2):
                        dve.wait_ge(normed[j], START + i)
                        dve.tensor_copy(gain[:, j, :], gains[:, bass.ds(2 * i + j, 1)]).then_inc(gained[j], 1)
                        dve.wait_ge(rooted[0], START + 2 * (2 * i + j) + 2)
                        dve.wait_ge(rooted[1], START + 2 * i + j + 1)
                        dve.reciprocal(rinv[:, j, :], rinv[:, j, :]).then_inc(inverted[j], 1)
                        dve.wait_ge(inverted[j], START + i + 1)
                        dve.wait_ge(gained[j], START + i + 1)
                        dve.wait_ge(stored[j], START + 16 * i)
                        dve.scalar_tensor_tensor(out=out[:, j, :], in0=raw[:, j, :], scalar=gain[:, j, :],
                                                 in1=rinv[:, j, :], op0=ALU.mult, op1=ALU.mult).then_inc(normed[j], 1)
                for j in range(2):
                    dve.wait_ge(normed[j], START + NQ // 2)
                base, pairs = tile_range("xbc")
                with dve.Fori(0, pairs) as i:
                    for j in range(2):
                        f = bass.ds(2 * i + j, 1)
                        dve.wait_ge(activated[j], START + i)
                        dve.tensor_copy(tap[:, j, :], taps[:, f, :].rearrange("p o t -> p (o t)"))
                        dve.tensor_copy(pre_s[:, j, :, 0:WIDTH - 1],
                                        past_s[:, f, :].rearrange("p o (b t) -> p (o b) t", b=NB_DEC)
                                        ).then_inc(tapped[j], 1)
                        dve.wait_ge(tapped[j], START + i + 1)
                        dve.wait_ge(padded[j], START + i + 1)
                        dve.wait_ge(stored[j], START + 16 * (i + base))
                        acc_p = raw[:, j, 0:SEQ]
                        acc_s = raw[:, j, SEQ:NTOK].rearrange("p (b t) -> p b t", b=NB_DEC)
                        for t in range(WIDTH):
                            w = tap[:, j, t:t + 1]
                            if t == 0:
                                dve.tensor_scalar(acc_p, pre[:, j, 0:SEQ], w, None, ALU.mult)
                                dve.tensor_scalar(acc_s, pre_s[:, j, :, 0:T_DEC], w, None,
                                                  ALU.mult).then_inc(conv[j], 1)
                            else:
                                dve.wait_ge(conv[j], START + i * WIDTH + t)
                                dve.scalar_tensor_tensor(out=acc_p, in0=pre[:, j, t:t + SEQ], scalar=w,
                                                         in1=acc_p, op0=ALU.mult, op1=ALU.add)
                                dve.scalar_tensor_tensor(out=acc_s, in0=pre_s[:, j, :, t:t + T_DEC], scalar=w,
                                                         in1=acc_s, op0=ALU.mult, op1=ALU.add).then_inc(conv[j], 1)
                        dve.tensor_copy(tail[:, f, 0:WIDTH - 1].rearrange("p o t -> p (o t)"),
                                        pre[:, j, SEQ:SEQ + WIDTH - 1])
                        dve.tensor_copy(tail[:, f, WIDTH - 1:].rearrange("p o (b t) -> p (o b) t", b=NB_DEC),
                                        pre_s[:, j, :, T_DEC:]).then_inc(tails[j], 1)


def project_tokens(kit, x_hi, x_lo):
    nc, dram = kit.nc, kit.dram
    NTT = NT + 1
    NV = D + NH
    with ExitStack() as mem:
        def sb(n, s, d=F32):
            return mem.enter_context(nc.sbuf_tensor(n, s, d))

        w_raw = sb("wv_raw", [P, 2, NV])
        w_hi, w_lo = sb("wv_hi", [P, KD, NV], F32R), sb("wv_lo", [P, KD, NV], F32R)
        v_out = sb("v_out", [P, 2, D])
        dt_raw, dt_abs, dt_exp, dt_all = (sb(n, [P, NTT, NH]) for n in ("dt_raw", "dt_abs", "dt_exp", "dt_all"))
        bias = sb("dt_bias", [P, NH])
        acc = [mem.enter_context(nc.psum_tensor(f"v_ps{j}", [P, 3 * 512], F32)) for j in range(2)]
        w_loaded, w_hi_made, w_split = (kit.sems(f"wv_{n}", 2) for n in ("loaded", "hi", "split"))
        made, v_copied, dt_copied, stored = (kit.sems(f"v_{n}", 2) for n in ("made", "copied", "dt", "stored"))
        small, soft, dt_stored = kit.sems("dt_small"), kit.sems("dt_soft"), kit.sems("dt_stored")

        with nc.Block() as block:
            @block.sync
            def _(sp):
                sp.dma_start(bias[:], dram["dt_bias"].partition_broadcast(P)).then_inc(small, 16)
                for k in range(KD):
                    if k >= 2:
                        sp.wait_ge(w_split[k % 2], START + k // 2)
                    sp.dma_start(w_raw[:, k % 2, :], dram["w_tok"][k]).then_inc(w_loaded[k % 2], 16)

            @block.gpsimd
            def _(pool):
                kit.prime(pool)
                for k in range(KD):
                    pool.wait_ge(w_loaded[k % 2], START + 16 * (k // 2 + 1))
                    pool.tensor_copy(w_hi[:, k, :], w_raw[:, k % 2, :]).then_inc(w_hi_made[k % 2], 1)
                    pool.wait_ge(w_hi_made[k % 2], START + k // 2 + 1)
                    pool.tensor_tensor(w_lo[:, k, :], w_raw[:, k % 2, :], w_hi[:, k, :].bitcast(F32),
                                       ALU.subtract).then_inc(w_split[k % 2], 1)

            @block.tensor
            def _(pe):
                for t in range(NTT):
                    j = t % 2
                    if t >= 2:
                        pe.wait_ge(v_copied[j], START + t // 2)
                        pe.wait_ge(dt_copied[j], START + t // 2)
                    for k in range(KD):
                        if t == 0:
                            pe.wait_ge(w_split[k % 2], START + k // 2 + 1)
                        tok = slice(t * P, (t + 1) * P)
                        for wt, xt in ((w_hi, x_hi), (w_lo, x_hi), (w_hi, x_lo)):
                            for c in range(0, NV, TG):
                                w = min(TG, NV - c)
                                mm = pe.matmul(bank(acc[j], c, w), xt[:, k, tok], wt[:, k, c:c + w],
                                               start=(k == 0 and wt is w_hi and xt is x_hi),
                                               stop=(k == KD - 1 and xt is x_lo))
                    mm.then_inc(made[j], 1)

            @block.scalar
            def _(act):
                for t in range(NTT):
                    j = t % 2
                    act.wait_ge(made[j], START + t // 2 + 1)
                    if t >= 2:
                        act.wait_ge(stored[j], START + 16 * (t // 2))
                    full = D // TG
                    act.activation(v_out[:, j, 0:full * TG].rearrange("p (g c) -> p g c", g=full),
                                   in_banks(acc[j])[:, 0:full, :], ACT.Copy)
                    act.activation(v_out[:, j, full * TG:], in_banks(acc[j])[:, full, 0:D - full * TG],
                                   ACT.Copy).then_inc(v_copied[j], 1)
                    act.wait_ge(v_copied[j], START + t // 2 + 1)
                    act.dma_start(dram["v"][t * P:(t + 1) * P, :], v_out[:, j, :]).then_inc(stored[j], 16)
                act.wait_ge(soft, START + 2)
                act.activation(dt_exp[:], dt_abs[:], ACT.Exp).then_inc(soft, 1)
                act.wait_ge(soft, START + 3)
                act.activation(dt_abs[:], dt_exp[:], ACT.Ln, bias=1.0).then_inc(soft, 1)
                act.wait_ge(soft, START + 5)
                act.dma_start(dram["dt"].rearrange("(t p) h -> p t h", p=P), dt_all[:]).then_inc(dt_stored, 16)
                act.wait_ge(dt_stored, START + 16)
                for j in range(2):
                    act.wait_ge(stored[j], START + 16 * ((NTT + 1 - j) // 2))

            @block.vector
            def _(dve):
                dve.wait_ge(small, START + 16)
                for t in range(NTT):
                    j = t % 2
                    dve.wait_ge(v_copied[j], START + t // 2 + 1)
                    dve.tensor_tensor(dt_raw[:, t, :], bank(acc[j], D, TG)[:, D % TG:NV - D // TG * TG], bias[:],
                                      ALU.add).then_inc(dt_copied[j], 1)
                dve.wait_ge(dt_copied[0], START + (NTT + 1) // 2)
                dve.wait_ge(dt_copied[1], START + NTT // 2)
                dve.tensor_scalar(dt_all[:], dt_raw[:], -1.0, None, ALU.mult).then_inc(soft, 1)
                dve.wait_ge(soft, START + 1)
                dve.tensor_tensor(dt_abs[:], dt_all[:], dt_raw[:], ALU.min).then_inc(soft, 1)
                dve.wait_ge(soft, START + 4)
                dve.scalar_tensor_tensor(out=dt_all[:], in0=dt_raw[:], scalar=0.0, in1=dt_abs[:],
                                         op0=ALU.max, op1=ALU.add).then_inc(soft, 1)


def attend_prompt(kit):
    nc, dram = kit.nc, kit.dram
    SLOT_ITEMS = 2 * NT
    N = 2 * SLOT_ITEMS
    items = [(jp, (jp * NT + qt) * 2 + h, qt, h) for jp in range(2) for qt in range(NT) for h in range(2)]
    pieces, total = [], 0
    for _, _, qt, _ in items:
        row = [(total + n, b0, min(4, qt + 1 - b0)) for n, b0 in enumerate(range(0, qt + 1, 4))]
        total += len(row)
        pieces.append(row)
    SLOT_PIECES = total // 2
    LOADS = 8 + 1 + 2
    with ExitStack() as mem:
        def sb(n, s, d=F32):
            return mem.enter_context(nc.sbuf_tensor(n, s, d))

        q_raw, k_raw, v_raw = sb("att_q", [P, 2, 2, SEQ]), sb("att_k", [P, 2, 2, SEQ]), sb("att_v", [P, 2, NT, P])
        q_two = sb("att_q2", [P, 2, 2, SEQ], F32R)
        k_hi, k_lo = sb("att_khi", [P, 2, 2, SEQ], F32R), sb("att_klo", [P, 2, 2, SEQ], F32R)
        v_hi, v_lo = sb("att_vhi", [P, 2, NT, P], F32R), sb("att_vlo", [P, 2, NT, P], F32R)
        bias = sb("att_bias", [P, 2, 2, SEQ])
        logits, probs = sb("att_s", [P, 2, SEQ]), sb("att_p", [P, 2, SEQ])
        p_hi, p_lo = sb("att_pThi", [P, 2, NT, P], F32R), sb("att_pTlo", [P, 2, NT, P], F32R)
        top, neg, den, rden = (sb(f"att_{n}", [P, 2, 1]) for n in ("max", "negmax", "den", "rden"))
        oT = sb("att_oT", [P, 2, SEQ])
        s_ps = [mem.enter_context(nc.psum_tensor(f"att_s_ps{j}", [P, 1024], F32)) for j in range(2)]
        t_ps = [mem.enter_context(nc.psum_tensor(f"att_t_ps{j}", [P, 512], F32)) for j in range(2)]
        pv_ps = [mem.enter_context(nc.psum_tensor(f"att_pv_ps{j}", [P, 512], F32)) for j in range(2)]

        loaded, stored, pair_done = (kit.sems(f"att_{n}", 2) for n in ("loaded", "stored", "pair"))
        cast, split, prepared = (kit.sems(f"att_{n}", 2) for n in ("cast", "split", "prepared"))
        scored, biased, negated, exped = (kit.sems(f"att_{n}", 2) for n in ("scored", "biased", "negated", "exped"))
        inverted, normed = kit.sems("att_inverted", 2), kit.sems("att_normed", 2)
        flipped, hi_kept, lo_kept = (kit.sems(f"att_{n}", 2) for n in ("flipped", "hi", "lo"))
        multiplied, o_kept = kit.sems("att_multiplied", 2), kit.sems("att_okept", 2)

        def nth(i, m):
            return SLOT_ITEMS * i + m // 2

        def nth_piece(i, pn):
            return SLOT_PIECES * i + pn // 2

        def steps(first, second, third):
            for n in range(-2, N + 1):
                yield tuple(k if 0 <= k < N else None for k in (n + first, n + second, n + third))

        with nc.Block() as block:
            @block.sync
            def _(sp):
                sp.wait_ge(kit.skewed, 16 * (1 + 2 * T_DEC))
                with sp.Fori(0, NPAIR // 2) as i:
                    for jp in range(2):
                        pair = 2 * i + jp
                        sp.wait_ge(pair_done[jp], START + i)
                        for h in range(2):
                            for half in range(2):
                                rows = slice(half * HD, (half + 1) * HD)
                                sp.dma_start(q_raw[rows, jp, h, :], dram["qk"][bass.ds(pair * P + h * HD, HD), 0:SEQ]
                                             ).then_inc(loaded[jp], 16)
                                sp.dma_start(k_raw[rows, jp, h, :], dram["qk"][bass.ds(pair * P + (D + h * HD), HD), 0:SEQ]
                                             ).then_inc(loaded[jp], 16)
                            sp.dma_start(bias[:, jp, h, :], dram["bias_rows"][bass.ds((2 * pair + h) * P, P), :]
                                         ).then_inc(loaded[jp], 16)
                        sp.dma_start(v_raw[:, jp], dram["v"][0:SEQ, bass.ds(pair * P, P)]
                                     .rearrange("(t p) c -> p t c", p=P)).then_inc(loaded[jp], 16)

            @block.gpsimd
            def _(pool):
                kit.prime(pool)
                with pool.Fori(0, NPAIR // 2) as i:
                    for jp in range(2):
                        pool.wait_ge(cast[jp], START + i + 1)
                        pool.tensor_tensor(k_lo[:, jp], k_raw[:, jp], k_hi[:, jp].bitcast(F32), ALU.subtract)
                        pool.tensor_tensor(v_lo[:, jp], v_raw[:, jp], v_hi[:, jp].bitcast(F32),
                                           ALU.subtract).then_inc(split[jp], 1)
                        pool.wait_ge(split[jp], START + i + 1)
                        low = q_two[HD:P, jp]
                        pool.tensor_tensor(low, q_raw[HD:P, jp], low.bitcast(F32), ALU.subtract).then_inc(prepared[jp], 1)
                        pool.wait_ge(prepared[jp], START + i + 1)

            @block.tensor
            def _(pe):
                def score(i, n):
                    jp, m, qt, h = items[n]
                    j = m % 2
                    if qt == 0 and h == 0:
                        pe.wait_ge(prepared[jp], START + i + 1)
                    pe.wait_ge(biased[j], START + nth(i, m))
                    for c in range(0, (qt + 1) * P, 512):
                        w = min(512, (qt + 1) * P - c)
                        q = q_two[:, jp, h, qt * P:(qt + 1) * P]
                        pe.matmul(s_ps[j][:, c:c + w], q, k_hi[:, jp, h, c:c + w], start=True, stop=False)
                        mm = pe.matmul(s_ps[j][:, c:c + w], q, k_lo[:, jp, h, c:c + w], start=False, stop=True)
                    mm.then_inc(scored[j], 1)

                def turn(i, n):
                    j = items[n][1] % 2
                    pe.wait_ge(normed[j], START + nth(i, items[n][1]) + 1)
                    for pn, b0, nb in pieces[n]:
                        s = pn % 2
                        pe.wait_ge(lo_kept[s], START + nth_piece(i, pn))
                        for b in range(nb):
                            mm = pe.transpose(t_ps[s][:, b * P:(b + 1) * P],
                                              probs[:, j, (b0 + b) * P:(b0 + b + 1) * P], kit.c(C_IDENT, P))
                        mm.then_inc(flipped[s], 1)

                def values(i, n):
                    jp, m, qt, h = items[n]
                    j = m % 2
                    pe.wait_ge(o_kept[j], START + nth(i, m))
                    cols = slice(h * HD, (h + 1) * HD)
                    for pn, b0, nb in pieces[n]:
                        pe.wait_ge(lo_kept[pn % 2], START + nth_piece(i, pn) + 1)
                        for b in range(b0, b0 + nb):
                            out = pv_ps[j][0:HD, 0:P]
                            pe.matmul(out, v_hi[:, jp, b, cols], p_hi[:, j, b, :], start=(b == 0), stop=False)
                            pe.matmul(out, v_hi[:, jp, b, cols], p_lo[:, j, b, :], start=False, stop=False)
                            mm = pe.matmul(out, v_lo[:, jp, b, cols], p_hi[:, j, b, :], start=False, stop=(b == qt))
                    mm.then_inc(multiplied[j], 1)

                with pe.Fori(0, NPAIR // 2) as i:
                    for t, v, sc in steps(0, -1, 2):
                        if t is not None:
                            turn(i, t)
                        if v is not None:
                            values(i, v)
                        if sc is not None:
                            score(i, sc)

            @block.vector
            def _(dve):
                def bias_max(i, n):
                    jp, m, qt, h = items[n]
                    j, w = m % 2, (qt + 1) * P
                    if qt == 0 and h == 0:
                        dve.wait_ge(loaded[jp], START + LOADS * 16 * (i + 1))
                    dve.wait_ge(scored[j], START + nth(i, m) + 1)
                    dve.wait_ge(exped[j], START + nth(i, m))
                    kit.settle(dve)
                    dve.tensor_tensor_reduce(out=logits[:, j, 0:w], in0=s_ps[j][:, 0:w],
                                             in1=bias[:, jp, h, SEQ - w:SEQ], scale=1.0, scalar=-3e38,
                                             op0=ALU.add, op1=ALU.max,
                                             accum_out=top[:, j, :]).then_inc(biased[j], 1)
                    dve.wait_ge(biased[j], START + nth(i, m) + 1)
                    dve.tensor_scalar(neg[:, j, :], top[:, j, :], -1.0, None, ALU.mult).then_inc(negated[j], 1)

                def normalise(i, n):
                    _, m, qt, _ = items[n]
                    j, w = m % 2, (qt + 1) * P
                    dve.wait_ge(exped[j], START + nth(i, m) + 1)
                    dve.reciprocal(rden[:, j, :], den[:, j, :]).then_inc(inverted[j], 1)
                    dve.wait_ge(inverted[j], START + nth(i, m) + 1)
                    dve.tensor_scalar(probs[:, j, 0:w], probs[:, j, 0:w], rden[:, j, :], None,
                                      ALU.mult).then_inc(normed[j], 1)

                def keep_low(i, n):
                    m = items[n][1]
                    j = m % 2
                    for pn, b0, nb in pieces[n]:
                        s = pn % 2
                        dve.wait_ge(hi_kept[s], START + nth_piece(i, pn) + 1)
                        dve.tensor_tensor(p_lo[:, j, b0:b0 + nb, :].rearrange("p b q -> p (b q)"), t_ps[s][:, 0:nb * P],
                                          p_hi[:, j, b0:b0 + nb, :].rearrange("p b q -> p (b q)").bitcast(F32),
                                          ALU.subtract).then_inc(lo_kept[s], 1)

                with dve.Fori(0, NPAIR // 2) as i:
                    for nm, lo, bm in steps(1, 0, 2):
                        if nm is not None:
                            normalise(i, nm)
                        if lo is not None:
                            keep_low(i, lo)
                        if bm is not None:
                            bias_max(i, bm)

            @block.scalar
            def _(act):
                def cast_pair(i, jp):
                    act.wait_ge(loaded[jp], START + LOADS * 16 * (i + 1))
                    act.activation(k_hi[:, jp], k_raw[:, jp], ACT.Copy)
                    act.activation(v_hi[:, jp], v_raw[:, jp], ACT.Copy)
                    act.activation(q_two[:, jp], q_raw[:, jp], ACT.Copy).then_inc(cast[jp], 1)

                def exponent(i, n):
                    _, m, qt, _ = items[n]
                    j, w = m % 2, (qt + 1) * P
                    act.wait_ge(negated[j], START + nth(i, m) + 1)
                    if n >= 2:
                        for pn, _, _ in pieces[n - 2]:
                            act.wait_ge(flipped[pn % 2], START + nth_piece(i, pn) + 1)
                    else:
                        act.wait_ge(flipped[0], START + SLOT_PIECES * i)
                        act.wait_ge(flipped[1], START + SLOT_PIECES * i)
                    act.activation(probs[:, j, 0:w], logits[:, j, 0:w], ACT.Exp, bias=neg[:, j, :],
                                   accum_out=den[:, j, :]).then_inc(exped[j], 1)

                def keep_high(i, n):
                    m = items[n][1]
                    j = m % 2
                    for k, (pn, b0, nb) in enumerate(pieces[n]):
                        act.wait_ge(flipped[pn % 2], START + nth_piece(i, pn) + 1)
                        if k == 0:
                            act.wait_ge(multiplied[j], START + nth(i, m))
                        act.activation(p_hi[:, j, b0:b0 + nb, :].rearrange("p b q -> p (b q)"),
                                       t_ps[pn % 2][:, 0:nb * P], ACT.Copy).then_inc(hi_kept[pn % 2], 1)

                def keep_out(i, n):
                    jp, m, qt, h = items[n]
                    j = m % 2
                    act.wait_ge(multiplied[j], START + nth(i, m) + 1)
                    if qt == 0 and h == 0:
                        act.wait_ge(stored[jp], START + 16 * i)
                    act.activation(oT[h * HD:(h + 1) * HD, jp, qt * P:(qt + 1) * P], pv_ps[j][0:HD, 0:P],
                                   ACT.Copy).then_inc(o_kept[j], 1)
                    if qt == NT - 1 and h == 1:
                        act.wait_ge(o_kept[j], START + nth(i, m) + 1)
                        act.sem_inc(pair_done[jp], 1)
                        act.dma_start(dram["mix"][bass.ds((2 * i + jp) * P, P), 0:SEQ], oT[:, jp, :]).then_inc(stored[jp], 16)

                def body(i, last):
                    for n, (ex, hi, out) in enumerate(steps(1, 0, -1)):
                        if n == N // 4:
                            cast_pair(i, 1)
                        if n == 3 * N // 4 and not last:
                            cast_pair(i + 1, 0)
                        if ex is not None:
                            exponent(i, ex)
                        if hi is not None:
                            keep_high(i, hi)
                        if out is not None:
                            keep_out(i, out)

                cast_pair(0, 0)
                with act.Fori(0, NPAIR // 2 - 1) as i:
                    body(i, False)
                body(NPAIR // 2 - 1, True)
                for jp in range(2):
                    act.wait_ge(stored[jp], START + 16 * (NPAIR // 2))


def attend_sample(kit):
    nc, dram = kit.nc, kit.dram
    R = NH * T_DEC
    with ExitStack() as mem:
        def sb(n, s, d=F32):
            return mem.enter_context(nc.sbuf_tensor(n, s, d))

        kT, v = sb("sa_k", [P, 2, NPAIR, NKEY]), sb("sa_v", [P, 2, VT, D])
        v_new = sb("sa_vnew", [T_DEC, 2, D])
        q_all, k_new = sb("sa_q", [P, NPAIR, NS]), sb("sa_knew", [P, NPAIR, NS])
        q_diag = sb("sa_qdiag", [P, 2, NPAIR, R])
        bias = sb("sa_bias", [R, NKEY])
        logits, probs = sb("sa_s", [R, 2, NKEY]), sb("sa_p", [R, 2, NKEY])
        turned, turned_new = sb("sa_pT", [P, 2, VT, R]), sb("sa_pTn", [T_DEC, 2, R])
        top, neg, den, rden = (sb(f"sa_{n}", [R, 2, 1]) for n in ("max", "negmax", "den", "rden"))
        own, o_tok = sb("sa_own", [R, 2, D]), sb("sa_o", [T_DEC, 2, D])
        oT = sb("sa_oT", [P, KD, NS])
        s_ps = mem.enter_context(nc.psum_tensor("sa_s_ps", [P, 1024], F32))
        t_ps = mem.enter_context(nc.psum_tensor("sa_t_ps", [P, 512], F32))
        pv_ps = mem.enter_context(nc.psum_tensor("sa_pv_ps", [P, 1024], F32))
        o_ps = mem.enter_context(nc.psum_tensor("sa_o_ps", [P, 1024], F32))
        ot_ps = mem.enter_context(nc.psum_tensor("sa_ot_ps", [P, 512], F32))

        loaded, placed = kit.sems("sa_loaded", 2), kit.sems("sa_placed", 2)
        common, zeroed, placing = kit.sems("sa_common"), kit.sems("sa_zeroed"), kit.sems("sa_placing")
        scored, biased, negated, exped = (kit.sems(f"sa_{n}", 2) for n in ("scored", "biased", "negated", "exped"))
        flipped, turned_done, multiplied = (kit.sems(f"sa_{n}", 2) for n in ("flipped", "turned", "multiplied"))
        inverted, owned, gathered, copied = (kit.sems(f"sa_{n}", 2) for n in ("inverted", "owned", "gathered", "copied"))
        o_turned, o_kept, stored = kit.sems("sa_oturned"), kit.sems("sa_okept"), kit.sems("sa_stored")

        with nc.Block() as block:
            @block.sync
            def _(sp):
                qk = dram["qk"].rearrange("(f p) t -> p f t", p=P)
                sp.dma_start(q_all[:], qk[:, 0:NPAIR, SEQ:NTOK]).then_inc(common, 16)
                sp.dma_start(k_new[:], qk[:, NPAIR:2 * NPAIR, SEQ:NTOK]).then_inc(common, 16)
                sp.dma_start(bias[:], dram["bias_sample"]).then_inc(common, 16)
                with sp.Fori(0, NB_DEC // 2) as i:
                    for j in range(2):
                        b = 2 * i + j
                        sp.wait_ge(multiplied[j], START + i)
                        sp.dma_start(kT[:, j, :, 0:FAR + DENSE], dram["cache_k"][bass.ds(b, 1)]
                                     .rearrange("o p (f t) -> p (o f) t", f=NPAIR)).then_inc(loaded[j], 16)
                        sp.dma_start(v[:, j], dram["cache_v"][bass.ds(b, 1)]
                                     .rearrange("o p (t c) -> p (o t) c", t=VT)).then_inc(loaded[j], 16)
                        sp.dma_start(v_new[:, j, :], dram["v"][bass.ds(b * T_DEC + SEQ, T_DEC), :]).then_inc(loaded[j], 16)

            @block.gpsimd
            def _(pool):
                kit.prime(pool)
                pool.memset(q_diag[:], 0.0).then_inc(zeroed, 1)
                pool.wait_ge(zeroed, START + 1)
                pool.wait_ge(common, START + 48)
                with pool.Fori(0, NB_DEC // 2) as i:
                    for j in range(2):
                        tok = bass.ds((2 * i + j) * T_DEC, T_DEC)
                        pool.wait_ge(scored[j], START + i)
                        pool.tensor_copy(kT[:, j, :, FAR + DENSE:], k_new[:, :, tok]).then_inc(placing, 1)
                        for h in range(2):
                            pool.wait_ge(placing, START + 2 * (2 * i + j) + h + 1)
                            rows = q_diag[h * HD:(h + 1) * HD, j]
                            cols = bass.AP(rows.tensor, rows.offset + h * T_DEC,
                                           [list(rows.ap[0]), [R + 2 * T_DEC, NPAIR], [1, T_DEC]])
                            pool.tensor_copy(cols, q_all[h * HD:(h + 1) * HD, :, tok]).then_inc(
                                placed[j] if h else placing, 1)
                        pool.wait_ge(placed[j], START + i + 1)

            @block.tensor
            def _(pe):
                with pe.Fori(0, NB_DEC // 2) as i:
                    for j in range(2):
                        pe.wait_ge(loaded[j], START + 48 * (i + 1))
                        pe.wait_ge(placed[j], START + i + 1)
                        if j:
                            pe.wait_ge(biased[0], START + i + 1)
                        else:
                            pe.wait_ge(biased[1], START + i)
                        for f in range(NPAIR):
                            for c, w in ((0, 512), (512, NKEY - 512)):
                                mm = pe.matmul(s_ps[0:R, c:c + w], q_diag[:, j, f, :], kT[:, j, f, c:c + w],
                                               start=(f == 0), stop=(f == NPAIR - 1))
                        mm.then_inc(scored[j], 1)
                        pe.wait_ge(exped[j], START + i + 1)
                        if j:
                            pe.wait_ge(turned_done[0], START + i + 1)
                        else:
                            pe.wait_ge(turned_done[1], START + i)
                        kit.settle(pe)
                        for t in range(VT):
                            pe.transpose(t_ps[:, t * R:(t + 1) * R], probs[:, j, t * P:(t + 1) * P],
                                         kit.c(C_IDENT, R, R))
                        pe.transpose(t_ps[0:T_DEC, VT * R:(VT + 1) * R], probs[:, j, VT * P:NKEY],
                                     kit.c(C_IDENT, R, R)).then_inc(flipped[j], 1)
                        pe.wait_ge(turned_done[j], START + i + 1)
                        if j:
                            pe.wait_ge(owned[0], START + i + 1)
                        else:
                            pe.wait_ge(owned[1], START + i)
                        for c in (0, 512):
                            for t in range(VT):
                                pe.matmul(pv_ps[0:R, c:c + 512], turned[:, j, t, :], v[:, j, t, c:c + 512],
                                          start=(t == 0), stop=False)
                            mm = pe.matmul(pv_ps[0:R, c:c + 512], turned_new[:, j, :], v_new[:, j, c:c + 512],
                                           start=False, stop=True)
                        mm.then_inc(multiplied[j], 1)
                        pe.wait_ge(owned[j], START + i + 1)
                        if j:
                            pe.wait_ge(copied[0], START + i + 1)
                        else:
                            pe.wait_ge(copied[1], START + i)
                        kit.settle(pe)
                        for c in (0, 512):
                            mm = pe.matmul(o_ps[0:T_DEC, c:c + 512], kit.c(C_SEL, T_DEC, R), own[:, j, c:c + 512],
                                           start=True, stop=True)
                        mm.then_inc(gathered[j], 1)
                        pe.wait_ge(copied[j], START + i + 1)
                        if j:
                            pe.wait_ge(o_kept, START + 2 * i + 1)
                        else:
                            pe.wait_ge(o_kept, START + 2 * i)
                        kit.settle(pe)
                        for f in range(KD):
                            mm = pe.transpose(ot_ps[:, f * T_DEC:(f + 1) * T_DEC], o_tok[:, j, f * P:(f + 1) * P],
                                              kit.c(C_IDENT, T_DEC, T_DEC))
                        mm.then_inc(o_turned, 1)

            @block.vector
            def _(dve):
                dve.wait_ge(common, START + 48)
                with dve.Fori(0, NB_DEC // 2) as i:
                    for j in range(2):
                        dve.wait_ge(scored[j], START + i + 1)
                        dve.wait_ge(exped[j], START + i)
                        kit.settle(dve)
                        dve.tensor_tensor_reduce(out=logits[:, j, :], in0=s_ps[0:R, 0:NKEY], in1=bias[:], scale=1.0,
                                                 scalar=-3e38, op0=ALU.add, op1=ALU.max,
                                                 accum_out=top[:, j, :]).then_inc(biased[j], 1)
                        dve.wait_ge(biased[j], START + i + 1)
                        dve.tensor_scalar(neg[:, j, :], top[:, j, :], -1.0, None, ALU.mult).then_inc(negated[j], 1)
                        dve.wait_ge(exped[j], START + i + 1)
                        dve.reciprocal(rden[:, j, :], den[:, j, :]).then_inc(inverted[j], 1)
                        dve.wait_ge(inverted[j], START + i + 1)
                        dve.wait_ge(multiplied[j], START + i + 1)
                        dve.wait_ge(gathered[j], START + i)
                        dve.scalar_tensor_tensor(out=own[:, j, :], in0=pv_ps[0:R, :], scalar=rden[:, j, :],
                                                 in1=kit.c(C_DIAG, D, R), op0=ALU.mult, op1=ALU.mult).then_inc(owned[j], 1)
                        dve.wait_ge(o_turned, START + 2 * i + j + 1)
                        dve.tensor_copy(oT[:, :, bass.ds((2 * i + j) * T_DEC, T_DEC)],
                                        ot_ps[:, 0:KD * T_DEC].rearrange("p (f t) -> p f t", f=KD)).then_inc(o_kept, 1)

            @block.scalar
            def _(act):
                with act.Fori(0, NB_DEC // 2) as i:
                    for j in range(2):
                        act.wait_ge(negated[j], START + i + 1)
                        act.wait_ge(inverted[j], START + i)
                        act.wait_ge(flipped[j], START + i)
                        act.activation(probs[:, j, :], logits[:, j, :], ACT.Exp, bias=neg[:, j, :],
                                       accum_out=den[:, j, :]).then_inc(exped[j], 1)
                        act.wait_ge(flipped[j], START + i + 1)
                        act.wait_ge(multiplied[j], START + i)
                        act.activation(turned[:, j].rearrange("p t r -> p (t r)"), t_ps[:, 0:VT * R], ACT.Copy)
                        act.activation(turned_new[:, j, :], t_ps[0:T_DEC, VT * R:(VT + 1) * R],
                                       ACT.Copy).then_inc(turned_done[j], 1)
                        act.wait_ge(gathered[j], START + i + 1)
                        act.wait_ge(o_turned, START + 2 * i + j)
                        act.activation(o_tok[:, j, :], o_ps[0:T_DEC, :], ACT.Copy).then_inc(copied[j], 1)
                act.wait_ge(o_kept, START + NB_DEC)
                act.dma_start(dram["mix"][0:D, SEQ:NTOK].rearrange("(f p) t -> p f t", p=P), oT[:]).then_inc(stored, 16)
                act.wait_ge(stored, START + 16)


def scan_prompt(kit, neg_a, skip):
    nc, dram = kit.nc, kit.dram
    HG = NH // 2
    with ExitStack() as mem:
        def sb(n, s, d=F32):
            return mem.enter_context(nc.sbuf_tensor(n, s, d))

        def ps(n, w):
            return mem.enter_context(nc.psum_tensor(n, [P, w], F32))

        xbc, zT, dt = sb("ssd_xbc", [P, 2, XBC_TILES, P]), sb("ssd_z", [P, 2, KD, P]), sb("ssd_dt", [P, 2, NH])
        dta, decays = sb("ssd_dta", [P, NH]), sb("ssd_decays", [P, 3, NH])
        x_tok, xdt, xw = sb("ssd_x", [P, D]), sb("ssd_xdt", [P, D]), sb("ssd_xw", [P, D])
        b_tok, cb = sb("ssd_btok", [P, 2 * P]), sb("ssd_cb", [P, 2, P])
        steps, mixm = sb("ssd_steps", [P, 2, 4, P]), sb("ssd_m", [P, 4, 4, P])
        y, yT, state = sb("ssd_y", [P, D]), sb("ssd_yT", [P, 2, KD, P]), sb("ssd_state", [P, D])
        skipped = sb("ssd_skip", [P, KD, P])
        turn_ps, misc_ps, seg_ps = ps("ssd_turn", D), ps("ssd_misc", 512), ps("ssd_seg", 512)
        in_ps, off_ps = ps("ssd_in", D), ps("ssd_off", D)

        loaded = kit.sems("ssd_loaded", 2)
        (zeroed, dta_made, x_turned, bcb_made, sums_made, sums_exp, x_kept, xdt_made, xw_made, btok_kept, cb_masked,
         steps_made, seg_made, seg_exp, mix_made, in_made, off_made, y_scaled, y_summed, y_turned, skip_made, y_skipped,
         state_made, state_decayed, state_summed) = (kit.sems(f"ssd_{n}") for n in (
             "zeroed", "dta_done", "xturned", "bcb", "sums", "sumsexp", "xkept", "xdtdone", "xwdone", "btokkept",
             "cbmasked", "stepsdone", "segdone", "segexp", "mixdone", "indone", "offdone", "yscaled", "ysummed",
             "yturned", "skipdone", "yskipped", "stdone", "stdecayed", "stsummed"))
        gated = kit.sems("ssd_gated", 2)
        stored, state_stored = kit.sems("ssd_stored", 2), kit.sems("ssd_ststored")

        def heads(ap):
            return ap.rearrange("p (h c) -> p h c", h=NH)

        def per_head(ap, w=HD):
            return ap.unsqueeze(2).broadcast_to([P, ap.shape[1], w])

        with nc.Block() as block:
            @block.sync
            def _(sp):
                def load(i, j):
                    sp.wait_ge(gated[j], START + i)
                    cols = bass.ds((2 * i + j) * P, P)
                    sp.dma_start(xbc[:, j], dram["xbc"][:, cols].rearrange("(f p) t -> p f t", p=P)).then_inc(loaded[j], 16)
                    sp.dma_start(zT[:, j], dram["z"][:, cols].rearrange("(f p) t -> p f t", p=P)).then_inc(loaded[j], 16)
                    sp.dma_start(dt[:, j, :], dram["dt"][cols, :]).then_inc(loaded[j], 16)

                def store(i, j):
                    sp.wait_ge(gated[j], START + i + 1)
                    sp.dma_start(dram["mix"][D:2 * D, bass.ds((2 * i + j) * P, P)].rearrange("(f p) t -> p f t", p=P),
                                 yT[:, j]).then_inc(stored[j], 16)

                load(0, 0)
                with sp.Fori(0, NT // 2 - 1) as i:
                    load(i, 1)
                    store(i, 0)
                    load(i + 1, 0)
                    store(i, 1)
                load(NT // 2 - 1, 1)
                store(NT // 2 - 1, 0)
                store(NT // 2 - 1, 1)
                for j in range(2):
                    sp.wait_ge(stored[j], START + 16 * (NT // 2))

            @block.tensor
            def _(pe):
                with pe.Fori(0, NT // 2) as i:
                    for j in range(2):
                        n = 2 * i + j
                        pe.wait_ge(loaded[j], START + 48 * (i + 1))
                        pe.wait_ge(y_skipped, START + n)
                        for f in range(KD):
                            mm = pe.transpose(turn_ps[:, f * P:(f + 1) * P], xbc[:, j, f, :], kit.c(C_IDENT, P))
                        mm.then_inc(x_turned, 1)
                        pe.wait_ge(btok_kept, START + n)
                        pe.wait_ge(cb_masked, START + n)
                        for g in range(2):
                            pe.transpose(misc_ps[:, g * P:(g + 1) * P], xbc[:, j, KD + g, :], kit.c(C_IDENT, P))
                        for g in range(2):
                            mm = pe.matmul(misc_ps[:, (2 + g) * P:(3 + g) * P], xbc[:, j, KD + g, :],
                                           xbc[:, j, KD + 2 + g, :], start=True, stop=True)
                        mm.then_inc(bcb_made, 1)
                        pe.wait_ge(dta_made, START + n + 1)
                        pe.wait_ge(seg_exp, START + 4 * n)
                        for s, m in enumerate((C_UPPER, C_LOWER, C_ONES)):
                            mm = pe.matmul(seg_ps[:, s * NH:(s + 1) * NH], kit.c(m, P), dta[:], start=True, stop=True)
                        mm.then_inc(sums_made, 1)
                        pe.wait_ge(state_summed, START + n)
                        pe.wait_ge(zeroed, START + 1)
                        for g in range(2):
                            mm = pe.matmul(off_ps[:, g * 512:(g + 1) * 512], xbc[:, j, KD + 2 + g, :],
                                           state[:, g * 512:(g + 1) * 512], start=True, stop=True)
                        mm.then_inc(off_made, 1)
                        for q in range(4):
                            pe.wait_ge(steps_made, START + 4 * n + q + 1)
                            if q == 0:
                                pe.wait_ge(sums_exp, START + n + 1)
                            else:
                                pe.wait_ge(seg_exp, START + 4 * n + q)
                            pe.matmul(seg_ps[:], kit.c(C_LOWER, P), steps[:, q % 2].rearrange("p h t -> p (h t)"),
                                      start=True, stop=True).then_inc(seg_made, 1)
                        pe.wait_ge(y_scaled, START + n + 1)
                        pe.wait_ge(xw_made, START + n + 1)
                        pe.wait_ge(btok_kept, START + n + 1)
                        for g in range(2):
                            mm = pe.matmul(off_ps[:, g * 512:(g + 1) * 512], b_tok[:, g * P:(g + 1) * P],
                                           xw[:, g * 512:(g + 1) * 512], start=True, stop=True)
                        mm.then_inc(state_made, 1)
                        for h in range(NH):
                            if h == 0:
                                pe.wait_ge(xdt_made, START + n + 1)
                                pe.wait_ge(y_summed, START + n)
                            if h % 4 == 0:
                                pe.wait_ge(mix_made, START + 4 * n + h // 4 + 1)
                            mm = pe.matmul(in_ps[:, h * HD:(h + 1) * HD], mixm[:, h // 4, h % 4, :],
                                           xdt[:, h * HD:(h + 1) * HD], start=True, stop=True)
                        mm.then_inc(in_made, 1)
                        pe.wait_ge(y_summed, START + n + 1)
                        for f in range(KD):
                            mm = pe.transpose(turn_ps[:, f * P:(f + 1) * P], y[:, f * P:(f + 1) * P], kit.c(C_IDENT, P))
                        mm.then_inc(y_turned, 1)

            @block.gpsimd
            def _(pool):
                kit.prime(pool)
                pool.memset(state[:], 0.0).then_inc(zeroed, 1)
                with pool.Fori(0, NT // 2) as i:
                    for j in range(2):
                        n = 2 * i + j
                        pool.wait_ge(loaded[j], START + 48 * (i + 1))
                        pool.wait_ge(sums_made, START + n)
                        pool.tensor_tensor(dta[:], dt[:, j, :], neg_a[:], ALU.mult).then_inc(dta_made, 1)
                        pool.wait_ge(dta_made, START + n + 1)
                        for q in range(4):
                            if q < 2:
                                pool.wait_ge(seg_made, START + 4 * n)
                            else:
                                pool.wait_ge(seg_made, START + 4 * n + q - 1)
                            pool.tensor_tensor(steps[:, q % 2], kit.c(C_UPPER, P).unsqueeze(1).broadcast_to([P, 4, P]),
                                               per_head(dta[:, 4 * q:4 * q + 4], P), ALU.mult).then_inc(steps_made, 1)
                        pool.wait_ge(x_kept, START + n + 1)
                        pool.wait_ge(in_made, START + n)
                        pool.tensor_tensor(heads(xdt[:]), heads(x_tok[:]), per_head(dt[:, j, :]), ALU.mult).then_inc(xdt_made, 1)
                        pool.wait_ge(xdt_made, START + n + 1)
                        pool.wait_ge(sums_exp, START + n + 1)
                        pool.wait_ge(state_made, START + n)
                        pool.tensor_tensor(heads(xw[:]), heads(xdt[:]), per_head(decays[:, 1, :]), ALU.mult).then_inc(xw_made, 1)
                        pool.wait_ge(y_skipped, START + n)
                        pool.tensor_tensor(skipped[:], xbc[:, j, 0:KD, :],
                                           skip[:].unsqueeze(2).broadcast_to([P, KD, P]), ALU.mult).then_inc(skip_made, 1)
                        pool.wait_ge(off_made, START + n + 1)
                        pool.tensor_tensor(heads(state[:]), heads(state[:]), per_head(decays[:, 2, :]),
                                           ALU.mult).then_inc(state_decayed, 1)

            @block.scalar
            def _(act):
                with act.Fori(0, NT // 2) as i:
                    for j in range(2):
                        n = 2 * i + j
                        act.wait_ge(x_turned, START + n + 1)
                        act.wait_ge(xdt_made, START + n)
                        act.activation(x_tok[:], turn_ps[:], ACT.Copy).then_inc(x_kept, 1)
                        act.wait_ge(bcb_made, START + n + 1)
                        act.wait_ge(state_made, START + n)
                        act.activation(b_tok[:], misc_ps[:, 0:2 * P], ACT.Copy).then_inc(btok_kept, 1)
                        act.wait_ge(sums_made, START + n + 1)
                        act.wait_ge(state_decayed, START + n)
                        act.wait_ge(y_scaled, START + n)
                        act.activation(decays[:].rearrange("p s h -> p (s h)"), seg_ps[:, 0:3 * NH],
                                       ACT.Exp).then_inc(sums_exp, 1)
                        for q in range(4):
                            act.wait_ge(seg_made, START + 4 * n + q + 1)
                            act.wait_ge(in_made, START + n)
                            act.activation(mixm[:, q].rearrange("p h t -> p (h t)"), seg_ps[:], ACT.Exp).then_inc(seg_exp, 1)

            @block.vector
            def _(dve):
                with dve.Fori(0, NT // 2) as i:
                    for j in range(2):
                        n = 2 * i + j
                        dve.wait_ge(btok_kept, START + n + 1)
                        dve.wait_ge(mix_made, START + 4 * n)
                        dve.tensor_tensor(cb[:], misc_ps[:, 2 * P:4 * P].rearrange("p (g t) -> p g t", g=2),
                                          kit.c(C_UPPER, P).unsqueeze(1).broadcast_to([P, 2, P]),
                                          ALU.mult).then_inc(cb_masked, 1)
                        dve.wait_ge(off_made, START + n + 1)
                        dve.wait_ge(sums_exp, START + n + 1)
                        dve.wait_ge(y_turned, START + n)
                        dve.tensor_tensor(heads(y[:]), heads(off_ps[:]), per_head(decays[:, 0, :]),
                                          ALU.mult).then_inc(y_scaled, 1)
                        dve.wait_ge(cb_masked, START + n + 1)
                        for q in range(4):
                            dve.wait_ge(seg_exp, START + 4 * n + q + 1)
                            dve.tensor_tensor(mixm[:, q], mixm[:, q], cb[:, q // 2, :].unsqueeze(1).broadcast_to([P, 4, P]),
                                              ALU.mult).then_inc(mix_made, 1)
                        dve.wait_ge(state_made, START + n + 1)
                        dve.wait_ge(state_decayed, START + n + 1)
                        dve.tensor_tensor(state[:], state[:], off_ps[:], ALU.add).then_inc(state_summed, 1)
                        dve.wait_ge(in_made, START + n + 1)
                        dve.wait_ge(y_scaled, START + n + 1)
                        dve.tensor_tensor(y[:], y[:], in_ps[:], ALU.add).then_inc(y_summed, 1)
                        dve.wait_ge(y_turned, START + n + 1)
                        dve.wait_ge(skip_made, START + n + 1)
                        dve.wait_ge(stored[j], START + 16 * i)
                        yt = yT[:, j].rearrange("p f t -> p (f t)")
                        dve.tensor_tensor(yt, turn_ps[:], skipped[:].rearrange("p f t -> p (f t)"),
                                          ALU.add).then_inc(y_skipped, 1)
                        dve.wait_ge(y_skipped, START + n + 1)
                        dve.tensor_tensor(yt, yt, zT[:, j].rearrange("p f t -> p (f t)"), ALU.mult).then_inc(gated[j], 1)

        with nc.Block() as block:
            @block.gpsimd
            def _(pool):
                kit.prime(pool)

            @block.sync
            def _(sp):
                sp.dma_start(dram["ssm_p"], state[:]).then_inc(state_stored, 16)
                sp.wait_ge(state_stored, START + 16)


def scan_sample(kit, neg_a, skip):
    nc, dram = kit.nc, kit.dram
    with ExitStack() as mem:
        def sb(n, s, d=F32):
            return mem.enter_context(nc.sbuf_tensor(n, s, d))

        def ps(n, w):
            return mem.enter_context(nc.psum_tensor(n, [P, w], F32))

        xbc, zT, dt = sb("ss_xbc", [P, XBC_TILES, NS]), sb("ss_z", [P, KD, NS]), sb("ss_dt", [NS, NH])
        dta, decays = sb("ss_dta", [NS, NH]), sb("ss_decays", [NS, 2, NH])
        x_tok, xdt, xw = sb("ss_x", [NS, D]), sb("ss_xdt", [NS, D]), sb("ss_xw", [NS, D])
        b_tok, cb = sb("ss_btok", [NS, 2 * P]), sb("ss_cb", [NS, 2, NS])
        steps, mixm = sb("ss_steps", [NS, NH, NS]), sb("ss_m", [NS, NH, NS])
        y, yT, skipped = sb("ss_y", [NS, D]), sb("ss_yT", [P, KD, NS]), sb("ss_skip", [P, KD, NS])
        off_sum = sb("ss_offsum", [NS, D])
        state, total = sb("ss_state", [P, 2, D]), sb("ss_total", [P, 2, NH])
        c_own, b_own, row_own = sb("ss_cown", [P, 2, 2, NS]), sb("ss_bown", [NS, 2, 2 * P]), sb("ss_rown", [NS, 2, P])
        turn_ps, misc_ps, seg_ps = ps("ss_turn", D), ps("ss_misc", 512), ps("ss_seg", 512)
        in_ps, off_ps = ps("ss_in", D), ps("ss_off", D)

        loaded, state_loaded = kit.sems("ss_loaded"), kit.sems("ss_stloaded", 2)
        (dta_made, x_turned, bc_made, sums_made, kept, cb_masked, steps_made, seg_made, seg_exp, mix_made, xdt_made,
         xw_made, in_made, in_kept, zeroed) = (kit.sems(f"ss_{n}") for n in (
             "dta_done", "xturned", "bc", "sums", "kept", "cbm", "stepsd", "segd", "sege", "mixd", "xdtd", "xwd",
             "ind", "ink", "zero"))
        owned, off_made, off_summed, state_made, total_exp, decayed, updated, state_stored = (
            kit.sems(f"ss_{n}", 2) for n in ("owned", "offd", "offs", "std", "totd", "dec", "upd", "sts"))
        finish = kit.sems("ss_finish")
        y_turned, stored = kit.sems("ss_yturned"), kit.sems("ss_stored")

        def heads(ap):
            return ap.rearrange("p (h c) -> p h c", h=NH)

        def per_head(ap, rows, w=HD):
            return ap.unsqueeze(2).broadcast_to([rows, NH, w])

        with nc.Block() as block:
            @block.gpsimd
            def _(pool):
                kit.prime(pool)

            @block.sync
            def _(sp):
                sp.dma_start(xbc[:], dram["xbc"][:, SEQ:NTOK].rearrange("(f p) t -> p f t", p=P)).then_inc(loaded, 16)
                sp.dma_start(zT[:], dram["z"][:, SEQ:NTOK].rearrange("(f p) t -> p f t", p=P)).then_inc(loaded, 16)
                sp.dma_start(dt[:], dram["dt"][SEQ:NTOK, :]).then_inc(loaded, 16)
                with sp.Fori(0, NB_DEC // 2) as i:
                    for j in range(2):
                        sp.wait_ge(state_stored[j], START + 16 * i)
                        sp.dma_start(state[:, j, :], dram["state_in"][bass.ds(2 * i + j, 1)]
                                     .rearrange("o n c -> n (o c)")).then_inc(state_loaded[j], 16)

            @block.tensor
            def _(pe):
                pe.wait_ge(loaded, START + 48)
                for f in range(KD):
                    mm = pe.transpose(turn_ps[0:NS, f * P:(f + 1) * P], xbc[:, f, :], kit.c(C_IDENT, P))
                mm.then_inc(x_turned, 1)
                for g in range(2):
                    pe.transpose(misc_ps[0:NS, g * P:(g + 1) * P], xbc[:, KD + g, :], kit.c(C_IDENT, P))
                for g in range(2):
                    mm = pe.matmul(misc_ps[0:NS, 2 * P + g * NS:2 * P + (g + 1) * NS], xbc[:, KD + g, :],
                                   xbc[:, KD + 2 + g, :], start=True, stop=True)
                mm.then_inc(bc_made, 1)
                pe.wait_ge(dta_made, START + 1)
                for s, m in enumerate((C_UPPER_S, C_LOWER_S)):
                    mm = pe.matmul(seg_ps[0:NS, s * NH:(s + 1) * NH], kit.c(m, NS, NS), dta[:], start=True, stop=True)
                mm.then_inc(sums_made, 1)
                pe.wait_ge(steps_made, START + 1)
                pe.wait_ge(kept, START + 3)
                pe.matmul(seg_ps[0:NS, :], kit.c(C_LOWER_S, NS, NS), steps[:].rearrange("p h t -> p (h t)"),
                          start=True, stop=True).then_inc(seg_made, 1)
                pe.wait_ge(mix_made, START + 1)
                pe.wait_ge(xdt_made, START + 1)
                for h in range(NH):
                    mm = pe.matmul(in_ps[0:NS, h * HD:(h + 1) * HD], mixm[:, h, :], xdt[:, h * HD:(h + 1) * HD],
                                   start=True, stop=True)
                mm.then_inc(in_made, 1)
                pe.wait_ge(in_kept, START + 1)
                pe.wait_ge(xw_made, START + 1)
                with pe.Fori(0, NB_DEC // 2) as i:
                    for j in range(2):
                        pe.wait_ge(state_loaded[j], START + 16 * (i + 1))
                        pe.wait_ge(owned[j], START + i + 1)
                        if j:
                            pe.wait_ge(off_summed[0], START + i + 1)
                        else:
                            pe.wait_ge(off_summed[1], START + i)
                        for g in range(2):
                            mm = pe.matmul(off_ps[0:NS, g * 512:(g + 1) * 512], c_own[:, j, g, :],
                                           state[:, j, g * 512:(g + 1) * 512], start=True, stop=True)
                        mm.then_inc(off_made[j], 1)
                        if j:
                            pe.wait_ge(updated[0], START + i + 1)
                        else:
                            pe.wait_ge(updated[1], START + i)
                        pe.matmul(misc_ps[:, 0:NH], row_own[:, j, :], dta[:], start=True, stop=True)
                        for g in range(2):
                            mm = pe.matmul(in_ps[:, g * 512:(g + 1) * 512], b_own[:, j, g * P:(g + 1) * P],
                                           xw[:, g * 512:(g + 1) * 512], start=True, stop=True)
                        mm.then_inc(state_made[j], 1)
                pe.wait_ge(finish, START + 3)
                for f in range(KD):
                    mm = pe.transpose(turn_ps[:, f * NS:(f + 1) * NS], y[:, f * P:(f + 1) * P], kit.c(C_IDENT, NS, NS))
                mm.then_inc(y_turned, 1)

            @block.scalar
            def _(act):
                act.wait_ge(x_turned, START + 1)
                act.activation(x_tok[:], turn_ps[0:NS, :], ACT.Copy).then_inc(kept, 1)
                act.wait_ge(bc_made, START + 1)
                act.activation(b_tok[:], misc_ps[0:NS, 0:2 * P], ACT.Copy).then_inc(kept, 1)
                act.wait_ge(sums_made, START + 1)
                act.activation(decays[:].rearrange("p s h -> p (s h)"), seg_ps[0:NS, 0:2 * NH], ACT.Exp).then_inc(kept, 1)
                act.wait_ge(seg_made, START + 1)
                act.activation(mixm[:].rearrange("p h t -> p (h t)"), seg_ps[0:NS, :], ACT.Exp).then_inc(seg_exp, 1)
                with act.Fori(0, NB_DEC // 2) as i:
                    for j in range(2):
                        act.wait_ge(state_made[j], START + i + 1)
                        act.wait_ge(updated[j], START + i)
                        act.activation(total[:, j, :], misc_ps[:, 0:NH], ACT.Exp).then_inc(total_exp[j], 1)
                        act.wait_ge(updated[j], START + i + 1)
                        act.dma_start(dram["ssm_s"][bass.ds(2 * i + j, 1)].rearrange("o n c -> n (o c)"),
                                      state[:, j, :]).then_inc(state_stored[j], 16)
                for j in range(2):
                    act.wait_ge(state_stored[j], START + 16 * (NB_DEC // 2))
                act.wait_ge(finish, START + 5)
                act.dma_start(dram["mix"][D:2 * D, SEQ:NTOK].rearrange("(f p) t -> p f t", p=P), yT[:]).then_inc(stored, 16)
                act.wait_ge(stored, START + 16)

            @block.vector
            def _(dve):
                dve.memset(off_sum[:], 0.0).then_inc(zeroed, 1)
                dve.wait_ge(loaded, START + 48)
                dve.tensor_tensor(dta[:], dt[:], neg_a[0:NS, :], ALU.mult).then_inc(dta_made, 1)
                dve.wait_ge(dta_made, START + 1)
                dve.tensor_tensor(steps[:], kit.c(C_UPPER_S, NS, NS).unsqueeze(1).broadcast_to([NS, NH, NS]),
                                  per_head(dta[:], NS, NS), ALU.mult).then_inc(steps_made, 1)
                dve.wait_ge(kept, START + 3)
                dve.tensor_tensor(heads(xdt[:]), heads(x_tok[:]), per_head(dt[:], NS), ALU.mult).then_inc(xdt_made, 1)
                dve.wait_ge(xdt_made, START + 1)
                dve.tensor_tensor(heads(xw[:]), heads(xdt[:]), per_head(decays[:, 1, :], NS), ALU.mult).then_inc(xw_made, 1)
                dve.tensor_tensor(cb[:], misc_ps[0:NS, 2 * P:2 * P + 2 * NS].rearrange("p (g t) -> p g t", g=2),
                                  kit.c(C_UPPER_S, NS, NS).unsqueeze(1).broadcast_to([NS, 2, NS]),
                                  ALU.mult).then_inc(cb_masked, 1)
                dve.wait_ge(cb_masked, START + 1)
                dve.wait_ge(seg_exp, START + 1)
                for g in range(2):
                    last = dve.tensor_tensor(mixm[:, g * NH // 2:(g + 1) * NH // 2, :], mixm[:, g * NH // 2:(g + 1) * NH // 2, :],
                                             cb[:, g, :].unsqueeze(1).broadcast_to([NS, NH // 2, NS]), ALU.mult)
                last.then_inc(mix_made, 1)
                dve.wait_ge(in_made, START + 1)
                dve.tensor_copy(y[:], in_ps[0:NS, :]).then_inc(in_kept, 1)
                dve.tensor_tensor(skipped[:], xbc[:, 0:KD, :], skip[:].unsqueeze(2).broadcast_to([P, KD, NS]),
                                  ALU.mult)
                dve.wait_ge(zeroed, START + 1)
                with dve.Fori(0, NB_DEC // 2) as i:
                    for j in range(2):
                        b = 2 * i + j
                        dve.wait_ge(state_made[j], START + i)
                        dve.tensor_tensor(c_own[:, j], xbc[:, KD + 2:KD + 4, :],
                                          kit.const[:, bass.ds(b * NS + C_BMASK, NS)].unsqueeze(1).broadcast_to([P, 2, NS]),
                                          ALU.mult)
                        own = kit.const[0:NS, bass.ds(b + C_BROW, 1)]
                        dve.tensor_tensor(b_own[:, j, :], b_tok[:], own.broadcast_to([NS, 2 * P]), ALU.mult)
                        dve.tensor_tensor(row_own[:, j, :], kit.c(C_ONES, P, NS), own.broadcast_to([NS, P]),
                                          ALU.mult).then_inc(owned[j], 1)
                        dve.wait_ge(off_made[j], START + i + 1)
                        if j:
                            dve.wait_ge(off_summed[0], START + i + 1)
                        else:
                            dve.wait_ge(off_summed[1], START + i)
                        dve.tensor_tensor(off_sum[:], off_sum[:], off_ps[0:NS, :], ALU.add).then_inc(off_summed[j], 1)
                        dve.wait_ge(total_exp[j], START + i + 1)
                        dve.tensor_tensor(heads(state[:, j, :]), heads(state[:, j, :]), per_head(total[:, j, :], P),
                                          ALU.mult).then_inc(decayed[j], 1)
                        dve.wait_ge(decayed[j], START + i + 1)
                        dve.tensor_tensor(state[:, j, :], state[:, j, :], in_ps[:], ALU.add).then_inc(updated[j], 1)
                dve.wait_ge(off_summed[1], START + NB_DEC // 2)
                dve.tensor_tensor(heads(off_sum[:]), heads(off_sum[:]), per_head(decays[:, 0, :], NS), ALU.mult).then_inc(finish, 1)
                dve.wait_ge(finish, START + 1)
                dve.tensor_tensor(y[:], y[:], off_sum[:], ALU.add).then_inc(finish, 2)
                dve.wait_ge(y_turned, START + 1)
                dve.tensor_tensor(yT[:].rearrange("p f t -> p (f t)"), turn_ps[:, 0:KD * NS],
                                  skipped[:].rearrange("p f t -> p (f t)"), ALU.add).then_inc(finish, 1)
                dve.wait_ge(finish, START + 4)
                dve.tensor_tensor(yT[:], yT[:], zT[:], ALU.mult).then_inc(finish, 1)


def out_project(kit, h, gain):
    nc, dram = kit.nc, kit.dram
    KM = 2 * KD
    with ExitStack() as mem:
        def sb(n, s, d=F32):
            return mem.enter_context(nc.sbuf_tensor(n, s, d))

        m_hi, m_lo = sb("mix_hi", [P, KM, NTOK], F32R), sb("mix_lo", [P, KM, NTOK], F32R)
        eps = sb("mix_eps", [P, 1])
        loaded, hi_made, split = (kit.sems(f"mix_{n}", 2) for n in ("loaded", "hi", "split"))
        squared, summed = kit.sems("mix_squared", 2), kit.sems("mix_summed", 2)
        rooted, inverted = kit.sems("mix_rooted"), kit.sems("mix_inverted")
        reloaded, scaled = kit.sems("mix_reloaded", 2), kit.sems("mix_scaled", 2)
        eps_set, hi2, split2 = kit.sems("mix_eps"), kit.sems("mix_hi2", 2), kit.sems("mix_split2", 2)
        with ExitStack() as tmp:
            sq, raw, rinv = (tmp.enter_context(nc.sbuf_tensor(f"mix_{n}", [P, 2, NTOK], F32))
                             for n in ("sq", "raw", "rinv"))
            acc = [tmp.enter_context(nc.psum_tensor(f"mix_ps{g}", [P, 3 * 512], F32)) for g in range(2)]
            with nc.Block() as block:
                @block.gpsimd
                def _(pool):
                    kit.prime(pool)

                @block.sync
                def _(sp):
                    for k in range(KD):
                        if k >= 2:
                            sp.wait_ge(squared[k % 2], START + k // 2)
                        sp.dma_start(raw[:, k % 2, :], dram["mix"][D + k * P:D + (k + 1) * P, :]).then_inc(loaded[k % 2], 16)
                    for k in range(KM):
                        if k < 2:
                            sp.wait_ge(squared[k % 2], START + KD // 2)
                        else:
                            sp.wait_ge(split[k % 2], START + k // 2)
                        sp.dma_start(raw[:, k % 2, :], dram["mix"][k * P:(k + 1) * P, :]).then_inc(reloaded[k % 2], 16)

                @block.scalar
                def _(act):
                    for k in range(KD):
                        act.wait_ge(loaded[k % 2], START + 16 * (k // 2 + 1))
                        if k >= 2:
                            act.wait_ge(summed[k % 2], START + k // 2)
                        act.activation(sq[:, k % 2, :], raw[:, k % 2, :], ACT.Square).then_inc(squared[k % 2], 1)
                    act.wait_ge(eps_set, START + 1)
                    act.wait_ge(summed[0], START + KD // 2)
                    act.wait_ge(summed[1], START + KD // 2)
                    for g in range(2):
                        last = act.activation(grouped(rinv[:, g, :]), in_banks(acc[g]), ACT.Sqrt, bias=eps[:], scale=2.0 / D)
                    last.then_inc(rooted, 1)
                    for k in range(KM):
                        act.wait_ge(reloaded[k % 2], START + 16 * (k // 2 + 1))
                        if k >= KD:
                            act.wait_ge(scaled[k % 2], START + (k - KD) // 2 + 1)
                        act.activation(m_hi[:, k, :], raw[:, k % 2, :], ACT.Copy).then_inc(hi_made[k % 2], 1)

                @block.tensor
                def _(pe):
                    for k in range(KD):
                        g = k // (KD // 2)
                        pe.wait_ge(squared[k % 2], START + k // 2 + 1)
                        for c, w in GROUPS:
                            mm = pe.matmul(bank(acc[g], c, w), kit.c(C_ONES, P), sq[:, k % 2, c:c + w],
                                           start=(k % (KD // 2) == 0), stop=(k % (KD // 2) == KD // 2 - 1))
                        mm.then_inc(summed[k % 2], 1)

                @block.vector
                def _(dve):
                    dve.memset(eps[:], EPS).then_inc(eps_set, 1)
                    dve.wait_ge(rooted, START + 1)
                    dve.reciprocal(rinv[:], rinv[:]).then_inc(inverted, 1)
                    dve.wait_ge(inverted, START + 1)
                    for k in range(KM):
                        if k >= KD:
                            dve.wait_ge(reloaded[k % 2], START + 16 * (k // 2 + 1))
                            dve.scalar_tensor_tensor(out=raw[:, k % 2, :], in0=raw[:, k % 2, :],
                                                     scalar=gain[:, k - KD:k - KD + 1],
                                                     in1=rinv[:, (k - KD) // (KD // 2), :],
                                                     op0=ALU.mult, op1=ALU.mult).then_inc(scaled[k % 2], 1)
                        dve.wait_ge(hi_made[k % 2], START + k // 2 + 1)
                        dve.tensor_tensor(m_lo[:, k, :], raw[:, k % 2, :], m_hi[:, k, :].bitcast(F32),
                                          ALU.subtract).then_inc(split[k % 2], 1)
                    dve.wait_ge(split[1], START + KM // 2)

        with ExitStack() as tmp:
            w_raw = tmp.enter_context(nc.sbuf_tensor("wo_raw", [P, 2, KM // 2 * P], F32))
            w_hi = tmp.enter_context(nc.sbuf_tensor("wo_hi", [P, 2, KM // 2, P], F32R))
            w_lo = tmp.enter_context(nc.sbuf_tensor("wo_lo", [P, 2, KM // 2, P], F32R))
            acc = [tmp.enter_context(nc.psum_tensor(f"wo_ps{g}", [P, 3 * 512], F32)) for g in range(2)]
            w_loaded, w_hi_made, w_split, w_used = (kit.sems(f"wo_{n}", 2) for n in ("loaded", "hi", "split", "used"))
            made, added, x_loaded = kit.sems("wo_made", 2), kit.sems("wo_added", 2), kit.sems("wo_x")
            with nc.Block() as block:
                @block.sync
                def _(sp):
                    sp.dma_start(h[:], dram["x"].rearrange("(f p) t -> p f t", p=P)).then_inc(x_loaded, 16)
                    with sp.Fori(0, KD) as i:
                        for s in range(2):
                            sp.wait_ge(w_split[s], START + i)
                            sp.dma_start(w_raw[:, s, :], dram["w_out"][bass.ds(i, 1), :, s * D:(s + 1) * D]
                                         .rearrange("o p c -> p (o c)")).then_inc(w_loaded[s], 16)

                @block.gpsimd
                def _(pool):
                    kit.prime(pool)
                    with pool.Fori(0, KD) as i:
                        for s in range(2):
                            pool.wait_ge(w_loaded[s], START + 16 * (i + 1))
                            pool.wait_ge(w_used[s], START + i)
                            raw_w = w_raw[:, s, :].rearrange("p (k m) -> p k m", m=P)
                            kit.settle(pool)
                            pool.tensor_copy(w_hi[:, s], raw_w).then_inc(w_hi_made[s], 1)
                            pool.wait_ge(w_hi_made[s], START + i + 1)
                            pool.tensor_tensor(w_lo[:, s], raw_w, w_hi[:, s].bitcast(F32), ALU.subtract).then_inc(w_split[s], 1)

                @block.tensor
                def _(pe):
                    with pe.Fori(0, KD // 2) as i:
                        for j in range(2):
                            pe.wait_ge(added[j], START + i)
                            for s in range(2):
                                pe.wait_ge(w_split[s], START + 2 * i + j + 1)
                                for kk in range(KM // 2):
                                    k = s * (KM // 2) + kk
                                    for wt, xt in ((w_hi, m_hi), (w_hi, m_lo), (w_lo, m_hi)):
                                        for c, w in GROUPS:
                                            mm = pe.matmul(bank(acc[j], c, w), wt[:, s, kk, :], xt[:, k, c:c + w],
                                                           start=(k == 0 and wt is w_hi and xt is m_hi),
                                                           stop=(k == KM - 1 and wt is w_lo))
                                if s == 0:
                                    mm.then_inc(w_used[0], 1)
                            mm.then_inc(made[j], 1)

                @block.vector
                def _(dve):
                    dve.wait_ge(x_loaded, START + 16)
                    with dve.Fori(0, KD // 2) as i:
                        for j in range(2):
                            row = h[:, bass.ds(2 * i + j, 1), :].rearrange("p o t -> p (o t)")
                            dve.wait_ge(made[j], START + i + 1)
                            dve.sem_inc(w_used[1], 1)
                            dve.tensor_tensor(grouped(row), grouped(row), in_banks(acc[j]), ALU.add).then_inc(added[j], 1)
                    for j in range(2):
                        dve.wait_ge(added[j], START + KD // 2)


def feed_forward(kit, h, x_hi, x_lo):
    nc, dram = kit.nc, kit.dram
    with ExitStack() as mem:
        def sb(n, s, d=F32):
            return mem.enter_context(nc.sbuf_tensor(n, s, d))

        w_raw, w_hi, w_lo = sb("wf_raw", [P, 2, D]), sb("wf_hi", [P, 2, KD, P], F32R), sb("wf_lo", [P, 2, KD, P], F32R)
        r_hi, r_lo = sb("r_hi", [P, FT, NTOK], F32R), sb("r_lo", [P, FT, NTOK], F32R)
        relu, r_sq = sb("relu", [P, 2, NTOK]), sb("r_sq", [P, 2, NTOK])
        acc = [mem.enter_context(nc.psum_tensor(f"ff_ps{j}", [P, 3 * 512], F32)) for j in range(2)]
        w_loaded, w_hi_made, w_split = (kit.sems(f"wf_{n}", 2) for n in ("loaded", "hi", "split"))
        w_used = kit.sems("wf_used", 2)
        up_made, relued, squared, hi_made, split = (kit.sems(f"ff_{n}", 2) for n in ("up", "relu", "sq", "hi", "split"))
        down_made, added = kit.sems("ff_down", 2), kit.sems("ff_added", 2)
        stored = kit.sems("ff_stored")
        UN = 2 * FT // 2

        with nc.Block() as block:
            @block.sync
            def _(sp):
                with sp.Fori(0, NFC) as i:
                    for n in range(2 * FT):
                        j = n % 2
                        sp.wait_ge(w_split[j], START + UN * i + n // 2)
                        src = dram["w_up"] if n < FT else dram["w_down"]
                        sp.dma_start(w_raw[:, j, :], src[bass.ds(FT * i + n % FT, 1)]
                                     .rearrange("o p c -> p (o c)")).then_inc(w_loaded[j], 16)

            @block.gpsimd
            def _(pool):
                kit.prime(pool)
                with pool.Fori(0, NFC) as i:
                    for n in range(2 * FT):
                        j = n % 2
                        pool.wait_ge(w_loaded[j], START + (UN * i + n // 2 + 1) * 16)
                        pool.wait_ge(w_used[j], START + UN * i + n // 2)
                        raw_w = w_raw[:, j, :].rearrange("p (k m) -> p k m", m=P)
                        kit.settle(pool)
                        pool.tensor_copy(w_hi[:, j], raw_w).then_inc(w_hi_made[j], 1)
                        pool.wait_ge(w_hi_made[j], START + UN * i + n // 2 + 1)
                        pool.tensor_tensor(w_lo[:, j], raw_w, w_hi[:, j].bitcast(F32),
                                           ALU.subtract).then_inc(w_split[j], 1)

            @block.tensor
            def _(pe):
                with pe.Fori(0, NFC) as i:
                    for f in range(FT):
                        j = f % 2
                        pe.wait_ge(w_split[j], START + UN * i + f // 2 + 1)
                        if f < 2:
                            pe.wait_ge(added[j], START + KD // 2 * i)
                        else:
                            pe.wait_ge(squared[j], START + FT // 2 * i + f // 2)
                        for k in range(KD):
                            for wt, xt in ((w_hi, x_hi), (w_hi, x_lo), (w_lo, x_hi)):
                                for c, w in GROUPS:
                                    mm = pe.matmul(bank(acc[j], c, w), wt[:, j, k, :], xt[:, k, c:c + w],
                                                   start=(k == 0 and wt is w_hi and xt is x_hi),
                                                   stop=(k == KD - 1 and wt is w_lo))
                        mm.then_inc(up_made[j], 1)
                    for o in range(KD):
                        j, n = o % 2, FT + o // 2
                        s = n % 2
                        if o % 2 == 0:
                            pe.wait_ge(w_split[s], START + UN * i + n // 2 + 1)
                        if o < 2:
                            pe.wait_ge(squared[j], START + FT // 2 * (i + 1))
                        else:
                            pe.wait_ge(added[j], START + KD // 2 * i + o // 2)
                        for k in range(FT):
                            if o == 0:
                                pe.wait_ge(split[k % 2], START + FT // 2 * i + k // 2 + 1)
                            for wt, xt in ((w_hi, r_hi), (w_hi, r_lo), (w_lo, r_hi)):
                                for c, w in GROUPS:
                                    mm = pe.matmul(bank(acc[j], c, w), wt[:, s, (o % 2) * FT + k, :], xt[:, k, c:c + w],
                                                   start=(k == 0 and wt is w_hi and xt is r_hi),
                                                   stop=(k == FT - 1 and wt is w_lo))
                        mm.then_inc(down_made[j], 1)

            @block.scalar
            def _(act):
                with act.Fori(0, NFC) as i:
                    for f in range(FT):
                        j = f % 2
                        u = FT // 2 * i + f // 2
                        act.wait_ge(up_made[j], START + u + 1)
                        act.wait_ge(squared[j], START + u)
                        act.activation(grouped(relu[:, j, :]), in_banks(acc[j]), ACT.Relu).then_inc(relued[j], 1)
                        act.wait_ge(squared[j], START + u + 1)
                        act.wait_ge(down_made[0], START + KD // 2 * i)
                        act.wait_ge(down_made[1], START + KD // 2 * i)
                        act.activation(r_hi[:, f, :], r_sq[:, j, :], ACT.Copy).then_inc(hi_made[j], 1)
                        act.sem_inc(w_used[j], 1)
                    for o in range(KD):
                        j = o % 2
                        act.wait_ge(down_made[j], START + KD // 2 * i + o // 2 + 1)
                        if o % 2 == 1:
                            act.sem_inc(w_used[(o // 2) % 2], 1)

            @block.vector
            def _(dve):
                with dve.Fori(0, NFC) as i:
                    for f in range(FT):
                        j = f % 2
                        u = FT // 2 * i + f // 2
                        dve.wait_ge(relued[j], START + u + 1)
                        dve.wait_ge(split[j], START + u)
                        dve.tensor_tensor(r_sq[:, j, :], relu[:, j, :], relu[:, j, :], ALU.mult).then_inc(squared[j], 1)
                        dve.wait_ge(hi_made[j], START + u + 1)
                        dve.tensor_tensor(r_lo[:, f, :], r_sq[:, j, :], r_hi[:, f, :].bitcast(F32),
                                          ALU.subtract).then_inc(split[j], 1)
                    for o in range(KD):
                        j = o % 2
                        dve.wait_ge(down_made[j], START + KD // 2 * i + o // 2 + 1)
                        if o >= 2:
                            dve.wait_ge(added[j], START + KD // 2 * i + o // 2)
                        dve.tensor_tensor(grouped(h[:, o, :]), grouped(h[:, o, :]), in_banks(acc[j]), ALU.add).then_inc(added[j], 1)
                for j in range(2):
                    dve.wait_ge(added[j], START + KD // 2 * NFC)

        with nc.Block() as block:
            @block.gpsimd
            def _(pool):
                kit.prime(pool)

            @block.sync
            def _(sp):
                sp.dma_start(dram["y"].rearrange("(f p) t -> p f t", p=P), h[:]).then_inc(stored, 16)
                sp.wait_ge(stored, START + 16)


def prepare_parameters(kit, small, neg_a):
    nc, dram = kit.nc, kit.dram
    loaded, made = kit.sems("param_loaded"), kit.sems("param_made")
    with nc.Block() as block:
        @block.gpsimd
        def _(pool):
            kit.prime(pool)

        @block.sync
        def _(sp):
            sp.dma_start(small[:], dram["params"]).then_inc(loaded, 16)
            sp.dma_start(neg_a[:], dram["a_log"].partition_broadcast(P)).then_inc(loaded, 16)

        @block.scalar
        def _(act):
            act.wait_ge(loaded, START + 32)
            act.activation(neg_a[:], neg_a[:], ACT.Exp).then_inc(made, 1)

        @block.vector
        def _(dve):
            dve.wait_ge(made, START + 1)
            dve.tensor_scalar(neg_a[:], neg_a[:], -1.0, None, ALU.mult).then_inc(made, 1)
            dve.tensor_scalar(small[:, PAR_Q:PAR_Q + KD], small[:, PAR_Q:PAR_Q + KD], HD ** -0.5, None,
                              ALU.mult).then_inc(made, 1)
            dve.wait_ge(made, START + 3)


PAR_MIX, PAR_Q, PAR_K, PAR_FFN, PAR_SSM, PAR_SKIP = (KD * n for n in range(6))
PAR_END = 6 * KD


def build(nc, dram):
    with ExitStack() as stack:
        kit = Kit(nc, stack, dram)
        small = stack.enter_context(nc.sbuf_tensor("params", [P, PAR_END], F32))
        neg_a = stack.enter_context(nc.sbuf_tensor("neg_a", [P, NH], F32))
        skip = small[:, PAR_SKIP:PAR_SKIP + KD]
        with kit.part(), ExitStack() as mem:
            load_constants(kit)
            prepare_parameters(kit, small, neg_a)
            distance_table(kit)
            x_hi = mem.enter_context(nc.sbuf_tensor("u_hi", [P, KD, NPAD], F32R))
            x_lo = mem.enter_context(nc.sbuf_tensor("u_lo", [P, KD, NPAD], F32R))
            with ExitStack() as tmp:
                x = tmp.enter_context(nc.sbuf_tensor("x", [P, KD, NTOK], F32))
                loads = [[(x[:, k, :], dram["x"][k * P:(k + 1) * P, :])] for k in range(KD)]
                rms_split(kit, "mixnorm", x, loads, small[:, PAR_MIX:PAR_MIX + KD], x_hi, x_lo)
            project(kit, x_hi, x_lo, small[:, PAR_Q:PAR_Q + QK_TILES])
            project_tokens(kit, x_hi, x_lo)
        with kit.part():
            attend_prompt(kit)
            attend_sample(kit)
        with kit.part():
            scan_prompt(kit, neg_a, skip)
            scan_sample(kit, neg_a, skip)
        with kit.part(), ExitStack() as mem:
            h = mem.enter_context(nc.sbuf_tensor("h", [P, KD, NTOK], F32))
            out_project(kit, h, small[:, PAR_SSM:PAR_SSM + KD])
            x_hi = mem.enter_context(nc.sbuf_tensor("uf_hi", [P, KD, NTOK], F32R))
            x_lo = mem.enter_context(nc.sbuf_tensor("uf_lo", [P, KD, NTOK], F32R))
            rms_split(kit, "ffnnorm", h, [], small[:, PAR_FFN:PAR_FFN + KD], x_hi, x_lo)
            feed_forward(kit, h, x_hi, x_lo)


def tiles(w, rows_of_tile, cols_of_tile):
    k, n = w.shape
    t = w.reshape(k // rows_of_tile, rows_of_tile, n // cols_of_tile, cols_of_tile)
    return np.ascontiguousarray(t.transpose(2, 1, 0, 3)).reshape(n // cols_of_tile, rows_of_tile, -1)


def by_tile(v):
    return v.reshape(-1, P).T


def lay_out(a):
    f = {k: np.asarray(v) for k, v in a.items()}
    w_in = f["w_in"][0]
    q, k, v, z, xbc, dt = np.split(w_in, [D, 2 * D, 3 * D, 4 * D, 4 * D + XBC], axis=1)
    w_tok = np.concatenate([v, dt], axis=1).reshape(KD, P, D + NH)
    w_down = f["w_down"][0].reshape(NFC, FT, P, KD // 2, 2, P)
    def reach(cache):
        c = cache[0].reshape(NB_DEC, PAST, D)
        far = c.reshape(NB_DEC, PAST // 16, 16, D)[:, :FAR // 4, :4].reshape(NB_DEC, FAR, D)
        return np.concatenate([far, c[:, PAST - DENSE:]], axis=1)
    ck, cv = reach(f["cache_attn_k"]), reach(f["cache_attn_v"])
    taps = np.concatenate([f["conv_w"][0], f["conv_b"]], axis=0)
    params = np.concatenate([by_tile(f["norm_mix"][0]),
                             by_tile(np.tile(f["q_norm"][0], NH)), by_tile(np.tile(f["k_norm"][0], NH)),
                             by_tile(f["norm_ffn"][0]), by_tile(f["ssm_norm"][0]),
                             by_tile(np.repeat(f["d_skip"][0], HD))], axis=1)
    x = np.concatenate([f["x_prompt"][0], f["x_sample"].reshape(NS, D)], axis=0)
    out = {
        "x": x.T,
        "w_feat": tiles(np.concatenate([q, k, xbc, z], axis=1), P, P),
        "w_tok": w_tok,
        "conv_taps": taps.reshape(WIDTH + 1, XBC_TILES, P).transpose(2, 1, 0),
        "conv_past": f["state_conv"][0].reshape(NB_DEC * (WIDTH - 1), XBC_TILES, P).transpose(2, 1, 0),
        "dt_bias": f["dt_bias"].reshape(NH), "a_log": f["a_log"].reshape(NH), "rel_bias": f["rel_bias"],
        "params": params,
        "cache_k": ck.reshape(NB_DEC, FAR + DENSE, NPAIR, P).transpose(0, 3, 2, 1).reshape(NB_DEC, P, -1),
        "cache_v": cv.reshape(NB_DEC, VT, P, D).transpose(0, 2, 1, 3).reshape(NB_DEC, P, -1),
        "state_in": f["state_ssm"][0].reshape(NB_DEC, D, NSTATE).transpose(0, 2, 1),
        "w_out": tiles(f["w_out"][0], P, P),
        "w_up": tiles(f["w_up"][0], P, P),
        "w_down": w_down.transpose(0, 3, 2, 4, 1, 5).reshape(NFC * KD // 2, P, 2 * FT * P),
        "consts": shape_constants(), "onehot": distance_constants(),
    }
    return {n: np.ascontiguousarray(v) for n, v in out.items()}


_OUTS = {"y": (D, NTOK), "qk": (2 * D, NTOK), "v": (NPAD, D), "conv_tail": (P, XBC_TILES * 27),
         "ssm_p": (NSTATE, D), "ssm_s": (NB_DEC, NSTATE, D)}
_SCRATCH = {"xbc": (XBC, NTOK), "z": (D, NTOK), "dt": (NPAD, NH), "mix": (2 * D, NTOK), "table": (NH, LLEN), "bias_rows": (NH * P, SEQ),
            "bias_sample": (NH * T_DEC, NKEY)}


def kernel(**inputs):
    import concourse.bacc as bacc
    from concourse.bass_utils import run_bass_kernel_spmd

    nc = bacc.Bacc("TRN2", target_bir_lowering=False, num_devices=1)
    arrays, dram = {}, {}
    for name, a in lay_out(inputs).items():
        arrays[f"in_{name}"] = a
        dram[name] = nc.dram_tensor(f"in_{name}", a.shape, F32, kind="ExternalInput").ap()
    for name, shape in _OUTS.items():
        dram[name] = nc.dram_tensor(f"out_{name}", shape, F32, kind="ExternalOutput").ap()
    for name, shape in _SCRATCH.items():
        dram[name] = nc.dram_tensor(f"tmp_{name}", shape, F32).ap()
    build(nc, dram)
    r = run_bass_kernel_spmd(nc, [arrays], core_ids=[0]).results[0]
    y, qk, v, tail = r["out_y"], r["out_qk"], r["out_v"], r["out_conv_tail"]
    k = np.ascontiguousarray(qk[D:].T)
    conv = tail.reshape(P, XBC_TILES, (NB_DEC + 1) * (WIDTH - 1)).transpose(2, 1, 0).reshape(NB_DEC + 1, WIDTH - 1, XBC)
    outs = (
        y[:, :SEQ].T.reshape(1, SEQ, D),
        y[:, SEQ:].T.reshape(NB_DEC, T_DEC, D),
        k[:SEQ].reshape(1, 1, SEQ, NH, HD),
        v[:SEQ].reshape(1, 1, SEQ, NH, HD),
        conv[0].reshape(1, 1, WIDTH - 1, XBC),
        r["out_ssm_p"].T.reshape(1, 1, NH, HD, NSTATE),
        k[SEQ:].reshape(1, NB_DEC, T_DEC, NH, HD),
        v[SEQ:NTOK].reshape(1, NB_DEC, T_DEC, NH, HD),
        conv[1:].reshape(1, NB_DEC, WIDTH - 1, XBC),
        r["out_ssm_s"].transpose(0, 2, 1).reshape(1, NB_DEC, NH, HD, NSTATE),
    )
    return tuple(np.ascontiguousarray(o) for o in outs)
```

```python
import math
from contextlib import ExitStack, contextmanager

import numpy as np
import concourse.bass as bass
from concourse import mybir
from concourse.alu_op_type import AluOpType as ALU

ACT = mybir.ActivationFunctionType
F32 = mybir.dt.float32
F32R = mybir.dt.float32r
AX = mybir.AxisListType.X

P = 128
D = 1024
KD = D // P
SEQ = 1024
NT = SEQ // P
NB_DEC, T_DEC = 8, 4
NS = NB_DEC * T_DEC
NTOK = SEQ + NS
NPAD = SEQ + P
PAST = 1024
HD = 64
NH = D // HD
NPAIR = NH // 2
XBC = 1536
NSTATE = 128
WIDTH = 4
DFF = 4 * D
EPS = 1e-6
QK_TILES, XBC_TILES, Z_TILES = 2 * KD, XBC // P, KD
START = 1
NEG = -1e30
BRANCHES = ((128, 1), (512, 4), (2048, 16))
NBUCKET = 32
LMAX = PAST + T_DEC - 1
LLEN = LMAX + P
FAR = P
DENSE = 512
NKEY = FAR + DENSE + T_DEC
VT = (FAR + DENSE) // P
NG = 3
TG = NTOK // NG
GROUPS = tuple((g * TG, TG) for g in range(NG))
FC = 512
FT = FC // P
NFC = DFF // FC

C_IDENT, C_UPPER, C_LOWER, C_ONES, C_HEADONE = 0, P, 2 * P, 3 * P, 4 * P
C_UPPER_S, C_LOWER_S = 5 * P, 5 * P + NS
C_BMASK = C_LOWER_S + NS
C_BROW = C_BMASK + NB_DEC * NS
C_DIAG = C_BROW + NB_DEC
C_SEL = C_DIAG + D
C_END = C_SEL + T_DEC


def shape_constants():
    c = np.zeros((P, C_END), np.float32)
    r = np.arange(P)
    c[:, C_IDENT:C_IDENT + P] = np.eye(P)
    c[:, C_UPPER:C_UPPER + P] = r[:, None] <= r[None, :]
    c[:, C_LOWER:C_LOWER + P] = r[:, None] > r[None, :]
    c[:, C_ONES:C_ONES + P] = 1.0
    c[:, C_HEADONE:C_HEADONE + P] = r[:, None] // HD == r[None, :] // HD
    s = np.arange(NS)
    same = s[:, None] // T_DEC == s[None, :] // T_DEC
    c[:NS, C_UPPER_S:C_UPPER_S + NS] = same & (s[:, None] <= s[None, :])
    c[:NS, C_LOWER_S:C_LOWER_S + NS] = same & (s[:, None] > s[None, :])
    for b in range(NB_DEC):
        c[:, C_BMASK + b * NS:C_BMASK + (b + 1) * NS] = (s // T_DEC == b)[None, :]
        c[:NS, C_BROW + b] = s // T_DEC == b
    ht = r % (NH * T_DEC)
    c[:, C_DIAG:C_DIAG + D] = ht[:, None] // T_DEC == np.arange(D)[None, :] // HD
    c[:, C_SEL:C_SEL + T_DEC] = ht[:, None] % T_DEC == np.arange(T_DEC)[None, :]
    return c


def distance_constants():
    dist = LMAX - np.arange(LLEN)
    exact = NBUCKET // 2
    df = np.maximum(dist, 1).astype(np.float32)
    top = max(w for w, _ in BRANCHES)
    large = exact + (np.log(df / np.float32(exact)) / np.float32(math.log(top / exact))
                     * np.float32(NBUCKET - exact)).astype(np.int32)
    bucket = np.where(dist < exact, np.maximum(dist, 0), np.minimum(large, NBUCKET - 1))
    out = np.zeros((NBUCKET + 1, LLEN), np.float32)
    out[bucket, np.arange(LLEN)] = 1.0
    count = sum(((dist >= 0) & (dist <= w) & (dist % d == 0)).astype(np.int32) for w, d in BRANCHES)
    out[NBUCKET] = np.where(count > 0, np.log(np.maximum(count, 1)), NEG)
    return out


class Kit:

    def __init__(self, nc, stack, dram):
        self.nc, self.stack = nc, stack
        self.dram = dram
        self.const = stack.enter_context(nc.sbuf_tensor("const", [P, C_END], F32))
        self.part_stack, self.unprimed = None, []
        self.const_loaded = self.sems("const_loaded")
        self.skewed = self.sems("bias_skewed")

    def sems(self, name, n=1):
        made = [(self.part_stack or self.stack).enter_context(self.nc.semaphore(f"{name}{i}")) for i in range(n)]
        if self.part_stack:
            self.part_sems += made
            self.unprimed += made
        return made if n > 1 else made[0]

    @contextmanager
    def part(self):
        with ExitStack() as self.part_stack:
            self.part_sems = []
            names = ("tensor", "vector", "gpsimd")
            engines = (self.nc.tensor, self.nc.vector, self.nc.gpsimd)
            self.settled = {e.engine: self.sems(f"settled_{n}") for n, e in zip(names, engines)}
            yield
            used = self.part_sems
            with self.nc.Block() as block:
                @block.gpsimd
                def _(pool):
                    for sem in used:
                        pool.sem_clear(sem)
        self.part_stack, self.unprimed = None, []

    def prime(self, pool):
        for sem in self.unprimed:
            pool.sem_inc(sem, START)
        self.unprimed = []

    def settle(self, eng):
        eng.sem_inc(self.settled[eng.engine], 1)

    def c(self, start, width, rows=P):
        return self.const[0:rows, start:start + width]


def bank(acc, c, w):
    return acc[:, c // TG * 512:c // TG * 512 + w]


def in_banks(acc):
    return acc[:].rearrange("p (g c) -> p g c", g=NG)[:, :, 0:TG]


def grouped(ap):
    return ap.rearrange("p (g c) -> p g c", g=NG)


def load_constants(kit, x, x_loaded):
    nc = kit.nc
    primed = kit.sems("primed")
    with nc.Block() as block:
        @block.gpsimd
        def _(pool):
            kit.prime(pool)
            pool.sem_inc(primed, 1)

        @block.sync
        def _(sp):
            sp.dma_start(kit.const[:], kit.dram["consts"]).then_inc(kit.const_loaded, 16)
            sp.wait_ge(kit.const_loaded, 16)

        @block.scalar
        def _(act):
            act.wait_ge(primed, START + 1)
            for k in range(KD):
                act.dma_start(x[:, k, :], kit.dram["x"][k * P:(k + 1) * P, :]).then_inc(x_loaded[k], 16)


def distance_table(kit):
    nc, dram = kit.nc, kit.dram
    with ExitStack() as mem:
        onehot = mem.enter_context(nc.sbuf_tensor("onehot", [NBUCKET + 1, LLEN], F32))
        bias = mem.enter_context(nc.sbuf_tensor("bias_aug", [NBUCKET + 1, NH], F32))
        table = mem.enter_context(nc.sbuf_tensor("table", [NH, LLEN], F32))
        acc = mem.enter_context(nc.psum_tensor("table_ps", [P, 3 * 512], F32))
        loaded, made, copied, stored = (kit.sems(f"dist_{n}") for n in ("loaded", "made", "copied", "stored"))
        ones_set = kit.sems("dist_ones")
        with nc.Block() as block:
            @block.gpsimd
            def _(pool):
                kit.prime(pool)

            @block.sync
            def _(sp):
                sp.dma_start(onehot[:], dram["onehot"]).then_inc(loaded, 16)
                sp.dma_start(bias[0:NBUCKET, :], dram["rel_bias"]).then_inc(loaded, 16)
                sp.wait_ge(copied, START + 1)
                sp.dma_start(dram["table"], table[:]).then_inc(stored, 16)
                sp.wait_ge(stored, START + 16)

            @block.vector
            def _(dve):
                dve.memset(bias[NBUCKET:NBUCKET + 1, :], 1.0).then_inc(ones_set, 1)

            @block.tensor
            def _(pe):
                pe.wait_ge(loaded, START + 32)
                pe.wait_ge(ones_set, START + 1)
                for c in range(0, LLEN, 512):
                    w = min(512, LLEN - c)
                    mm = pe.matmul(acc[0:NH, c:c + w], bias[:], onehot[:, c:c + w], start=True, stop=True)
                mm.then_inc(made, 1)

            @block.scalar
            def _(act):
                act.wait_ge(made, START + 1)
                act.activation(table[:], acc[0:NH, 0:LLEN], ACT.Copy).then_inc(copied, 1)


def skew_rows(kit, eng, half):
    dram = kit.dram
    heads = NH // 2
    eng.dma_start(dram["bias_rows"][half * heads * P:(half + 1) * heads * P, :].rearrange("(h p) c -> h p c", h=heads),
                  bass.AP(dram["table"].tensor, half * heads * LLEN + LMAX - (NT - 1) * P,
                          [[LLEN, heads], [-1, P], [1, SEQ]])).then_inc(kit.skewed, 16)


def skew_sample(kit, eng):
    dram = kit.dram
    table_of, rows = dram["table"].tensor, dram["bias_sample"].rearrange("(h t) c -> h t c", h=NH)
    for t in range(T_DEC):
        eng.dma_start(rows[:, t, 0:FAR].rearrange("h (g r) -> h g r", r=4),
                      bass.AP(table_of, LMAX - PAST - t, [[LLEN, NH], [16, FAR // 4], [1, 4]])
                      ).then_inc(kit.skewed, 16)
        eng.dma_start(rows[:, t, FAR:NKEY],
                      bass.AP(table_of, LMAX - DENSE - t, [[LLEN, NH], [1, DENSE + T_DEC]])
                      ).then_inc(kit.skewed, 16)


class RmsSplit:

    def __init__(self, kit, mem, name, x, loaded, gain, x_hi, x_lo, sq, u, acc):
        self.kit, self.x, self.loaded, self.gain = kit, x, loaded, gain
        self.x_hi, self.x_lo, self.sq, self.u, self.acc = x_hi, x_lo, sq, u, acc
        self.rinv = mem.enter_context(kit.nc.sbuf_tensor(f"{name}_rinv", [P, NTOK], F32))
        self.eps = mem.enter_context(kit.nc.sbuf_tensor(f"{name}_eps", [P, 1], F32))
        self.squared, self.summed = kit.sems(f"{name}_squared", 2), kit.sems(f"{name}_summed", 2)
        self.rooted, self.inverted = kit.sems(f"{name}_rooted"), kit.sems(f"{name}_inverted")
        self.scaled, self.hi_made, self.lo_made = (kit.sems(f"{name}_{n}", 2) for n in ("scaled", "hi", "lo"))
        self.eps_set = kit.sems(f"{name}_eps")

    def scalar(self, act):
        for k in range(KD):
            if self.loaded:
                act.wait_ge(self.loaded[k], START + 16)
            if k >= 2:
                act.wait_ge(self.summed[k % 2], START + k // 2)
            act.activation(self.sq[:, k % 2, :], self.x[:, k, :], ACT.Square).then_inc(self.squared[k % 2], 1)
        act.wait_ge(self.summed[(KD - 1) % 2], START + KD // 2)
        act.wait_ge(self.eps_set, START + 1)
        act.activation(grouped(self.rinv[:]), in_banks(self.acc), ACT.Sqrt, bias=self.eps[:],
                       scale=1.0 / D).then_inc(self.rooted, 1)
        for k in range(KD):
            act.wait_ge(self.scaled[k % 2], START + k // 2 + 1)
            act.activation(self.x_hi[:, k, 0:NTOK], self.u[:, k % 2, :], ACT.Copy).then_inc(self.hi_made[k % 2], 1)

    def tensor(self, pe):
        for k in range(KD):
            pe.wait_ge(self.squared[k % 2], START + k // 2 + 1)
            for c, w in GROUPS:
                mm = pe.matmul(bank(self.acc, c, w), self.kit.c(C_ONES, P), self.sq[:, k % 2, c:c + w],
                               start=(k == 0), stop=(k == KD - 1))
            mm.then_inc(self.summed[k % 2], 1)

    def wait_tile(self, pe, k):
        pe.wait_ge(self.lo_made[k % 2], START + k // 2 + 1)

    def vector(self, dve):
        def scale(k):
            if k >= 2:
                dve.wait_ge(self.lo_made[k % 2], START + k // 2)
            dve.scalar_tensor_tensor(out=self.u[:, k % 2, :], in0=self.x[:, k, :], scalar=self.gain[:, k:k + 1],
                                     in1=self.rinv[:], op0=ALU.mult, op1=ALU.mult).then_inc(self.scaled[k % 2], 1)

        dve.memset(self.eps[:], EPS).then_inc(self.eps_set, 1)
        dve.wait_ge(self.rooted, START + 1)
        dve.reciprocal(self.rinv[:], self.rinv[:]).then_inc(self.inverted, 1)
        dve.wait_ge(self.inverted, START + 1)
        scale(0)
        for k in range(KD):
            if k + 1 < KD:
                scale(k + 1)
            dve.wait_ge(self.hi_made[k % 2], START + k // 2 + 1)
            dve.tensor_tensor(self.x_lo[:, k, 0:NTOK], self.u[:, k % 2, :], self.x_hi[:, k, 0:NTOK].bitcast(F32),
                              ALU.subtract).then_inc(self.lo_made[k % 2], 1)
        dve.wait_ge(self.lo_made[(KD - 1) % 2], START + KD // 2)


def project(kit, x, x_loaded, gain_x, x_hi, x_lo, gains):
    nc, dram = kit.nc, kit.dram
    NQ, NX, NZ = QK_TILES, XBC_TILES, Z_TILES
    with ExitStack() as mem:
        def sb(n, s, d=F32):
            return mem.enter_context(nc.sbuf_tensor(n, s, d))

        w_raw, w_hi, w_lo = sb("w_raw", [P, 2, D]), sb("w_hi", [P, 2, KD, P], F32R), sb("w_lo", [P, 2, KD, P], F32R)
        out = sb("proj_out", [P, 2, NTOK])
        raw, sq, rinv = sb("proj_raw", [P, 2, NTOK]), sb("proj_sq", [P, 2, NTOK]), sb("proj_rinv", [P, 2, NTOK])
        pre = sb("conv_pre", [P, 2, WIDTH - 1 + SEQ])
        pre_s = sb("conv_pre_s", [P, 2, NB_DEC, WIDTH - 1 + T_DEC])
        past_s = sb("conv_past", [P, XBC_TILES, NB_DEC * (WIDTH - 1)])
        taps = sb("conv_taps", [P, XBC_TILES, WIDTH + 1])
        tap = sb("conv_tap", [P, 2, WIDTH + 1])
        tail = sb("conv_tail", [P, XBC_TILES, (NB_DEC + 1) * (WIDTH - 1)])
        gain = sb("qk_gain", [P, 2, 1])
        eps = sb("qk_eps", [P, 1])
        acc = [mem.enter_context(nc.psum_tensor(f"proj_ps{j}", [P, 3 * 512], F32)) for j in range(2)]
        ssq = [mem.enter_context(nc.psum_tensor(f"proj_ss{j}", [P, 512], F32)) for j in range(2)]
        norm = RmsSplit(kit, mem, "mixnorm", x, x_loaded, gain_x, x_hi, x_lo, sq, raw, acc[1])

        w_loaded, w_hi_made, w_split = (kit.sems(f"w_{n}", 2) for n in ("loaded", "hi", "split"))
        made, freed = kit.sems("proj_made", 2), kit.sems("proj_freed", 2)
        squared = kit.sems("qk_squared", 2)
        summed, rooted = kit.sems("qk_summed", 2), kit.sems("qk_rooted", 2)
        inverted, normed = kit.sems("qk_inverted", 2), kit.sems("qk_normed", 2)
        gained = kit.sems("qk_gained", 2)
        stored = kit.sems("proj_stored", 2)
        small = kit.sems("proj_small")
        zeroed = kit.sems("proj_zeroed")
        tapped, padded, conv, activated = (kit.sems(f"conv_{n}", 2) for n in ("tapped", "padded", "mac", "silu"))
        tails, tail_stored = kit.sems("conv_tails", 2), kit.sems("tail_stored")
        z_silu = kit.sems("z_silu", 2)

        def tile_range(kind):
            return {"qk": (0, NQ // 2), "xbc": (NQ // 2, NX // 2), "z": ((NQ + NX) // 2, NZ // 2)}[kind]

        with nc.Block() as block:
            @block.sync
            def _(sp):
                sp.dma_start(taps[:], dram["conv_taps"]).then_inc(small, 16)
                sp.dma_start(past_s[:], dram["conv_past"]).then_inc(small, 16)
                with sp.Fori(0, (NQ + NX + NZ) // 2) as i:
                    for j in range(2):
                        sp.wait_ge(w_split[j], START + i)
                        sp.dma_start(w_raw[:, j, :], dram["w_feat"][bass.ds(2 * i + j, 1)]
                                     .rearrange("o p c -> p (o c)")).then_inc(w_loaded[j], 16)

            @block.gpsimd
            def _(pool):
                kit.prime(pool)
                with pool.Fori(0, (NQ + NX + NZ) // 2) as i:
                    for j in range(2):
                        pool.wait_ge(w_loaded[j], START + 16 * (i + 1))
                        pool.wait_ge(made[j], START + i)
                        raw_w = w_raw[:, j, :].rearrange("p (k m) -> p k m", k=KD)
                        kit.settle(pool)
                        pool.tensor_copy(w_hi[:, j], raw_w).then_inc(w_hi_made[j], 1)
                        pool.wait_ge(w_hi_made[j], START + i + 1)
                        pool.tensor_tensor(w_lo[:, j], raw_w, w_hi[:, j].bitcast(F32),
                                           ALU.subtract).then_inc(w_split[j], 1)

            @block.tensor
            def _(pe):
                norm.tensor(pe)

                def main(n, j, beside=(), first=False):
                    pe.wait_ge(w_split[j], START + n + 1)
                    pe.wait_ge(freed[j], START + n)
                    for k in range(KD):
                        if first:
                            norm.wait_tile(pe, k)
                        for wt, xt in ((w_hi, x_hi), (w_hi, x_lo), (w_lo, x_hi)):
                            for c, w in GROUPS:
                                mm = pe.matmul(bank(acc[j], c, w), wt[:, j, k, :], xt[:, k, c:c + w],
                                               start=(k == 0 and wt is w_hi and xt is x_hi),
                                               stop=(k == KD - 1 and wt is w_lo))
                        if beside and k in (1, 3):
                            head_sums(*beside, (0, 1) if k == 1 else (2,))
                    mm.then_inc(made[j], 1)

                def head_sums(n, j, groups):
                    pe.wait_ge(squared[j], START + n + 1)
                    for g in groups:
                        c, w = GROUPS[g]
                        s = g % 2
                        if s == 0:
                            pe.wait_ge(rooted[0], START + 2 * (2 * n + j) + g // 2)
                        else:
                            pe.wait_ge(rooted[1], START + 2 * n + j)
                        pe.matmul(ssq[s][:, 0:w], kit.c(C_HEADONE, P), sq[:, j, c:c + w],
                                  start=True, stop=True).then_inc(summed[s], 1)

                main(0, 0, first=True)
                with pe.Fori(0, NQ // 2 - 1) as i:
                    main(i, 1, (i, 0))
                    main(i + 1, 0, (i, 1))
                main(NQ // 2 - 1, 1, (NQ // 2 - 1, 0))
                main(NQ // 2, 0, (NQ // 2 - 1, 1))
                main(NQ // 2, 1)
                with pe.Fori(NQ // 2 + 1, (NQ + NX + NZ) // 2) as i:
                    main(i, 0)
                    main(i, 1)

            @block.scalar
            def _(act):
                norm.scalar(act)
                act.wait_ge(zeroed, START + 4)

                def copy(i, j):
                    act.wait_ge(made[j], START + i + 1)
                    act.wait_ge(normed[j], START + i)
                    act.wait_ge(norm.lo_made[j], START + KD // 2)
                    act.activation(grouped(raw[:, j, :]), in_banks(acc[j]), ACT.Copy)
                    act.activation(grouped(sq[:, j, :]), in_banks(acc[j]), ACT.Square).then_inc(squared[j], 1)
                    act.wait_ge(squared[j], START + i + 1)
                    act.sem_inc(freed[j], 1)

                def roots(i, j):
                    for g, (c, w) in enumerate(GROUPS):
                        s = g % 2
                        n = 2 * (2 * i + j) + g // 2 if s == 0 else 2 * i + j
                        act.wait_ge(summed[s], START + n + 1)
                        act.activation(rinv[:, j, c:c + w], ssq[s][:, 0:w], ACT.Sqrt, bias=eps[:],
                                       scale=1.0 / HD).then_inc(rooted[s], 1)

                def store(i, j):
                    act.wait_ge(normed[j], START + i + 1)
                    act.dma_start(dram["qk"][bass.ds((2 * i + j) * P, P), :], out[:, j, :]).then_inc(stored[j], 16)

                copy(0, 0)
                roots(0, 0)
                with act.Fori(0, NQ // 2 - 1) as i:
                    copy(i, 1)
                    store(i, 0)
                    roots(i, 1)
                    copy(i + 1, 0)
                    store(i, 1)
                    roots(i + 1, 0)
                copy(NQ // 2 - 1, 1)
                store(NQ // 2 - 1, 0)
                roots(NQ // 2 - 1, 1)
                store(NQ // 2 - 1, 1)
                skew_rows(kit, act, 0)

                base, pairs = tile_range("xbc")
                with act.Fori(0, pairs) as i:
                    for j in range(2):
                        act.wait_ge(made[j], START + i + base + 1)
                        act.wait_ge(conv[j], START + i * WIDTH)
                        act.wait_ge(tails[j], START + i)
                        full = SEQ // TG
                        act.activation(pre[:, j, WIDTH - 1:WIDTH - 1 + full * TG].rearrange("p (g c) -> p g c", g=full),
                                       in_banks(acc[j])[:, 0:full, :], ACT.Copy)
                        act.activation(pre[:, j, WIDTH - 1 + full * TG:], in_banks(acc[j])[:, full, 0:SEQ - full * TG],
                                       ACT.Copy)
                        act.activation(pre_s[:, j, :, WIDTH - 1:],
                                       in_banks(acc[j])[:, full, SEQ - full * TG:].rearrange("p (b t) -> p b t", b=NB_DEC),
                                       ACT.Copy).then_inc(padded[j], 1)
                        act.wait_ge(padded[j], START + i + 1)
                        act.sem_inc(freed[j], 1)
                        act.wait_ge(conv[j], START + (i + 1) * WIDTH)
                        act.activation(out[:, j, :], raw[:, j, :], ACT.Silu,
                                       bias=tap[:, j, WIDTH:WIDTH + 1]).then_inc(activated[j], 1)
                        act.wait_ge(activated[j], START + i + 1)
                        act.dma_start(dram["xbc"][bass.ds((2 * i + j) * P, P), :], out[:, j, :]).then_inc(stored[j], 16)

                skew_rows(kit, act, 1)
                skew_sample(kit, act)

                zbase, zpairs = tile_range("z")
                with act.Fori(0, zpairs) as i:
                    for j in range(2):
                        act.wait_ge(made[j], START + i + zbase + 1)
                        act.wait_ge(stored[j], START + 16 * (i + zbase))
                        act.activation(grouped(out[:, j, :]), in_banks(acc[j]), ACT.Silu).then_inc(z_silu[j], 1)
                        act.wait_ge(z_silu[j], START + i + 1)
                        act.sem_inc(freed[j], 1)
                        act.dma_start(dram["z"][bass.ds((2 * i + j) * P, P), :], out[:, j, :]).then_inc(stored[j], 16)
                for j in range(2):
                    act.wait_ge(stored[j], START + 16 * (NQ + NX + NZ) // 2)
                act.wait_ge(tails[0], START + NX // 2)
                act.wait_ge(tails[1], START + NX // 2)
                act.dma_start(dram["conv_tail"], tail[:].rearrange("p f c -> p (f c)")).then_inc(tail_stored, 16)
                act.wait_ge(tail_stored, START + 16)

            @block.vector
            def _(dve):
                dve.memset(eps[:], EPS).then_inc(zeroed, 1)
                dve.memset(pre[:, :, 0:WIDTH - 1], 0.0).then_inc(zeroed, 1)
                dve.memset(x_hi[:, :, NTOK:NPAD].bitcast(F32), 0.0).then_inc(zeroed, 1)
                dve.memset(x_lo[:, :, NTOK:NPAD].bitcast(F32), 0.0).then_inc(zeroed, 1)
                norm.vector(dve)
                dve.wait_ge(small, START + 32)
                with dve.Fori(0, NQ // 2) as i:
                    for j in range(2):
                        dve.wait_ge(normed[j], START + i)
                        dve.tensor_copy(gain[:, j, :], gains[:, bass.ds(2 * i + j, 1)]).then_inc(gained[j], 1)
                        dve.wait_ge(rooted[0], START + 2 * (2 * i + j) + 2)
                        dve.wait_ge(rooted[1], START + 2 * i + j + 1)
                        dve.reciprocal(rinv[:, j, :], rinv[:, j, :]).then_inc(inverted[j], 1)
                        dve.wait_ge(inverted[j], START + i + 1)
                        dve.wait_ge(gained[j], START + i + 1)
                        dve.wait_ge(stored[j], START + 16 * i)
                        dve.scalar_tensor_tensor(out=out[:, j, :], in0=raw[:, j, :], scalar=gain[:, j, :],
                                                 in1=rinv[:, j, :], op0=ALU.mult, op1=ALU.mult).then_inc(normed[j], 1)
                for j in range(2):
                    dve.wait_ge(normed[j], START + NQ // 2)
                base, pairs = tile_range("xbc")
                with dve.Fori(0, pairs) as i:
                    for j in range(2):
                        f = bass.ds(2 * i + j, 1)
                        dve.wait_ge(activated[j], START + i)
                        dve.tensor_copy(tap[:, j, :], taps[:, f, :].rearrange("p o t -> p (o t)"))
                        dve.tensor_copy(pre_s[:, j, :, 0:WIDTH - 1],
                                        past_s[:, f, :].rearrange("p o (b t) -> p (o b) t", b=NB_DEC)
                                        ).then_inc(tapped[j], 1)
                        dve.wait_ge(tapped[j], START + i + 1)
                        dve.wait_ge(padded[j], START + i + 1)
                        dve.wait_ge(stored[j], START + 16 * (i + base))
                        acc_p = raw[:, j, 0:SEQ]
                        acc_s = raw[:, j, SEQ:NTOK].rearrange("p (b t) -> p b t", b=NB_DEC)
                        for t in range(WIDTH):
                            w = tap[:, j, t:t + 1]
                            if t == 0:
                                dve.tensor_scalar(acc_p, pre[:, j, 0:SEQ], w, None, ALU.mult)
                                dve.tensor_scalar(acc_s, pre_s[:, j, :, 0:T_DEC], w, None,
                                                  ALU.mult).then_inc(conv[j], 1)
                            else:
                                dve.wait_ge(conv[j], START + i * WIDTH + t)
                                dve.scalar_tensor_tensor(out=acc_p, in0=pre[:, j, t:t + SEQ], scalar=w,
                                                         in1=acc_p, op0=ALU.mult, op1=ALU.add)
                                dve.scalar_tensor_tensor(out=acc_s, in0=pre_s[:, j, :, t:t + T_DEC], scalar=w,
                                                         in1=acc_s, op0=ALU.mult, op1=ALU.add).then_inc(conv[j], 1)
                        dve.tensor_copy(tail[:, f, 0:WIDTH - 1].rearrange("p o t -> p (o t)"),
                                        pre[:, j, SEQ:SEQ + WIDTH - 1])
                        dve.tensor_copy(tail[:, f, WIDTH - 1:].rearrange("p o (b t) -> p (o b) t", b=NB_DEC),
                                        pre_s[:, j, :, T_DEC:]).then_inc(tails[j], 1)


def project_tokens(kit, x_hi, x_lo):
    nc, dram = kit.nc, kit.dram
    NTT = NT + 1
    NV = D + NH
    with ExitStack() as mem:
        def sb(n, s, d=F32):
            return mem.enter_context(nc.sbuf_tensor(n, s, d))

        WS = 4
        w_raw = sb("wv_raw", [P, WS, NV])
        w_hi, w_lo = sb("wv_hi", [P, KD, NV], F32R), sb("wv_lo", [P, KD, NV], F32R)
        v_out = sb("v_out", [P, 2, D])
        dt_raw, dt_abs, dt_exp, dt_all = (sb(n, [P, NTT, NH]) for n in ("dt_raw", "dt_abs", "dt_exp", "dt_all"))
        bias = sb("dt_bias", [P, NH])
        acc = [mem.enter_context(nc.psum_tensor(f"v_ps{j}", [P, 3 * 512], F32)) for j in range(2)]
        w_loaded, w_hi_made, w_split = (kit.sems(f"wv_{n}", WS) for n in ("loaded", "hi", "split"))
        made, v_copied, dt_copied, stored = (kit.sems(f"v_{n}", 2) for n in ("made", "copied", "dt", "stored"))
        small, soft, dt_stored = kit.sems("dt_small"), kit.sems("dt_soft"), kit.sems("dt_stored")

        with nc.Block() as block:
            @block.sync
            def _(sp):
                sp.dma_start(bias[:], dram["dt_bias"].partition_broadcast(P)).then_inc(small, 16)
                for k in range(KD):
                    if k >= WS:
                        sp.wait_ge(w_split[k % WS], START + k // WS)
                    sp.dma_start(w_raw[:, k % WS, :], dram["w_tok"][k]).then_inc(w_loaded[k % WS], 16)

            @block.gpsimd
            def _(pool):
                kit.prime(pool)

            @block.tensor
            def _(pe):
                for t in range(NTT):
                    j = t % 2
                    if t >= 2:
                        pe.wait_ge(v_copied[j], START + t // 2)
                        pe.wait_ge(dt_copied[j], START + t // 2)
                    for k in range(KD):
                        if t == 0:
                            pe.wait_ge(w_split[k % WS], START + k // WS + 1)
                        tok = slice(t * P, (t + 1) * P)
                        for wt, xt in ((w_hi, x_hi), (w_lo, x_hi), (w_hi, x_lo)):
                            for c in range(0, NV, TG):
                                w = min(TG, NV - c)
                                mm = pe.matmul(bank(acc[j], c, w), xt[:, k, tok], wt[:, k, c:c + w],
                                               start=(k == 0 and wt is w_hi and xt is x_hi),
                                               stop=(k == KD - 1 and xt is x_lo))
                    mm.then_inc(made[j], 1)

            @block.scalar
            def _(act):
                for k in range(KD):
                    act.wait_ge(w_loaded[k % WS], START + 16 * (k // WS + 1))
                    act.activation(w_hi[:, k, :], w_raw[:, k % WS, :], ACT.Copy).then_inc(w_hi_made[k % WS], 1)
                for t in range(NTT):
                    j = t % 2
                    act.wait_ge(made[j], START + t // 2 + 1)
                    if t >= 2:
                        act.wait_ge(stored[j], START + 16 * (t // 2))
                    full = D // TG
                    act.activation(v_out[:, j, 0:full * TG].rearrange("p (g c) -> p g c", g=full),
                                   in_banks(acc[j])[:, 0:full, :], ACT.Copy)
                    act.activation(v_out[:, j, full * TG:], in_banks(acc[j])[:, full, 0:D - full * TG],
                                   ACT.Copy).then_inc(v_copied[j], 1)
                    act.wait_ge(v_copied[j], START + t // 2 + 1)
                    act.dma_start(dram["v"][t * P:(t + 1) * P, :], v_out[:, j, :]).then_inc(stored[j], 16)
                act.wait_ge(soft, START + 2)
                act.activation(dt_exp[:], dt_abs[:], ACT.Exp).then_inc(soft, 1)
                act.wait_ge(soft, START + 3)
                act.activation(dt_abs[:], dt_exp[:], ACT.Ln, bias=1.0).then_inc(soft, 1)
                act.wait_ge(soft, START + 5)
                act.dma_start(dram["dt"].rearrange("(t p) h -> p t h", p=P), dt_all[:]).then_inc(dt_stored, 16)
                act.wait_ge(dt_stored, START + 16)
                for j in range(2):
                    act.wait_ge(stored[j], START + 16 * ((NTT + 1 - j) // 2))

            @block.vector
            def _(dve):
                for k in range(KD):
                    dve.wait_ge(w_hi_made[k % WS], START + k // WS + 1)
                    dve.tensor_tensor(w_lo[:, k, :], w_raw[:, k % WS, :], w_hi[:, k, :].bitcast(F32),
                                      ALU.subtract).then_inc(w_split[k % WS], 1)
                dve.wait_ge(small, START + 16)
                for t in range(NTT):
                    j = t % 2
                    dve.wait_ge(v_copied[j], START + t // 2 + 1)
                    dve.tensor_tensor(dt_raw[:, t, :], bank(acc[j], D, TG)[:, D % TG:NV - D // TG * TG], bias[:],
                                      ALU.add).then_inc(dt_copied[j], 1)
                dve.wait_ge(dt_copied[0], START + (NTT + 1) // 2)
                dve.wait_ge(dt_copied[1], START + NTT // 2)
                dve.tensor_scalar(dt_all[:], dt_raw[:], -1.0, None, ALU.mult).then_inc(soft, 1)
                dve.wait_ge(soft, START + 1)
                dve.tensor_tensor(dt_abs[:], dt_all[:], dt_raw[:], ALU.min).then_inc(soft, 1)
                dve.wait_ge(soft, START + 4)
                dve.scalar_tensor_tensor(out=dt_all[:], in0=dt_raw[:], scalar=0.0, in1=dt_abs[:],
                                         op0=ALU.max, op1=ALU.add).then_inc(soft, 1)


def attend_prompt(kit):
    nc, dram = kit.nc, kit.dram
    SLOT_ITEMS = 2 * NT
    N = 2 * SLOT_ITEMS
    items = [(jp, (jp * NT + qt) * 2 + h, qt, h) for jp in range(2) for qt in range(NT) for h in range(2)]
    pieces, total = [], 0
    for _, _, qt, _ in items:
        row = [(total + n, b0, min(4, qt + 1 - b0)) for n, b0 in enumerate(range(0, qt + 1, 4))]
        total += len(row)
        pieces.append(row)
    SLOT_PIECES = total // 2
    LOADS = 8 + 1
    with ExitStack() as mem:
        def sb(n, s, d=F32):
            return mem.enter_context(nc.sbuf_tensor(n, s, d))

        q_raw, k_raw, v_raw = sb("att_q", [P, 2, 2, SEQ]), sb("att_k", [P, 2, 2, SEQ]), sb("att_v", [P, 2, NT, P])
        q_two = sb("att_q2", [P, 2, 2, SEQ], F32R)
        k_hi, k_lo = sb("att_khi", [P, 2, 2, SEQ], F32R), sb("att_klo", [P, 2, 2, SEQ], F32R)
        v_hi, v_lo = sb("att_vhi", [P, 2, NT, P], F32R), sb("att_vlo", [P, 2, NT, P], F32R)
        bias = sb("att_bias", [P, 2, 2, SEQ])
        logits, probs = sb("att_s", [P, 2, SEQ]), sb("att_p", [P, 2, SEQ])
        p_hi, p_lo = sb("att_pThi", [P, 2, NT, P], F32R), sb("att_pTlo", [P, 2, NT, P], F32R)
        top, neg, den, rden = (sb(f"att_{n}", [P, 2, 1]) for n in ("max", "negmax", "den", "rden"))
        oT = sb("att_oT", [P, 2, SEQ])
        s_ps = [mem.enter_context(nc.psum_tensor(f"att_s_ps{j}", [P, 1024], F32)) for j in range(2)]
        t_ps = [mem.enter_context(nc.psum_tensor(f"att_t_ps{j}", [P, 512], F32)) for j in range(2)]
        pv_ps = [mem.enter_context(nc.psum_tensor(f"att_pv_ps{j}", [P, 512], F32)) for j in range(2)]

        loaded, bias_loaded, stored, pair_done = (kit.sems(f"att_{n}", 2) for n in ("loaded", "bias", "stored", "pair"))
        cast, split, prepared = (kit.sems(f"att_{n}", 2) for n in ("cast", "split", "prepared"))
        scored, biased, negated, exped = (kit.sems(f"att_{n}", 2) for n in ("scored", "biased", "negated", "exped"))
        inverted, normed = kit.sems("att_inverted", 2), kit.sems("att_normed", 2)
        flipped, hi_kept, lo_kept = (kit.sems(f"att_{n}", 2) for n in ("flipped", "hi", "lo"))
        multiplied, o_kept = kit.sems("att_multiplied", 2), kit.sems("att_okept", 2)

        def nth(i, m):
            return SLOT_ITEMS * i + m // 2

        def nth_piece(i, pn):
            return SLOT_PIECES * i + pn // 2

        def steps(first, second, third):
            for n in range(-3, N + 1):
                yield tuple(k if 0 <= k < N else None for k in (n + first, n + second, n + third))

        with nc.Block() as block:
            @block.sync
            def _(sp):
                sp.wait_ge(kit.skewed, 16 * (2 + 2 * T_DEC))
                with sp.Fori(0, NPAIR // 2) as i:
                    for jp in range(2):
                        pair = 2 * i + jp
                        sp.wait_ge(prepared[jp], START + i)
                        for h in range(2):
                            for half in range(2):
                                rows = slice(half * HD, (half + 1) * HD)
                                sp.dma_start(q_raw[rows, jp, h, :], dram["qk"][bass.ds(pair * P + h * HD, HD), 0:SEQ]
                                             ).then_inc(loaded[jp], 16)
                                sp.dma_start(k_raw[rows, jp, h, :], dram["qk"][bass.ds(pair * P + (D + h * HD), HD), 0:SEQ]
                                             ).then_inc(loaded[jp], 16)
                        sp.dma_start(v_raw[:, jp], dram["v"][0:SEQ, bass.ds(pair * P, P)]
                                     .rearrange("(t p) c -> p t c", p=P)).then_inc(loaded[jp], 16)
                        sp.wait_ge(pair_done[jp], START + i)
                        for h in range(2):
                            sp.dma_start(bias[:, jp, h, :], dram["bias_rows"][bass.ds((2 * pair + h) * P, P), :]
                                         ).then_inc(bias_loaded[jp], 16)

            @block.gpsimd
            def _(pool):
                kit.prime(pool)
                with pool.Fori(0, NPAIR // 2) as i:
                    for jp in range(2):
                        pool.wait_ge(cast[jp], START + i + 1)
                        pool.tensor_tensor(k_lo[:, jp], k_raw[:, jp], k_hi[:, jp].bitcast(F32), ALU.subtract)
                        pool.tensor_tensor(v_lo[:, jp], v_raw[:, jp], v_hi[:, jp].bitcast(F32),
                                           ALU.subtract).then_inc(split[jp], 1)
                        pool.wait_ge(split[jp], START + i + 1)
                        low = q_two[HD:P, jp]
                        pool.tensor_tensor(low, q_raw[HD:P, jp], low.bitcast(F32), ALU.subtract).then_inc(prepared[jp], 1)
                        pool.wait_ge(prepared[jp], START + i + 1)

            @block.tensor
            def _(pe):
                def score(i, n):
                    jp, m, qt, h = items[n]
                    j = m % 2
                    if qt == 0 and h == 0:
                        pe.wait_ge(prepared[jp], START + i + 1)
                    pe.wait_ge(biased[j], START + nth(i, m))
                    for c in range(0, (qt + 1) * P, 512):
                        w = min(512, (qt + 1) * P - c)
                        q = q_two[:, jp, h, qt * P:(qt + 1) * P]
                        pe.matmul(s_ps[j][:, c:c + w], q, k_hi[:, jp, h, c:c + w], start=True, stop=False)
                        mm = pe.matmul(s_ps[j][:, c:c + w], q, k_lo[:, jp, h, c:c + w], start=False, stop=True)
                    mm.then_inc(scored[j], 1)

                def turn(i, n):
                    j = items[n][1] % 2
                    pe.wait_ge(normed[j], START + nth(i, items[n][1]) + 1)
                    for pn, b0, nb in pieces[n]:
                        s = pn % 2
                        pe.wait_ge(lo_kept[s], START + nth_piece(i, pn))
                        for b in range(nb):
                            mm = pe.transpose(t_ps[s][:, b * P:(b + 1) * P],
                                              probs[:, j, (b0 + b) * P:(b0 + b + 1) * P], kit.c(C_IDENT, P))
                        mm.then_inc(flipped[s], 1)

                def values(i, n):
                    jp, m, qt, h = items[n]
                    j = m % 2
                    pe.wait_ge(o_kept[j], START + nth(i, m))
                    cols = slice(h * HD, (h + 1) * HD)
                    for pn, b0, nb in pieces[n]:
                        pe.wait_ge(lo_kept[pn % 2], START + nth_piece(i, pn) + 1)
                        for b in range(b0, b0 + nb):
                            out = pv_ps[j][0:HD, 0:P]
                            pe.matmul(out, v_hi[:, jp, b, cols], p_hi[:, j, b, :], start=(b == 0), stop=False)
                            pe.matmul(out, v_hi[:, jp, b, cols], p_lo[:, j, b, :], start=False, stop=False)
                            mm = pe.matmul(out, v_lo[:, jp, b, cols], p_hi[:, j, b, :], start=False, stop=(b == qt))
                    mm.then_inc(multiplied[j], 1)

                with pe.Fori(0, NPAIR // 2) as i:
                    for sc, t, v in steps(3, 0, -1):
                        if sc is not None:
                            score(i, sc)
                        if t is not None:
                            turn(i, t)
                        if v is not None:
                            values(i, v)

            @block.vector
            def _(dve):
                def bias_max(i, n):
                    jp, m, qt, h = items[n]
                    j, w = m % 2, (qt + 1) * P
                    if qt == 0 and h == 0:
                        dve.wait_ge(bias_loaded[jp], START + 2 * 16 * (i + 1))
                    dve.wait_ge(scored[j], START + nth(i, m) + 1)
                    dve.wait_ge(exped[j], START + nth(i, m))
                    kit.settle(dve)
                    dve.tensor_tensor_reduce(out=logits[:, j, 0:w], in0=s_ps[j][:, 0:w],
                                             in1=bias[:, jp, h, SEQ - w:SEQ], scale=1.0, scalar=-3e38,
                                             op0=ALU.add, op1=ALU.max,
                                             accum_out=top[:, j, :]).then_inc(biased[j], 1)
                    dve.wait_ge(biased[j], START + nth(i, m) + 1)
                    dve.tensor_scalar(neg[:, j, :], top[:, j, :], -1.0, None, ALU.mult).then_inc(negated[j], 1)

                def normalise(i, n):
                    _, m, qt, _ = items[n]
                    j, w = m % 2, (qt + 1) * P
                    dve.wait_ge(exped[j], START + nth(i, m) + 1)
                    dve.reciprocal(rden[:, j, :], den[:, j, :]).then_inc(inverted[j], 1)
                    dve.wait_ge(inverted[j], START + nth(i, m) + 1)
                    dve.tensor_scalar(probs[:, j, 0:w], probs[:, j, 0:w], rden[:, j, :], None,
                                      ALU.mult).then_inc(normed[j], 1)

                def keep_low(i, n):
                    m = items[n][1]
                    j = m % 2
                    for pn, b0, nb in pieces[n]:
                        s = pn % 2
                        dve.wait_ge(hi_kept[s], START + nth_piece(i, pn) + 1)
                        dve.tensor_tensor(p_lo[:, j, b0:b0 + nb, :].rearrange("p b q -> p (b q)"), t_ps[s][:, 0:nb * P],
                                          p_hi[:, j, b0:b0 + nb, :].rearrange("p b q -> p (b q)").bitcast(F32),
                                          ALU.subtract).then_inc(lo_kept[s], 1)

                with dve.Fori(0, NPAIR // 2) as i:
                    for bm, nm, lo in steps(2, 1, 0):
                        if bm is not None:
                            bias_max(i, bm)
                        if nm is not None:
                            normalise(i, nm)
                        if lo is not None:
                            keep_low(i, lo)

            @block.scalar
            def _(act):
                def cast_part(i, jp, part):
                    if part == 0:
                        act.wait_ge(loaded[jp], START + LOADS * 16 * (i + 1))
                    if part < 2:
                        act.activation(k_hi[:, jp, part], k_raw[:, jp, part], ACT.Copy)
                    elif part == 2:
                        act.activation(v_hi[:, jp], v_raw[:, jp], ACT.Copy)
                    else:
                        h = part - 3
                        op = act.activation(q_two[:, jp, h], q_raw[:, jp, h], ACT.Copy)
                        if h == 1:
                            op.then_inc(cast[jp], 1)

                def exponent(i, n):
                    _, m, qt, _ = items[n]
                    j, w = m % 2, (qt + 1) * P
                    act.wait_ge(negated[j], START + nth(i, m) + 1)
                    if n >= 2:
                        for pn, _, _ in pieces[n - 2]:
                            act.wait_ge(flipped[pn % 2], START + nth_piece(i, pn) + 1)
                    else:
                        act.wait_ge(flipped[0], START + SLOT_PIECES * i)
                        act.wait_ge(flipped[1], START + SLOT_PIECES * i)
                    act.activation(probs[:, j, 0:w], logits[:, j, 0:w], ACT.Exp, bias=neg[:, j, :],
                                   accum_out=den[:, j, :]).then_inc(exped[j], 1)

                def keep_high(i, n):
                    m = items[n][1]
                    j = m % 2
                    for k, (pn, b0, nb) in enumerate(pieces[n]):
                        act.wait_ge(flipped[pn % 2], START + nth_piece(i, pn) + 1)
                        if k == 0:
                            act.wait_ge(multiplied[j], START + nth(i, m))
                        act.activation(p_hi[:, j, b0:b0 + nb, :].rearrange("p b q -> p (b q)"),
                                       t_ps[pn % 2][:, 0:nb * P], ACT.Copy).then_inc(hi_kept[pn % 2], 1)

                def keep_out(i, n):
                    jp, m, qt, h = items[n]
                    j = m % 2
                    act.wait_ge(multiplied[j], START + nth(i, m) + 1)
                    if qt == 0 and h == 0:
                        act.wait_ge(stored[jp], START + 16 * i)
                    act.activation(oT[h * HD:(h + 1) * HD, jp, qt * P:(qt + 1) * P], pv_ps[j][0:HD, 0:P],
                                   ACT.Copy).then_inc(o_kept[j], 1)
                    if qt == NT - 1 and h == 1:
                        act.wait_ge(o_kept[j], START + nth(i, m) + 1)
                        act.sem_inc(pair_done[jp], 1)
                        act.dma_start(dram["mix"][bass.ds((2 * i + jp) * P, P), 0:SEQ], oT[:, jp, :]).then_inc(stored[jp], 16)

                def body(i, last):
                    for n, (hi, ex, out) in enumerate(steps(0, 2, -1)):
                        if 4 <= n < 9:
                            cast_part(i, 1, n - 4)
                        if N // 2 + 4 <= n < N // 2 + 9 and not last:
                            cast_part(i + 1, 0, n - (N // 2 + 4))
                        if hi is not None:
                            keep_high(i, hi)
                        if ex is not None:
                            exponent(i, ex)
                        if out is not None:
                            keep_out(i, out)

                for part in range(5):
                    cast_part(0, 0, part)
                with act.Fori(0, NPAIR // 2 - 1) as i:
                    body(i, False)
                body(NPAIR // 2 - 1, True)
                for jp in range(2):
                    act.wait_ge(stored[jp], START + 16 * (NPAIR // 2))


def attend_sample(kit):
    nc, dram = kit.nc, kit.dram
    R = NH * T_DEC
    LAST = NB_DEC // 2 - 1
    VD = 2
    with ExitStack() as mem:
        def sb(n, s, d=F32):
            return mem.enter_context(nc.sbuf_tensor(n, s, d))

        kT = sb("sa_k", [P, 2, NPAIR, NKEY])
        v_raw = sb("sa_v", [P, 2, VT, D])
        v_hi, v_lo = sb("sa_vhi", [P, 2, VT, D], F32R), sb("sa_vlo", [P, VT, D], F32R)
        v_new = sb("sa_vnew", [T_DEC, 2, D])
        q_all, k_new = sb("sa_q", [P, NPAIR, NS]), sb("sa_knew", [P, NPAIR, NS])
        q_diag = sb("sa_qdiag", [P, 2, NPAIR, R])
        bias = sb("sa_bias", [R, NKEY])
        logits, probs = sb("sa_s", [R, NKEY]), sb("sa_p", [R, 2, NKEY])
        turned, turned_new = sb("sa_pT", [P, 2, VT, 2 * R], F32R), sb("sa_pTn", [T_DEC, 2, 2 * R])
        top, neg, den, rden = (sb(f"sa_{n}", [R, 2, 1]) for n in ("max", "negmax", "den", "rden"))
        own = sb("sa_own", [P, D])
        oT = sb("sa_oT", [P, KD, NS])
        s_ps = mem.enter_context(nc.psum_tensor("sa_s_ps", [P, 1024], F32))
        t_ps = mem.enter_context(nc.psum_tensor("sa_t_ps", [P, 512], F32))
        pv_ps = mem.enter_context(nc.psum_tensor("sa_pv_ps", [P, 1024], F32))
        o_ps = mem.enter_context(nc.psum_tensor("sa_o_ps", [P, 512], F32))

        k_loaded, v_loaded, placed = (kit.sems(f"sa_{n}", 2) for n in ("kloaded", "vloaded", "placed"))
        common, zeroed, placing = kit.sems("sa_common"), kit.sems("sa_zeroed"), kit.sems("sa_placing")
        v_cast, v_split_dve, v_split_pool = (kit.sems(f"sa_{n}", 2) for n in ("vcast", "vsplitd", "vsplitp"))
        scored, biased, negated, exped = (kit.sems(f"sa_{n}", 2) for n in ("scored", "biased", "negated", "exped"))
        inverted, normed = kit.sems("sa_inverted", 2), kit.sems("sa_normed", 2)
        flipped, hi_kept, lo_kept = (kit.sems(f"sa_{n}", 2) for n in ("flipped", "hi", "lo"))
        multiplied, owned, gathered, o_kept = (kit.sems(f"sa_{n}", 2) for n in
                                               ("multiplied", "owned", "gathered", "okept"))
        stored = kit.sems("sa_stored")

        def batches(eng, body):
            with eng.Fori(0, LAST) as i:
                for j in range(2):
                    body(i, j, False)
            for j in range(2):
                body(LAST, j, j == 1)

        def ahead(i, j):
            return (i + 1, 0) if j else (i, 1)

        def before(i, j):
            return (0, i + 1) if j else (1, i)

        with nc.Block() as block:
            @block.sync
            def _(sp):
                qk = dram["qk"].rearrange("(f p) t -> p f t", p=P)
                sp.dma_start(q_all[:], qk[:, 0:NPAIR, SEQ:NTOK]).then_inc(common, 16)
                sp.dma_start(k_new[:], qk[:, NPAIR:2 * NPAIR, SEQ:NTOK]).then_inc(common, 16)
                sp.dma_start(bias[:], dram["bias_sample"]).then_inc(common, 16)
                with sp.Fori(0, NB_DEC // 2) as i:
                    for j in range(2):
                        b = 2 * i + j
                        sp.wait_ge(scored[j], START + i)
                        sp.dma_start(kT[:, j, :, 0:FAR + DENSE], dram["cache_k"][bass.ds(b, 1)]
                                     .rearrange("o p (f t) -> p (o f) t", f=NPAIR)).then_inc(k_loaded[j], 16)
                        sp.wait_ge(v_split_dve[j], START + i)
                        sp.wait_ge(v_split_pool[j], START + i)
                        sp.dma_start(v_raw[:, j], dram["cache_v"][bass.ds(b, 1)]
                                     .rearrange("o p (t c) -> p (o t) c", t=VT)).then_inc(v_loaded[j], 16)
                        sp.wait_ge(multiplied[j], START + i)
                        sp.dma_start(v_new[:, j, :], dram["v"][bass.ds(b * T_DEC + SEQ, T_DEC), :]
                                     ).then_inc(v_loaded[j], 16)

            @block.gpsimd
            def _(pool):
                def place(i, j):
                    tok = bass.ds((2 * i + j) * T_DEC, T_DEC)
                    pool.wait_ge(scored[j], START + i)
                    pool.tensor_copy(kT[:, j, :, FAR + DENSE:], k_new[:, :, tok]).then_inc(placing, 1)
                    for h in range(2):
                        pool.wait_ge(placing, START + 2 * (2 * i + j) + h + 1)
                        rows = q_diag[h * HD:(h + 1) * HD, j]
                        cols = bass.AP(rows.tensor, rows.offset + h * T_DEC,
                                       [list(rows.ap[0]), [R + 2 * T_DEC, NPAIR], [1, T_DEC]])
                        pool.tensor_copy(cols, q_all[h * HD:(h + 1) * HD, :, tok]).then_inc(
                            placed[j] if h else placing, 1)
                    pool.wait_ge(placed[j], START + i + 1)

                def split(i, j):
                    pool.wait_ge(v_cast[j], START + i + 1)
                    s, n = before(i, j)
                    pool.wait_ge(multiplied[s], START + n)
                    pool.tensor_tensor(v_lo[:, VD:VT, :], v_raw[:, j, VD:VT, :], v_hi[:, j, VD:VT, :].bitcast(F32),
                                       ALU.subtract).then_inc(v_split_pool[j], 1)

                kit.prime(pool)
                pool.memset(turned_new[:], 0.0).then_inc(zeroed, 1)
                pool.wait_ge(zeroed, START + 1)
                pool.memset(q_diag[:], 0.0).then_inc(zeroed, 1)
                pool.wait_ge(zeroed, START + 2)
                pool.wait_ge(common, START + 48)
                for j in range(2):
                    place(0, j)
                with pool.Fori(0, LAST) as i:
                    for j in range(2):
                        split(i, j)
                        place(i + 1, j)
                for j in range(2):
                    split(LAST, j)

            @block.tensor
            def _(pe):
                def score(i, j):
                    pe.wait_ge(k_loaded[j], START + 16 * (i + 1))
                    pe.wait_ge(placed[j], START + i + 1)
                    s, n = before(i, j)
                    pe.wait_ge(biased[s], START + n)
                    for f in range(NPAIR):
                        for c, w in ((0, 512), (512, NKEY - 512)):
                            mm = pe.matmul(s_ps[0:R, c:c + w], q_diag[:, j, f, :], kT[:, j, f, c:c + w],
                                           start=(f == 0), stop=(f == NPAIR - 1))
                    mm.then_inc(scored[j], 1)

                def turn(i, j):
                    pe.wait_ge(normed[j], START + i + 1)
                    s, n = before(i, j)
                    pe.wait_ge(lo_kept[s], START + n)
                    kit.settle(pe)
                    for t in range(VT):
                        pe.transpose(t_ps[:, t * R:(t + 1) * R], probs[:, j, t * P:(t + 1) * P],
                                     kit.c(C_IDENT, R, R))
                    pe.transpose(t_ps[0:T_DEC, VT * R:(VT + 1) * R], probs[:, j, VT * P:NKEY],
                                 kit.c(C_IDENT, R, R)).then_inc(flipped[j], 1)

                def values(i, j):
                    pe.wait_ge(lo_kept[j], START + i + 1)
                    pe.wait_ge(v_split_dve[j], START + i + 1)
                    pe.wait_ge(v_split_pool[j], START + i + 1)
                    s, n = before(i, j)
                    pe.wait_ge(owned[s], START + n)
                    for c in (0, 512):
                        for t in range(VT):
                            for k, part in enumerate((v_hi[:, j], v_lo)):
                                pe.matmul(pv_ps[:, c:c + 512], turned[:, j, t, :], part[:, t, c:c + 512],
                                          start=(t == 0 and k == 0), stop=False)
                        mm = pe.matmul(pv_ps[:, c:c + 512], turned_new[:, j, :], v_new[:, j, c:c + 512],
                                       start=False, stop=True)
                    mm.then_inc(multiplied[j], 1)

                def gather(i, j):
                    pe.wait_ge(owned[j], START + i + 1)
                    pe.wait_ge(o_kept[j], START + i)
                    for f in range(KD):
                        c = (j * KD + f) * T_DEC
                        mm = pe.matmul(o_ps[:, c:c + T_DEC], own[:, f * P:(f + 1) * P], kit.c(C_SEL, T_DEC),
                                       start=True, stop=True)
                    mm.then_inc(gathered[j], 1)

                def step(i, j, last):
                    if not last:
                        score(*ahead(i, j))
                    values(i, j)
                    if not last:
                        turn(*ahead(i, j))
                    gather(i, j)

                score(0, 0)
                turn(0, 0)
                batches(pe, step)

            @block.vector
            def _(dve):
                def softmax(i, j):
                    dve.wait_ge(scored[j], START + i + 1)
                    s, n = before(i, j)
                    dve.wait_ge(exped[s], START + n)
                    kit.settle(dve)
                    dve.tensor_tensor_reduce(out=logits[:], in0=s_ps[0:R, 0:NKEY], in1=bias[:], scale=1.0,
                                             scalar=-3e38, op0=ALU.add, op1=ALU.max,
                                             accum_out=top[:, j, :]).then_inc(biased[j], 1)
                    dve.wait_ge(biased[j], START + i + 1)
                    dve.tensor_scalar(neg[:, j, :], top[:, j, :], -1.0, None, ALU.mult).then_inc(negated[j], 1)
                    dve.wait_ge(exped[j], START + i + 1)
                    dve.reciprocal(rden[:, j, :], den[:, j, :]).then_inc(inverted[j], 1)
                    dve.wait_ge(inverted[j], START + i + 1)
                    dve.tensor_scalar(probs[:, j, :], probs[:, j, :], rden[:, j, :], None,
                                      ALU.mult).then_inc(normed[j], 1)

                def keep_low(i, j):
                    dve.wait_ge(hi_kept[j], START + i + 1)
                    dve.tensor_tensor(turned[:, j, :, R:2 * R], t_ps[:, 0:VT * R].rearrange("p (t r) -> p t r", t=VT),
                                      turned[:, j, :, 0:R].bitcast(F32), ALU.subtract).then_inc(lo_kept[j], 1)

                def step(i, j, last):
                    dve.wait_ge(v_cast[j], START + i + 1)
                    s, n = before(i, j)
                    dve.wait_ge(multiplied[s], START + n)
                    dve.tensor_tensor(v_lo[:, 0:VD, :], v_raw[:, j, 0:VD, :], v_hi[:, j, 0:VD, :].bitcast(F32),
                                      ALU.subtract).then_inc(v_split_dve[j], 1)
                    if not last:
                        softmax(*ahead(i, j))
                    dve.wait_ge(multiplied[j], START + i + 1)
                    s, n = before(i, j)
                    dve.wait_ge(gathered[s], START + n)
                    dve.tensor_tensor(own[:], pv_ps[:], kit.c(C_DIAG, D), ALU.mult).then_inc(owned[j], 1)
                    if not last:
                        keep_low(*ahead(i, j))
                    dve.wait_ge(gathered[j], START + i + 1)
                    dve.tensor_copy(oT[:, :, bass.ds((2 * i + j) * T_DEC, T_DEC)],
                                    o_ps[:, j * KD * T_DEC:(j + 1) * KD * T_DEC].rearrange("p (f t) -> p f t", f=KD)
                                    ).then_inc(o_kept[j], 1)

                dve.wait_ge(common, START + 48)
                softmax(0, 0)
                keep_low(0, 0)
                batches(dve, step)

            @block.scalar
            def _(act):
                def exponent(i, j):
                    act.wait_ge(negated[j], START + i + 1)
                    act.wait_ge(flipped[j], START + i)
                    act.activation(probs[:, j, :], logits[:], ACT.Exp, bias=neg[:, j, :],
                                   accum_out=den[:, j, :]).then_inc(exped[j], 1)

                def cast(i, j):
                    act.wait_ge(v_loaded[j], START + 32 * (i + 1))
                    act.wait_ge(multiplied[j], START + i)
                    act.activation(v_hi[:, j], v_raw[:, j], ACT.Copy).then_inc(v_cast[j], 1)

                def keep_high(i, j):
                    act.wait_ge(flipped[j], START + i + 1)
                    act.wait_ge(multiplied[j], START + i)
                    act.activation(turned_new[:, j, 0:R], t_ps[0:T_DEC, VT * R:(VT + 1) * R], ACT.Copy)
                    act.activation(turned[:, j, :, 0:R], t_ps[:, 0:VT * R].rearrange("p (t r) -> p t r", t=VT),
                                   ACT.Copy).then_inc(hi_kept[j], 1)

                def step(i, j, last):
                    if not last:
                        exponent(*ahead(i, j))
                        cast(*ahead(i, j))
                        keep_high(*ahead(i, j))

                act.wait_ge(zeroed, START + 2)
                exponent(0, 0)
                cast(0, 0)
                keep_high(0, 0)
                batches(act, step)
                for j in range(2):
                    act.wait_ge(o_kept[j], START + NB_DEC // 2)
                act.dma_start(dram["mix"][0:D, SEQ:NTOK].rearrange("(f p) t -> p f t", p=P), oT[:]).then_inc(stored, 16)
                act.wait_ge(stored, START + 16)


def scan_prompt(kit, neg_a, skip):
    nc, dram = kit.nc, kit.dram
    HG = NH // 2
    with ExitStack() as mem:
        def sb(n, s, d=F32):
            return mem.enter_context(nc.sbuf_tensor(n, s, d))

        def ps(n, w):
            return mem.enter_context(nc.psum_tensor(n, [P, w], F32))

        xbc, zT, dt = sb("ssd_xbc", [P, 2, XBC_TILES, P]), sb("ssd_z", [P, 2, KD, P]), sb("ssd_dt", [P, 2, NH])
        dta, decays = sb("ssd_dta", [P, NH]), sb("ssd_decays", [P, 3, NH])
        x_tok, xdt, xw = sb("ssd_x", [P, D]), sb("ssd_xdt", [P, D]), sb("ssd_xw", [P, D])
        b_tok, cb = sb("ssd_btok", [P, 2 * P]), sb("ssd_cb", [P, 2, P])
        steps, mixm = sb("ssd_steps", [P, 2, 4, P]), sb("ssd_m", [P, 4, 4, P])
        y, yT, state = sb("ssd_y", [P, 2, D]), sb("ssd_yT", [P, 2, KD, P]), sb("ssd_state", [P, D])
        skipped = sb("ssd_skip", [P, KD, P])
        turn_ps, misc_ps, seg_ps = ps("ssd_turn", D), ps("ssd_misc", 512), ps("ssd_seg", 512)
        in_ps, off_ps = ps("ssd_in", D), ps("ssd_off", D)

        loaded = kit.sems("ssd_loaded", 2)
        (zeroed, dta_made, x_turned, bcb_made, sums_made, sums_exp, x_kept, xdt_made, xw_made, btok_kept, cb_masked,
         steps_made, seg_made, seg_exp, mix_made, in_made, off_made, y_scaled, y_summed, y_turned, skip_made, y_skipped,
         state_made, state_decayed, state_summed) = (kit.sems(f"ssd_{n}") for n in (
             "zeroed", "dta_done", "xturned", "bcb", "sums", "sumsexp", "xkept", "xdtdone", "xwdone", "btokkept",
             "cbmasked", "stepsdone", "segdone", "segexp", "mixdone", "indone", "offdone", "yscaled", "ysummed",
             "yturned", "skipdone", "yskipped", "stdone", "stdecayed", "stsummed"))
        gated = kit.sems("ssd_gated", 2)
        stored, state_stored = kit.sems("ssd_stored", 2), kit.sems("ssd_ststored")

        def chunks(eng, chunk):
            chunk(0, 0, True)
            chunk(0, 1, False)
            with eng.Fori(1, NT // 2) as i:
                for j in range(2):
                    chunk(i, j, False)

        def before(i, j):
            return (i, 0) if j else (i - 1, 1)

        def heads(ap):
            return ap.rearrange("p (h c) -> p h c", h=NH)

        def per_head(ap, w=HD):
            return ap.unsqueeze(2).broadcast_to([P, ap.shape[1], w])

        with nc.Block() as block:
            @block.sync
            def _(sp):
                def load(i, j):
                    sp.wait_ge(gated[j], START + i)
                    cols = bass.ds((2 * i + j) * P, P)
                    sp.dma_start(xbc[:, j], dram["xbc"][:, cols].rearrange("(f p) t -> p f t", p=P)).then_inc(loaded[j], 16)
                    sp.dma_start(zT[:, j], dram["z"][:, cols].rearrange("(f p) t -> p f t", p=P)).then_inc(loaded[j], 16)
                    sp.dma_start(dt[:, j, :], dram["dt"][cols, :]).then_inc(loaded[j], 16)

                def store(i, j):
                    sp.wait_ge(gated[j], START + i + 1)
                    sp.dma_start(dram["mix"][D:2 * D, bass.ds((2 * i + j) * P, P)].rearrange("(f p) t -> p f t", p=P),
                                 yT[:, j]).then_inc(stored[j], 16)

                load(0, 0)
                with sp.Fori(0, NT // 2 - 1) as i:
                    load(i, 1)
                    store(i, 0)
                    load(i + 1, 0)
                    store(i, 1)
                load(NT // 2 - 1, 1)
                store(NT // 2 - 1, 0)
                store(NT // 2 - 1, 1)
                for j in range(2):
                    sp.wait_ge(stored[j], START + 16 * (NT // 2))

            @block.tensor
            def _(pe):
                def turn_x(i, j):
                    pe.wait_ge(y_skipped, START + 2 * i + j)
                    for f in range(KD):
                        mm = pe.transpose(turn_ps[:, f * P:(f + 1) * P], xbc[:, j, f, :], kit.c(C_IDENT, P))
                    mm.then_inc(x_turned, 1)

                def turn_y(i, j):
                    n = 2 * i + j
                    pe.wait_ge(y_summed, START + n + 1)
                    pe.wait_ge(x_kept, START + n + 1)
                    for f in range(KD):
                        mm = pe.transpose(turn_ps[:, f * P:(f + 1) * P], y[:, j, f * P:(f + 1) * P], kit.c(C_IDENT, P))
                    mm.then_inc(y_turned, 1)

                def segment(i, j, q):
                    n = 2 * i + j
                    pe.wait_ge(steps_made, START + 4 * n + q + 1)
                    if q == 0:
                        pe.wait_ge(sums_exp, START + n + 1)
                    else:
                        pe.wait_ge(seg_exp, START + 4 * n + q)
                    pe.matmul(seg_ps[:], kit.c(C_LOWER, P), steps[:, q % 2].rearrange("p h t -> p (h t)"),
                              start=True, stop=True).then_inc(seg_made, 1)

                def chunk(i, j, first):
                    n = 2 * i + j
                    pe.wait_ge(loaded[j], START + 48 * (i + 1))
                    pe.wait_ge(btok_kept, START + n)
                    pe.wait_ge(cb_masked, START + n)
                    for g in range(2):
                        pe.transpose(misc_ps[:, g * P:(g + 1) * P], xbc[:, j, KD + g, :], kit.c(C_IDENT, P))
                    for g in range(2):
                        mm = pe.matmul(misc_ps[:, (2 + g) * P:(3 + g) * P], xbc[:, j, KD + g, :],
                                       xbc[:, j, KD + 2 + g, :], start=True, stop=True)
                    mm.then_inc(bcb_made, 1)
                    pe.wait_ge(dta_made, START + n + 1)
                    pe.wait_ge(seg_exp, START + 4 * n)
                    for s, m in enumerate((C_UPPER, C_LOWER, C_ONES)):
                        mm = pe.matmul(seg_ps[:, s * NH:(s + 1) * NH], kit.c(m, P), dta[:], start=True, stop=True)
                    mm.then_inc(sums_made, 1)
                    pe.wait_ge(state_summed, START + n)
                    pe.wait_ge(zeroed, START + 1)
                    for g in range(2):
                        mm = pe.matmul(off_ps[:, g * 512:(g + 1) * 512], xbc[:, j, KD + 2 + g, :],
                                       state[:, g * 512:(g + 1) * 512], start=True, stop=True)
                    mm.then_inc(off_made, 1)
                    segment(i, j, 0)
                    if not first:
                        turn_y(*before(i, j))
                    segment(i, j, 1)
                    turn_x(i, j)
                    segment(i, j, 2)
                    segment(i, j, 3)
                    pe.wait_ge(y_scaled, START + n + 1)
                    pe.wait_ge(xw_made, START + n + 1)
                    pe.wait_ge(btok_kept, START + n + 1)
                    for g in range(2):
                        mm = pe.matmul(off_ps[:, g * 512:(g + 1) * 512], b_tok[:, g * P:(g + 1) * P],
                                       xw[:, g * 512:(g + 1) * 512], start=True, stop=True)
                    mm.then_inc(state_made, 1)
                    pe.wait_ge(xdt_made, START + n + 1)
                    pe.wait_ge(y_summed, START + n)
                    for h in range(NH):
                        if h % 4 == 0:
                            pe.wait_ge(mix_made, START + 4 * n + h // 4 + 1)
                        mm = pe.matmul(in_ps[:, h * HD:(h + 1) * HD], mixm[:, h // 4, h % 4, :],
                                       xdt[:, h * HD:(h + 1) * HD], start=True, stop=True)
                    mm.then_inc(in_made, 1)

                chunks(pe, chunk)
                turn_y(NT // 2 - 1, 1)

            @block.gpsimd
            def _(pool):
                def chunk(i, j, first):
                    n = 2 * i + j
                    pool.wait_ge(loaded[j], START + 48 * (i + 1))
                    pool.wait_ge(sums_made, START + n)
                    pool.tensor_tensor(dta[:], dt[:, j, :], neg_a[:], ALU.mult).then_inc(dta_made, 1)
                    pool.wait_ge(dta_made, START + n + 1)
                    for q in range(4):
                        if q < 2:
                            pool.wait_ge(seg_made, START + 4 * n)
                        else:
                            pool.wait_ge(seg_made, START + 4 * n + q - 1)
                        pool.tensor_tensor(steps[:, q % 2], kit.c(C_UPPER, P).unsqueeze(1).broadcast_to([P, 4, P]),
                                           per_head(dta[:, 4 * q:4 * q + 4], P), ALU.mult).then_inc(steps_made, 1)
                    pool.wait_ge(x_kept, START + n + 1)
                    pool.wait_ge(in_made, START + n)
                    pool.tensor_tensor(heads(xdt[:]), heads(x_tok[:]), per_head(dt[:, j, :]), ALU.mult).then_inc(xdt_made, 1)
                    pool.wait_ge(xdt_made, START + n + 1)
                    pool.wait_ge(sums_exp, START + n + 1)
                    pool.wait_ge(state_made, START + n)
                    pool.tensor_tensor(heads(xw[:]), heads(xdt[:]), per_head(decays[:, 1, :]), ALU.mult).then_inc(xw_made, 1)
                    pool.wait_ge(off_made, START + n + 1)
                    pool.tensor_tensor(heads(state[:]), heads(state[:]), per_head(decays[:, 2, :]),
                                       ALU.mult).then_inc(state_decayed, 1)
                    pool.wait_ge(y_skipped, START + n)
                    pool.tensor_tensor(skipped[:], xbc[:, j, 0:KD, :],
                                       skip[:].unsqueeze(2).broadcast_to([P, KD, P]), ALU.mult).then_inc(skip_made, 1)

                kit.prime(pool)
                pool.memset(state[:], 0.0).then_inc(zeroed, 1)
                chunks(pool, chunk)

            @block.scalar
            def _(act):
                def segment(i, j, q):
                    n = 2 * i + j
                    act.wait_ge(seg_made, START + 4 * n + q + 1)
                    act.wait_ge(in_made, START + n)
                    act.activation(mixm[:, q].rearrange("p h t -> p (h t)"), seg_ps[:], ACT.Exp).then_inc(seg_exp, 1)

                def chunk(i, j, first):
                    n = 2 * i + j
                    act.wait_ge(bcb_made, START + n + 1)
                    act.wait_ge(state_made, START + n)
                    act.activation(b_tok[:], misc_ps[:, 0:2 * P], ACT.Copy).then_inc(btok_kept, 1)
                    act.wait_ge(sums_made, START + n + 1)
                    act.wait_ge(state_decayed, START + n)
                    act.wait_ge(y_scaled, START + n)
                    act.activation(decays[:].rearrange("p s h -> p (s h)"), seg_ps[:, 0:3 * NH],
                                   ACT.Exp).then_inc(sums_exp, 1)
                    segment(i, j, 0)
                    segment(i, j, 1)
                    act.wait_ge(x_turned, START + n + 1)
                    act.wait_ge(xdt_made, START + n)
                    act.activation(x_tok[:], turn_ps[:], ACT.Copy).then_inc(x_kept, 1)
                    segment(i, j, 2)
                    segment(i, j, 3)

                chunks(act, chunk)

            @block.vector
            def _(dve):
                def mix(i, j, q):
                    dve.wait_ge(seg_exp, START + 4 * (2 * i + j) + q + 1)
                    dve.tensor_tensor(mixm[:, q], mixm[:, q], cb[:, q // 2, :].unsqueeze(1).broadcast_to([P, 4, P]),
                                      ALU.mult).then_inc(mix_made, 1)

                def add_skip(i, j):
                    n = 2 * i + j
                    dve.wait_ge(y_turned, START + n + 1)
                    dve.wait_ge(skip_made, START + n + 1)
                    dve.wait_ge(stored[j], START + 16 * i)
                    dve.tensor_tensor(yT[:, j].rearrange("p f t -> p (f t)"), turn_ps[:],
                                      skipped[:].rearrange("p f t -> p (f t)"), ALU.add).then_inc(y_skipped, 1)

                def gate(i, j):
                    yt = yT[:, j].rearrange("p f t -> p (f t)")
                    dve.wait_ge(y_skipped, START + 2 * i + j + 1)
                    dve.tensor_tensor(yt, yt, zT[:, j].rearrange("p f t -> p (f t)"), ALU.mult).then_inc(gated[j], 1)

                def chunk(i, j, first):
                    n = 2 * i + j
                    dve.wait_ge(btok_kept, START + n + 1)
                    dve.wait_ge(mix_made, START + 4 * n)
                    dve.tensor_tensor(cb[:], misc_ps[:, 2 * P:4 * P].rearrange("p (g t) -> p g t", g=2),
                                      kit.c(C_UPPER, P).unsqueeze(1).broadcast_to([P, 2, P]),
                                      ALU.mult).then_inc(cb_masked, 1)
                    dve.wait_ge(off_made, START + n + 1)
                    dve.wait_ge(sums_exp, START + n + 1)
                    dve.tensor_tensor(heads(y[:, j, :]), heads(off_ps[:]), per_head(decays[:, 0, :]),
                                      ALU.mult).then_inc(y_scaled, 1)
                    dve.wait_ge(cb_masked, START + n + 1)
                    mix(i, j, 0)
                    if not first:
                        add_skip(*before(i, j))
                    mix(i, j, 1)
                    if not first:
                        gate(*before(i, j))
                    mix(i, j, 2)
                    mix(i, j, 3)
                    dve.wait_ge(state_made, START + n + 1)
                    dve.wait_ge(state_decayed, START + n + 1)
                    dve.tensor_tensor(state[:], state[:], off_ps[:], ALU.add).then_inc(state_summed, 1)
                    dve.wait_ge(in_made, START + n + 1)
                    dve.wait_ge(y_scaled, START + n + 1)
                    dve.tensor_tensor(y[:, j, :], y[:, j, :], in_ps[:], ALU.add).then_inc(y_summed, 1)

                chunks(dve, chunk)
                add_skip(NT // 2 - 1, 1)
                gate(NT // 2 - 1, 1)

        with nc.Block() as block:
            @block.gpsimd
            def _(pool):
                kit.prime(pool)

            @block.sync
            def _(sp):
                sp.dma_start(dram["ssm_p"], state[:]).then_inc(state_stored, 16)
                sp.wait_ge(state_stored, START + 16)


def scan_sample(kit, neg_a, skip):
    nc, dram = kit.nc, kit.dram
    with ExitStack() as mem:
        def sb(n, s, d=F32):
            return mem.enter_context(nc.sbuf_tensor(n, s, d))

        def ps(n, w):
            return mem.enter_context(nc.psum_tensor(n, [P, w], F32))

        xbc, zT, dt = sb("ss_xbc", [P, XBC_TILES, NS]), sb("ss_z", [P, KD, NS]), sb("ss_dt", [NS, NH])
        dta, decays = sb("ss_dta", [NS, NH]), sb("ss_decays", [NS, 2, NH])
        x_tok, xdt, xw = sb("ss_x", [NS, D]), sb("ss_xdt", [NS, D]), sb("ss_xw", [NS, D])
        b_tok, cb = sb("ss_btok", [NS, 2 * P]), sb("ss_cb", [NS, 2, NS])
        steps, mixm = sb("ss_steps", [NS, NH, NS]), sb("ss_m", [NS, NH, NS])
        y, yT, skipped = sb("ss_y", [NS, D]), sb("ss_yT", [P, KD, NS]), sb("ss_skip", [P, KD, NS])
        off_sum = sb("ss_offsum", [NS, D])
        state, total = sb("ss_state", [P, 2, D]), sb("ss_total", [P, 2, NH])
        c_own, b_own, row_own = sb("ss_cown", [P, 2, 2, NS]), sb("ss_bown", [NS, 2, 2 * P]), sb("ss_rown", [NS, 2, P])
        turn_ps, misc_ps, seg_ps = ps("ss_turn", D), ps("ss_misc", 512), ps("ss_seg", 512)
        in_ps, off_ps = ps("ss_in", D), ps("ss_off", D)

        loaded, state_loaded = kit.sems("ss_loaded"), kit.sems("ss_stloaded", 2)
        (dta_made, x_turned, bc_made, sums_made, kept, cb_masked, steps_made, seg_made, seg_exp, mix_made, xdt_made,
         xw_made, in_made, in_kept, zeroed) = (kit.sems(f"ss_{n}") for n in (
             "dta_done", "xturned", "bc", "sums", "kept", "cbm", "stepsd", "segd", "sege", "mixd", "xdtd", "xwd",
             "ind", "ink", "zero"))
        owned, off_made, off_summed, state_made, total_exp, decayed, updated, state_stored = (
            kit.sems(f"ss_{n}", 2) for n in ("owned", "offd", "offs", "std", "totd", "dec", "upd", "sts"))
        finish = kit.sems("ss_finish")
        y_turned, stored = kit.sems("ss_yturned"), kit.sems("ss_stored")

        def heads(ap):
            return ap.rearrange("p (h c) -> p h c", h=NH)

        def per_head(ap, rows, w=HD):
            return ap.unsqueeze(2).broadcast_to([rows, NH, w])

        with nc.Block() as block:
            @block.gpsimd
            def _(pool):
                kit.prime(pool)

            @block.sync
            def _(sp):
                sp.dma_start(xbc[:], dram["xbc"][:, SEQ:NTOK].rearrange("(f p) t -> p f t", p=P)).then_inc(loaded, 16)
                sp.dma_start(zT[:], dram["z"][:, SEQ:NTOK].rearrange("(f p) t -> p f t", p=P)).then_inc(loaded, 16)
                sp.dma_start(dt[:], dram["dt"][SEQ:NTOK, :]).then_inc(loaded, 16)
                with sp.Fori(0, NB_DEC // 2) as i:
                    for j in range(2):
                        sp.wait_ge(state_stored[j], START + 16 * i)
                        sp.dma_start(state[:, j, :], dram["state_in"][bass.ds(2 * i + j, 1)]
                                     .rearrange("o n c -> n (o c)")).then_inc(state_loaded[j], 16)

            @block.tensor
            def _(pe):
                pe.wait_ge(loaded, START + 48)
                for f in range(KD):
                    mm = pe.transpose(turn_ps[0:NS, f * P:(f + 1) * P], xbc[:, f, :], kit.c(C_IDENT, P))
                mm.then_inc(x_turned, 1)
                for g in range(2):
                    pe.transpose(misc_ps[0:NS, g * P:(g + 1) * P], xbc[:, KD + g, :], kit.c(C_IDENT, P))
                for g in range(2):
                    mm = pe.matmul(misc_ps[0:NS, 2 * P + g * NS:2 * P + (g + 1) * NS], xbc[:, KD + g, :],
                                   xbc[:, KD + 2 + g, :], start=True, stop=True)
                mm.then_inc(bc_made, 1)
                pe.wait_ge(dta_made, START + 1)
                for s, m in enumerate((C_UPPER_S, C_LOWER_S)):
                    mm = pe.matmul(seg_ps[0:NS, s * NH:(s + 1) * NH], kit.c(m, NS, NS), dta[:], start=True, stop=True)
                mm.then_inc(sums_made, 1)
                pe.wait_ge(steps_made, START + 1)
                pe.wait_ge(kept, START + 3)
                pe.matmul(seg_ps[0:NS, :], kit.c(C_LOWER_S, NS, NS), steps[:].rearrange("p h t -> p (h t)"),
                          start=True, stop=True).then_inc(seg_made, 1)
                pe.wait_ge(mix_made, START + 1)
                pe.wait_ge(xdt_made, START + 1)
                for h in range(NH):
                    mm = pe.matmul(in_ps[0:NS, h * HD:(h + 1) * HD], mixm[:, h, :], xdt[:, h * HD:(h + 1) * HD],
                                   start=True, stop=True)
                mm.then_inc(in_made, 1)
                pe.wait_ge(in_kept, START + 1)
                pe.wait_ge(xw_made, START + 1)
                with pe.Fori(0, NB_DEC // 2) as i:
                    for j in range(2):
                        pe.wait_ge(state_loaded[j], START + 16 * (i + 1))
                        pe.wait_ge(owned[j], START + i + 1)
                        if j:
                            pe.wait_ge(off_summed[0], START + i + 1)
                        else:
                            pe.wait_ge(off_summed[1], START + i)
                        for g in range(2):
                            mm = pe.matmul(off_ps[0:NS, g * 512:(g + 1) * 512], c_own[:, j, g, :],
                                           state[:, j, g * 512:(g + 1) * 512], start=True, stop=True)
                        mm.then_inc(off_made[j], 1)
                        if j:
                            pe.wait_ge(updated[0], START + i + 1)
                        else:
                            pe.wait_ge(updated[1], START + i)
                        pe.matmul(misc_ps[:, 0:NH], row_own[:, j, :], dta[:], start=True, stop=True)
                        for g in range(2):
                            mm = pe.matmul(in_ps[:, g * 512:(g + 1) * 512], b_own[:, j, g * P:(g + 1) * P],
                                           xw[:, g * 512:(g + 1) * 512], start=True, stop=True)
                        mm.then_inc(state_made[j], 1)
                pe.wait_ge(finish, START + 3)
                for f in range(KD):
                    mm = pe.transpose(turn_ps[:, f * NS:(f + 1) * NS], y[:, f * P:(f + 1) * P], kit.c(C_IDENT, NS, NS))
                mm.then_inc(y_turned, 1)

            @block.scalar
            def _(act):
                act.wait_ge(x_turned, START + 1)
                act.activation(x_tok[:], turn_ps[0:NS, :], ACT.Copy).then_inc(kept, 1)
                act.wait_ge(bc_made, START + 1)
                act.activation(b_tok[:], misc_ps[0:NS, 0:2 * P], ACT.Copy).then_inc(kept, 1)
                act.wait_ge(sums_made, START + 1)
                act.activation(decays[:].rearrange("p s h -> p (s h)"), seg_ps[0:NS, 0:2 * NH], ACT.Exp).then_inc(kept, 1)
                act.wait_ge(seg_made, START + 1)
                act.activation(mixm[:].rearrange("p h t -> p (h t)"), seg_ps[0:NS, :], ACT.Exp).then_inc(seg_exp, 1)
                with act.Fori(0, NB_DEC // 2) as i:
                    for j in range(2):
                        act.wait_ge(state_made[j], START + i + 1)
                        act.wait_ge(updated[j], START + i)
                        act.activation(total[:, j, :], misc_ps[:, 0:NH], ACT.Exp).then_inc(total_exp[j], 1)
                        act.wait_ge(updated[j], START + i + 1)
                        act.dma_start(dram["ssm_s"][bass.ds(2 * i + j, 1)].rearrange("o n c -> n (o c)"),
                                      state[:, j, :]).then_inc(state_stored[j], 16)
                for j in range(2):
                    act.wait_ge(state_stored[j], START + 16 * (NB_DEC // 2))
                act.wait_ge(finish, START + 5)
                act.dma_start(dram["mix"][D:2 * D, SEQ:NTOK].rearrange("(f p) t -> p f t", p=P), yT[:]).then_inc(stored, 16)
                act.wait_ge(stored, START + 16)

            @block.vector
            def _(dve):
                dve.memset(off_sum[:], 0.0).then_inc(zeroed, 1)
                dve.wait_ge(loaded, START + 48)
                dve.tensor_tensor(dta[:], dt[:], neg_a[0:NS, :], ALU.mult).then_inc(dta_made, 1)
                dve.wait_ge(dta_made, START + 1)
                dve.tensor_tensor(steps[:], kit.c(C_UPPER_S, NS, NS).unsqueeze(1).broadcast_to([NS, NH, NS]),
                                  per_head(dta[:], NS, NS), ALU.mult).then_inc(steps_made, 1)
                dve.wait_ge(kept, START + 3)
                dve.tensor_tensor(heads(xdt[:]), heads(x_tok[:]), per_head(dt[:], NS), ALU.mult).then_inc(xdt_made, 1)
                dve.wait_ge(xdt_made, START + 1)
                dve.tensor_tensor(heads(xw[:]), heads(xdt[:]), per_head(decays[:, 1, :], NS), ALU.mult).then_inc(xw_made, 1)
                dve.tensor_tensor(cb[:], misc_ps[0:NS, 2 * P:2 * P + 2 * NS].rearrange("p (g t) -> p g t", g=2),
                                  kit.c(C_UPPER_S, NS, NS).unsqueeze(1).broadcast_to([NS, 2, NS]),
                                  ALU.mult).then_inc(cb_masked, 1)
                dve.wait_ge(cb_masked, START + 1)
                dve.wait_ge(seg_exp, START + 1)
                for g in range(2):
                    last = dve.tensor_tensor(mixm[:, g * NH // 2:(g + 1) * NH // 2, :], mixm[:, g * NH // 2:(g + 1) * NH // 2, :],
                                             cb[:, g, :].unsqueeze(1).broadcast_to([NS, NH // 2, NS]), ALU.mult)
                last.then_inc(mix_made, 1)
                dve.wait_ge(in_made, START + 1)
                dve.tensor_copy(y[:], in_ps[0:NS, :]).then_inc(in_kept, 1)
                dve.tensor_tensor(skipped[:], xbc[:, 0:KD, :], skip[:].unsqueeze(2).broadcast_to([P, KD, NS]),
                                  ALU.mult)
                dve.wait_ge(zeroed, START + 1)

                def own_rows(i, j):
                    b = 2 * i + j
                    dve.wait_ge(state_made[j], START + i)
                    dve.tensor_tensor(c_own[:, j], xbc[:, KD + 2:KD + 4, :],
                                      kit.const[:, bass.ds(b * NS + C_BMASK, NS)].unsqueeze(1).broadcast_to([P, 2, NS]),
                                      ALU.mult)
                    own = kit.const[0:NS, bass.ds(b + C_BROW, 1)]
                    dve.tensor_tensor(b_own[:, j, :], b_tok[:], own.broadcast_to([NS, 2 * P]), ALU.mult)
                    dve.tensor_tensor(row_own[:, j, :], kit.c(C_ONES, P, NS), own.broadcast_to([NS, P]),
                                      ALU.mult).then_inc(owned[j], 1)

                def step(i, j, last):
                    if not last:
                        own_rows(i + 1 if j else i, 1 - j)
                    dve.wait_ge(off_made[j], START + i + 1)
                    if j:
                        dve.wait_ge(off_summed[0], START + i + 1)
                    else:
                        dve.wait_ge(off_summed[1], START + i)
                    dve.tensor_tensor(off_sum[:], off_sum[:], off_ps[0:NS, :], ALU.add).then_inc(off_summed[j], 1)
                    dve.wait_ge(total_exp[j], START + i + 1)
                    dve.tensor_tensor(heads(state[:, j, :]), heads(state[:, j, :]), per_head(total[:, j, :], P),
                                      ALU.mult).then_inc(decayed[j], 1)
                    dve.wait_ge(decayed[j], START + i + 1)
                    dve.tensor_tensor(state[:, j, :], state[:, j, :], in_ps[:], ALU.add).then_inc(updated[j], 1)

                own_rows(0, 0)
                with dve.Fori(0, NB_DEC // 2 - 1) as i:
                    for j in range(2):
                        step(i, j, False)
                for j in range(2):
                    step(NB_DEC // 2 - 1, j, j == 1)
                dve.wait_ge(off_summed[1], START + NB_DEC // 2)
                dve.tensor_tensor(heads(off_sum[:]), heads(off_sum[:]), per_head(decays[:, 0, :], NS), ALU.mult).then_inc(finish, 1)
                dve.wait_ge(finish, START + 1)
                dve.tensor_tensor(y[:], y[:], off_sum[:], ALU.add).then_inc(finish, 2)
                dve.wait_ge(y_turned, START + 1)
                dve.tensor_tensor(yT[:].rearrange("p f t -> p (f t)"), turn_ps[:, 0:KD * NS],
                                  skipped[:].rearrange("p f t -> p (f t)"), ALU.add).then_inc(finish, 1)
                dve.wait_ge(finish, START + 4)
                dve.tensor_tensor(yT[:], yT[:], zT[:], ALU.mult).then_inc(finish, 1)


def out_project(kit, h, gain):
    nc, dram = kit.nc, kit.dram
    KM = 2 * KD
    with ExitStack() as mem:
        def sb(n, s, d=F32):
            return mem.enter_context(nc.sbuf_tensor(n, s, d))

        m_hi, m_lo = sb("mix_hi", [P, KM, NTOK], F32R), sb("mix_lo", [P, KM, NTOK], F32R)
        eps = sb("mix_eps", [P, 1])
        loaded, hi_made, lo_made = (kit.sems(f"mix_{n}", 2) for n in ("loaded", "hi", "lo"))
        ssd_loaded, ssd_hi_made, ssd_lo_made = kit.sems("mix_ssd", KD), kit.sems("mix_ssdhi", 2), kit.sems("mix_ssdlo", 2)
        squared, summed, scaled = (kit.sems(f"mix_{n}", 2) for n in ("squared", "summed", "scaled"))
        rooted, inverted, eps_set = kit.sems("mix_rooted", 2), kit.sems("mix_inverted", 2), kit.sems("mix_eps")
        with ExitStack() as tmp:
            sq, raw, rinv = (tmp.enter_context(nc.sbuf_tensor(f"mix_{n}", [P, 2, NTOK], F32))
                             for n in ("sq", "raw", "rinv"))
            ssd = h
            acc = [tmp.enter_context(nc.psum_tensor(f"mix_ps{g}", [P, 3 * 512], F32)) for g in range(2)]
            with nc.Block() as block:
                @block.gpsimd
                def _(pool):
                    kit.prime(pool)
                    for k in range(KD):
                        pool.wait_ge(hi_made[k % 2], START + k // 2 + 1)
                        pool.tensor_tensor(m_lo[:, k, :], raw[:, k % 2, :], m_hi[:, k, :].bitcast(F32),
                                           ALU.subtract).then_inc(lo_made[k % 2], 1)
                    for g in range(2):
                        pool.wait_ge(lo_made[g], START + KD // 2)

                @block.sync
                def _(sp):
                    for k in range(KD):
                        sp.dma_start(ssd[:, k, :], dram["mix"][D + k * P:D + (k + 1) * P, :]).then_inc(ssd_loaded[k], 16)
                    for k in range(KD):
                        if k >= 2:
                            sp.wait_ge(lo_made[k % 2], START + k // 2)
                        sp.dma_start(raw[:, k % 2, :], dram["mix"][k * P:(k + 1) * P, :]).then_inc(loaded[k % 2], 16)

                @block.scalar
                def _(act):
                    def root(g):
                        act.wait_ge(eps_set, START + 1)
                        for j in range(2):
                            act.wait_ge(summed[j], START + (g + 1) * KD // 4)
                        act.activation(grouped(rinv[:, g, :]), in_banks(acc[g]), ACT.Sqrt, bias=eps[:],
                                       scale=2.0 / D).then_inc(rooted[g], 1)

                    def cast_attention(k):
                        act.wait_ge(loaded[k % 2], START + 16 * (k // 2 + 1))
                        act.activation(m_hi[:, k, :], raw[:, k % 2, :], ACT.Copy).then_inc(hi_made[k % 2], 1)

                    for k in range(KD):
                        act.wait_ge(ssd_loaded[k], START + 16)
                        if k >= 2:
                            act.wait_ge(summed[k % 2], START + k // 2)
                        act.activation(sq[:, k % 2, :], ssd[:, k, :], ACT.Square).then_inc(squared[k % 2], 1)
                        if k == KD // 2 + 1:
                            root(0)
                    cast_attention(0)
                    cast_attention(1)
                    root(1)
                    for k in range(KD):
                        act.wait_ge(scaled[k % 2], START + k // 2 + 1)
                        act.activation(m_hi[:, KD + k, :], ssd[:, k, :], ACT.Copy).then_inc(ssd_hi_made[k % 2], 1)
                        if k >= 2:
                            cast_attention(k)

                @block.tensor
                def _(pe):
                    for k in range(KD):
                        g = k // (KD // 2)
                        pe.wait_ge(squared[k % 2], START + k // 2 + 1)
                        for c, w in GROUPS:
                            mm = pe.matmul(bank(acc[g], c, w), kit.c(C_ONES, P), sq[:, k % 2, c:c + w],
                                           start=(k % (KD // 2) == 0), stop=(k % (KD // 2) == KD // 2 - 1))
                        mm.then_inc(summed[k % 2], 1)

                @block.vector
                def _(dve):
                    def invert(g):
                        dve.wait_ge(rooted[g], START + 1)
                        dve.reciprocal(rinv[:, g, :], rinv[:, g, :]).then_inc(inverted[g], 1)

                    def scale(k):
                        dve.wait_ge(inverted[k // (KD // 2)], START + 1)
                        dve.scalar_tensor_tensor(out=ssd[:, k, :], in0=ssd[:, k, :], scalar=gain[:, k:k + 1],
                                                 in1=rinv[:, k // (KD // 2), :], op0=ALU.mult,
                                                 op1=ALU.mult).then_inc(scaled[k % 2], 1)

                    dve.memset(eps[:], EPS).then_inc(eps_set, 1)
                    invert(0)
                    for k in range(KD // 2):
                        scale(k)
                    invert(1)
                    for k in range(KD):
                        if k >= 2 and k + 2 < KD:
                            scale(k + 2)
                        dve.wait_ge(ssd_hi_made[k % 2], START + k // 2 + 1)
                        dve.tensor_tensor(m_lo[:, KD + k, :], ssd[:, k, :], m_hi[:, KD + k, :].bitcast(F32),
                                          ALU.subtract).then_inc(ssd_lo_made[k % 2], 1)
                    for g in range(2):
                        dve.wait_ge(ssd_lo_made[g], START + KD // 2)

        with ExitStack() as tmp:
            w_raw = tmp.enter_context(nc.sbuf_tensor("wo_raw", [P, 2, KM // 2 * P], F32))
            w_hi = tmp.enter_context(nc.sbuf_tensor("wo_hi", [P, 2, KM // 2, P], F32R))
            w_lo = tmp.enter_context(nc.sbuf_tensor("wo_lo", [P, 2, KM // 2, P], F32R))
            acc = [tmp.enter_context(nc.psum_tensor(f"wo_ps{g}", [P, 3 * 512], F32)) for g in range(2)]
            w_loaded, w_hi_made, w_split, w_used = (kit.sems(f"wo_{n}", 2) for n in ("loaded", "hi", "split", "used"))
            made, added, x_loaded = kit.sems("wo_made", 2), kit.sems("wo_added", 2), kit.sems("wo_x")
            with nc.Block() as block:
                @block.sync
                def _(sp):
                    with sp.Fori(0, KD) as i:
                        for s in range(2):
                            sp.wait_ge(w_split[s], START + i)
                            sp.dma_start(w_raw[:, s, :], dram["w_out"][bass.ds(i, 1), :, s * D:(s + 1) * D]
                                         .rearrange("o p c -> p (o c)")).then_inc(w_loaded[s], 16)

                @block.scalar
                def _(act):
                    act.wait_ge(w_loaded[1], START + 16)
                    act.dma_start(h[:], dram["x"].rearrange("(f p) t -> p f t", p=P)).then_inc(x_loaded, 16)

                @block.gpsimd
                def _(pool):
                    kit.prime(pool)
                    with pool.Fori(0, KD) as i:
                        for s in range(2):
                            pool.wait_ge(w_loaded[s], START + 16 * (i + 1))
                            pool.wait_ge(w_used[s], START + i)
                            raw_w = w_raw[:, s, :].rearrange("p (k m) -> p k m", m=P)
                            kit.settle(pool)
                            pool.tensor_copy(w_hi[:, s], raw_w).then_inc(w_hi_made[s], 1)
                            pool.wait_ge(w_hi_made[s], START + i + 1)
                            pool.tensor_tensor(w_lo[:, s], raw_w, w_hi[:, s].bitcast(F32), ALU.subtract).then_inc(w_split[s], 1)

                @block.tensor
                def _(pe):
                    with pe.Fori(0, KD // 2) as i:
                        for j in range(2):
                            pe.wait_ge(added[j], START + i)
                            for s in range(2):
                                pe.wait_ge(w_split[s], START + 2 * i + j + 1)
                                for kk in range(KM // 2):
                                    k = s * (KM // 2) + kk
                                    for wt, xt in ((w_hi, m_hi), (w_hi, m_lo), (w_lo, m_hi)):
                                        for c, w in GROUPS:
                                            mm = pe.matmul(bank(acc[j], c, w), wt[:, s, kk, :], xt[:, k, c:c + w],
                                                           start=(k == 0 and wt is w_hi and xt is m_hi),
                                                           stop=(k == KM - 1 and wt is w_lo))
                                if s == 0:
                                    mm.then_inc(w_used[0], 1)
                            mm.then_inc(made[j], 1)

                @block.vector
                def _(dve):
                    dve.wait_ge(x_loaded, START + 16)
                    with dve.Fori(0, KD // 2) as i:
                        for j in range(2):
                            row = h[:, bass.ds(2 * i + j, 1), :].rearrange("p o t -> p (o t)")
                            dve.wait_ge(made[j], START + i + 1)
                            dve.sem_inc(w_used[1], 1)
                            dve.tensor_tensor(grouped(row), grouped(row), in_banks(acc[j]), ALU.add).then_inc(added[j], 1)
                    for j in range(2):
                        dve.wait_ge(added[j], START + KD // 2)


def feed_forward(kit, h, gain, x_hi, x_lo):
    nc, dram = kit.nc, kit.dram
    with ExitStack() as mem:
        def sb(n, s, d=F32):
            return mem.enter_context(nc.sbuf_tensor(n, s, d))

        w_raw, w_hi, w_lo = sb("wf_raw", [P, 2, D]), sb("wf_hi", [P, 2, KD, P], F32R), sb("wf_lo", [P, 2, KD, P], F32R)
        r_hi, r_lo = sb("r_hi", [P, FT, NTOK], F32R), sb("r_lo", [P, FT, NTOK], F32R)
        relu, r_sq = sb("relu", [P, 2, NTOK]), sb("r_sq", [P, 2, NTOK])
        acc = [mem.enter_context(nc.psum_tensor(f"ff_ps{j}", [P, 3 * 512], F32)) for j in range(2)]
        w_loaded, w_hi_made, w_split = (kit.sems(f"wf_{n}", 2) for n in ("loaded", "hi", "split"))
        w_used = kit.sems("wf_used", 2)
        up_made, relued, squared, hi_made, split = (kit.sems(f"ff_{n}", 2) for n in ("up", "relu", "sq", "hi", "split"))
        down_made, added = kit.sems("ff_down", 2), kit.sems("ff_added", 2)
        stored = kit.sems("ff_stored")
        UN = 2 * FT // 2
        norm = RmsSplit(kit, mem, "ffnnorm", h, None, gain, x_hi, x_lo, relu, r_sq, acc[1])

        with nc.Block() as block:
            @block.sync
            def _(sp):
                with sp.Fori(0, NFC) as i:
                    for n in range(2 * FT):
                        j = n % 2
                        sp.wait_ge(w_split[j], START + UN * i + n // 2)
                        src = dram["w_up"] if n < FT else dram["w_down"]
                        sp.dma_start(w_raw[:, j, :], src[bass.ds(FT * i + n % FT, 1)]
                                     .rearrange("o p c -> p (o c)")).then_inc(w_loaded[j], 16)
                for o in range(KD):
                    sp.wait_ge(added[o % 2], START + KD // 2 * (NFC - 1) + o // 2 + 1)
                    sp.dma_start(dram["y"][o * P:(o + 1) * P, :], h[:, o, :]).then_inc(stored, 16)
                sp.wait_ge(stored, START + 16 * KD)

            @block.gpsimd
            def _(pool):
                kit.prime(pool)
                with pool.Fori(0, NFC) as i:
                    for n in range(2 * FT):
                        j = n % 2
                        pool.wait_ge(w_loaded[j], START + (UN * i + n // 2 + 1) * 16)
                        pool.wait_ge(w_used[j], START + UN * i + n // 2)
                        raw_w = w_raw[:, j, :].rearrange("p (k m) -> p k m", m=P)
                        kit.settle(pool)
                        pool.tensor_copy(w_hi[:, j], raw_w).then_inc(w_hi_made[j], 1)
                        pool.wait_ge(w_hi_made[j], START + UN * i + n // 2 + 1)
                        pool.tensor_tensor(w_lo[:, j], raw_w, w_hi[:, j].bitcast(F32),
                                           ALU.subtract).then_inc(w_split[j], 1)

            @block.tensor
            def _(pe):
                norm.tensor(pe)

                def chunk(i, first):
                    for f in range(FT):
                        j = f % 2
                        pe.wait_ge(w_split[j], START + UN * i + f // 2 + 1)
                        if f < 2:
                            pe.wait_ge(added[j], START + KD // 2 * i)
                        else:
                            pe.wait_ge(squared[j], START + FT // 2 * i + f // 2)
                        for k in range(KD):
                            if first and f == 0:
                                norm.wait_tile(pe, k)
                            for wt, xt in ((w_hi, x_hi), (w_hi, x_lo), (w_lo, x_hi)):
                                for c, w in GROUPS:
                                    mm = pe.matmul(bank(acc[j], c, w), wt[:, j, k, :], xt[:, k, c:c + w],
                                                   start=(k == 0 and wt is w_hi and xt is x_hi),
                                                   stop=(k == KD - 1 and wt is w_lo))
                        mm.then_inc(up_made[j], 1)
                    for o in range(KD):
                        j, n = o % 2, FT + o // 2
                        s = n % 2
                        if o % 2 == 0:
                            pe.wait_ge(w_split[s], START + UN * i + n // 2 + 1)
                        if o < 2:
                            pe.wait_ge(squared[j], START + FT // 2 * (i + 1))
                        else:
                            pe.wait_ge(added[j], START + KD // 2 * i + o // 2)
                        for k in range(FT):
                            if o == 0:
                                pe.wait_ge(split[k % 2], START + FT // 2 * i + k // 2 + 1)
                            for wt, xt in ((w_hi, r_hi), (w_hi, r_lo), (w_lo, r_hi)):
                                for c, w in GROUPS:
                                    mm = pe.matmul(bank(acc[j], c, w), wt[:, s, (o % 2) * FT + k, :], xt[:, k, c:c + w],
                                                   start=(k == 0 and wt is w_hi and xt is r_hi),
                                                   stop=(k == FT - 1 and wt is w_lo))
                        mm.then_inc(down_made[j], 1)

                chunk(0, True)
                with pe.Fori(1, NFC) as i:
                    chunk(i, False)

            @block.scalar
            def _(act):
                norm.scalar(act)
                with act.Fori(0, NFC) as i:
                    for f in range(FT):
                        j = f % 2
                        u = FT // 2 * i + f // 2
                        act.wait_ge(up_made[j], START + u + 1)
                        act.wait_ge(squared[j], START + u)
                        act.activation(grouped(relu[:, j, :]), in_banks(acc[j]), ACT.Relu).then_inc(relued[j], 1)
                        act.wait_ge(squared[j], START + u + 1)
                        act.wait_ge(down_made[0], START + KD // 2 * i)
                        act.wait_ge(down_made[1], START + KD // 2 * i)
                        act.activation(r_hi[:, f, :], r_sq[:, j, :], ACT.Copy).then_inc(hi_made[j], 1)
                        act.sem_inc(w_used[j], 1)
                    for o in range(KD):
                        j = o % 2
                        act.wait_ge(down_made[j], START + KD // 2 * i + o // 2 + 1)
                        if o % 2 == 1:
                            act.sem_inc(w_used[(o // 2) % 2], 1)

            @block.vector
            def _(dve):
                norm.vector(dve)
                with dve.Fori(0, NFC) as i:
                    for f in range(FT):
                        j = f % 2
                        u = FT // 2 * i + f // 2
                        dve.wait_ge(relued[j], START + u + 1)
                        dve.wait_ge(split[j], START + u)
                        dve.tensor_tensor(r_sq[:, j, :], relu[:, j, :], relu[:, j, :], ALU.mult).then_inc(squared[j], 1)
                        dve.wait_ge(hi_made[j], START + u + 1)
                        dve.tensor_tensor(r_lo[:, f, :], r_sq[:, j, :], r_hi[:, f, :].bitcast(F32),
                                          ALU.subtract).then_inc(split[j], 1)
                    for o in range(KD):
                        j = o % 2
                        dve.wait_ge(down_made[j], START + KD // 2 * i + o // 2 + 1)
                        if o >= 2:
                            dve.wait_ge(added[j], START + KD // 2 * i + o // 2)
                        dve.tensor_tensor(grouped(h[:, o, :]), grouped(h[:, o, :]), in_banks(acc[j]), ALU.add).then_inc(added[j], 1)
                for j in range(2):
                    dve.wait_ge(added[j], START + KD // 2 * NFC)


def prepare_parameters(kit, small, neg_a):
    nc, dram = kit.nc, kit.dram
    loaded, made = kit.sems("param_loaded"), kit.sems("param_made")
    with nc.Block() as block:
        @block.gpsimd
        def _(pool):
            kit.prime(pool)

        @block.sync
        def _(sp):
            sp.dma_start(small[:], dram["params"]).then_inc(loaded, 16)
            sp.dma_start(neg_a[:], dram["a_log"].partition_broadcast(P)).then_inc(loaded, 16)

        @block.scalar
        def _(act):
            act.wait_ge(loaded, START + 32)
            act.activation(neg_a[:], neg_a[:], ACT.Exp).then_inc(made, 1)

        @block.vector
        def _(dve):
            dve.wait_ge(made, START + 1)
            dve.tensor_scalar(neg_a[:], neg_a[:], -1.0, None, ALU.mult).then_inc(made, 1)
            dve.tensor_scalar(small[:, PAR_Q:PAR_Q + KD], small[:, PAR_Q:PAR_Q + KD], HD ** -0.5, None,
                              ALU.mult).then_inc(made, 1)
            dve.wait_ge(made, START + 3)


PAR_MIX, PAR_Q, PAR_K, PAR_FFN, PAR_SSM, PAR_SKIP = (KD * n for n in range(6))
PAR_END = 6 * KD


def build(nc, dram):
    with ExitStack() as stack:
        kit = Kit(nc, stack, dram)
        small = stack.enter_context(nc.sbuf_tensor("params", [P, PAR_END], F32))
        neg_a = stack.enter_context(nc.sbuf_tensor("neg_a", [P, NH], F32))
        skip = small[:, PAR_SKIP:PAR_SKIP + KD]
        with kit.part(), ExitStack() as mem:
            x_loaded = kit.sems("x_loaded", KD)
            x_hi = mem.enter_context(nc.sbuf_tensor("u_hi", [P, KD, NPAD], F32R))
            x_lo = mem.enter_context(nc.sbuf_tensor("u_lo", [P, KD, NPAD], F32R))
            x_mem = mem.enter_context(ExitStack())
            x = x_mem.enter_context(nc.sbuf_tensor("x", [P, KD, NTOK], F32))
            load_constants(kit, x, x_loaded)
            prepare_parameters(kit, small, neg_a)
            distance_table(kit)
            project(kit, x, x_loaded, small[:, PAR_MIX:PAR_MIX + KD], x_hi, x_lo, small[:, PAR_Q:PAR_Q + QK_TILES])
            x_mem.close()
            project_tokens(kit, x_hi, x_lo)
        with kit.part():
            attend_prompt(kit)
            attend_sample(kit)
        with kit.part():
            scan_prompt(kit, neg_a, skip)
            scan_sample(kit, neg_a, skip)
        with kit.part(), ExitStack() as mem:
            h = mem.enter_context(nc.sbuf_tensor("h", [P, KD, NTOK], F32))
            out_project(kit, h, small[:, PAR_SSM:PAR_SSM + KD])
            x_hi = mem.enter_context(nc.sbuf_tensor("uf_hi", [P, KD, NTOK], F32R))
            x_lo = mem.enter_context(nc.sbuf_tensor("uf_lo", [P, KD, NTOK], F32R))
            feed_forward(kit, h, small[:, PAR_FFN:PAR_FFN + KD], x_hi, x_lo)


def tiles(w, rows_of_tile, cols_of_tile):
    k, n = w.shape
    t = w.reshape(k // rows_of_tile, rows_of_tile, n // cols_of_tile, cols_of_tile)
    return np.ascontiguousarray(t.transpose(2, 1, 0, 3)).reshape(n // cols_of_tile, rows_of_tile, -1)


def by_tile(v):
    return v.reshape(-1, P).T


def lay_out(a):
    f = {k: np.asarray(v) for k, v in a.items()}
    w_in = f["w_in"][0]
    q, k, v, z, xbc, dt = np.split(w_in, [D, 2 * D, 3 * D, 4 * D, 4 * D + XBC], axis=1)
    w_tok = np.concatenate([v, dt], axis=1).reshape(KD, P, D + NH)
    w_down = f["w_down"][0].reshape(NFC, FT, P, KD // 2, 2, P)
    def reach(cache):
        c = cache[0].reshape(NB_DEC, PAST, D)
        far = c.reshape(NB_DEC, PAST // 16, 16, D)[:, :FAR // 4, :4].reshape(NB_DEC, FAR, D)
        return np.concatenate([far, c[:, PAST - DENSE:]], axis=1)
    ck, cv = reach(f["cache_attn_k"]), reach(f["cache_attn_v"])
    taps = np.concatenate([f["conv_w"][0], f["conv_b"]], axis=0)
    params = np.concatenate([by_tile(f["norm_mix"][0]),
                             by_tile(np.tile(f["q_norm"][0], NH)), by_tile(np.tile(f["k_norm"][0], NH)),
                             by_tile(f["norm_ffn"][0]), by_tile(f["ssm_norm"][0]),
                             by_tile(np.repeat(f["d_skip"][0], HD))], axis=1)
    x = np.concatenate([f["x_prompt"][0], f["x_sample"].reshape(NS, D)], axis=0)
    out = {
        "x": x.T,
        "w_feat": tiles(np.concatenate([q, k, xbc, z], axis=1), P, P),
        "w_tok": w_tok,
        "conv_taps": taps.reshape(WIDTH + 1, XBC_TILES, P).transpose(2, 1, 0),
        "conv_past": f["state_conv"][0].reshape(NB_DEC * (WIDTH - 1), XBC_TILES, P).transpose(2, 1, 0),
        "dt_bias": f["dt_bias"].reshape(NH), "a_log": f["a_log"].reshape(NH), "rel_bias": f["rel_bias"],
        "params": params,
        "cache_k": ck.reshape(NB_DEC, FAR + DENSE, NPAIR, P).transpose(0, 3, 2, 1).reshape(NB_DEC, P, -1),
        "cache_v": cv.reshape(NB_DEC, VT, P, D).transpose(0, 2, 1, 3).reshape(NB_DEC, P, -1),
        "state_in": f["state_ssm"][0].reshape(NB_DEC, D, NSTATE).transpose(0, 2, 1),
        "w_out": tiles(f["w_out"][0], P, P),
        "w_up": tiles(f["w_up"][0], P, P),
        "w_down": w_down.transpose(0, 3, 2, 4, 1, 5).reshape(NFC * KD // 2, P, 2 * FT * P),
        "consts": shape_constants(), "onehot": distance_constants(),
    }
    return {n: np.ascontiguousarray(v) for n, v in out.items()}


_OUTS = {"y": (D, NTOK), "qk": (2 * D, NTOK), "v": (NPAD, D), "conv_tail": (P, XBC_TILES * 27),
         "ssm_p": (NSTATE, D), "ssm_s": (NB_DEC, NSTATE, D)}
_SCRATCH = {"xbc": (XBC, NTOK), "z": (D, NTOK), "dt": (NPAD, NH), "mix": (2 * D, NTOK), "table": (NH, LLEN), "bias_rows": (NH * P, SEQ),
            "bias_sample": (NH * T_DEC, NKEY)}


def kernel(**inputs):
    import concourse.bacc as bacc
    from concourse.bass_utils import run_bass_kernel_spmd

    nc = bacc.Bacc("TRN2", target_bir_lowering=False, num_devices=1)
    arrays, dram = {}, {}
    for name, a in lay_out(inputs).items():
        arrays[f"in_{name}"] = a
        dram[name] = nc.dram_tensor(f"in_{name}", a.shape, F32, kind="ExternalInput").ap()
    for name, shape in _OUTS.items():
        dram[name] = nc.dram_tensor(f"out_{name}", shape, F32, kind="ExternalOutput").ap()
    for name, shape in _SCRATCH.items():
        dram[name] = nc.dram_tensor(f"tmp_{name}", shape, F32).ap()
    build(nc, dram)
    r = run_bass_kernel_spmd(nc, [arrays], core_ids=[0]).results[0]
    y, qk, v, tail = r["out_y"], r["out_qk"], r["out_v"], r["out_conv_tail"]
    k = np.ascontiguousarray(qk[D:].T)
    conv = tail.reshape(P, XBC_TILES, (NB_DEC + 1) * (WIDTH - 1)).transpose(2, 1, 0).reshape(NB_DEC + 1, WIDTH - 1, XBC)
    outs = (
        y[:, :SEQ].T.reshape(1, SEQ, D),
        y[:, SEQ:].T.reshape(NB_DEC, T_DEC, D),
        k[:SEQ].reshape(1, 1, SEQ, NH, HD),
        v[:SEQ].reshape(1, 1, SEQ, NH, HD),
        conv[0].reshape(1, 1, WIDTH - 1, XBC),
        r["out_ssm_p"].T.reshape(1, 1, NH, HD, NSTATE),
        k[SEQ:].reshape(1, NB_DEC, T_DEC, NH, HD),
        v[SEQ:NTOK].reshape(1, NB_DEC, T_DEC, NH, HD),
        conv[1:].reshape(1, NB_DEC, WIDTH - 1, XBC),
        r["out_ssm_s"].transpose(0, 2, 1).reshape(1, NB_DEC, NH, HD, NSTATE),
    )
    return tuple(np.ascontiguousarray(o) for o in outs)
```
